# Optimizing a Trainium2 kernel written in Bass

```python
import jax, jax.numpy as jnp
from jax import lax
import numpy as np

D_MODEL = 1024
BATCH = 1
SEQ = 1024
DEPTH = 1
DEC_BATCH = 8
DEC_SEQ = 8
PAST_LEN = 4096
PAGE_SIZE = 128

POOL_WINDOWS = (2, 4, 8, 16)
POOL_GROUPS = len(POOL_WINDOWS)
POOL_GROUP_DIM = D_MODEL // 8
POOL_DIM = POOL_GROUPS * POOL_GROUP_DIM
POOL_STATE = max(POOL_WINDOWS) - 1
N_HEADS = 8
QK_NOPE = 64
QK_ROPE = 32
QK_HEAD = QK_NOPE + QK_ROPE
V_HEAD = 64
Q_LORA = 384
KV_LORA = 256
ATTN_DIM = N_HEADS * V_HEAD
ROPE_THETA = 10000.0
SCALE = QK_HEAD ** -0.5
Q_BLOCK = 128
NEG = -1e30
N_BRANCH = 2
OFF_KV = Q_LORA
OFF_KR = OFF_KV + KV_LORA
OFF_POOL = OFF_KR + QK_ROPE
OFF_GATE = OFF_POOL + POOL_DIM
IN_COLS = OFF_GATE + N_BRANCH * D_MODEL
PEER_HEADS = 8
PEER_NKEYS = 128
PEER_EXPERTS = PEER_NKEYS * PEER_NKEYS
PEER_QDIM = 256
PEER_HALF = PEER_QDIM // 2
PEER_TOPK = 16
PEER_BLOCK = 128
EPS = 1e-6

kernel_name = 'pool_mla_peer_hybrid_step'

def rmsnorm(x, w):
    x32 = x.astype(jnp.float32)
    y = x32 * lax.rsqrt(jnp.mean(x32 * x32, axis=-1, keepdims=True) + EPS)
    return (y * w.astype(jnp.float32)).astype(x.dtype)

def rope(x, pos):
    half = QK_ROPE // 2
    inv_freq = ROPE_THETA ** (-jnp.arange(half, dtype=jnp.float32) / half)
    ang = pos.astype(jnp.float32)[:, None] * inv_freq[None, :]
    cos = jnp.cos(ang)[:, None, :]
    sin = jnp.sin(ang)[:, None, :]
    x32 = x.astype(jnp.float32)
    x1, x2 = x32[..., :half], x32[..., half:]
    return jnp.concatenate([x1 * cos - x2 * sin, x1 * sin + x2 * cos], axis=-1).astype(x.dtype)

def mixer_projections(xn, pos, p):
    proj = jnp.einsum('btd,de->bte', xn, p['w_in'])
    q_lat = proj[..., :OFF_KV]
    kv_lat = proj[..., OFF_KV:OFF_KR]
    k_rope = proj[..., OFF_KR:OFF_POOL]
    u_pool = proj[..., OFF_POOL:OFF_GATE]
    gates = proj[..., OFF_GATE:]
    q = jnp.einsum('btr,rhd->bthd', rmsnorm(q_lat, p['q_lat_norm_w']), p['w_q_up'])
    q = jnp.concatenate([q[..., :QK_NOPE], rope(q[..., QK_NOPE:], pos)], axis=-1)
    q = rmsnorm(q, p['q_norm_w'])
    c = rmsnorm(kv_lat, p['kv_lat_norm_w'])
    kr = rope(k_rope[:, :, None, :], pos)[:, :, 0, :]
    return q, c, kr, u_pool, gates

def mla_keys(c, kr, p):
    k_nope = jnp.einsum('btc,chd->bthd', c, p['w_uk'])
    kr_b = jnp.broadcast_to(kr[:, :, None, :], k_nope.shape[:-1] + (QK_ROPE,))
    return rmsnorm(jnp.concatenate([k_nope, kr_b], axis=-1), p['k_norm_w'])

def prompt_attention(q, c, kr, p):
    B, S = q.shape[:2]
    k = mla_keys(c, kr, p)
    v = jnp.einsum('btc,chd->bthd', c, p['w_uv'])
    key_pos = jnp.arange(S)

    def block(i):
        q_blk = lax.dynamic_slice_in_dim(q, i * Q_BLOCK, Q_BLOCK, axis=1)
        s = jnp.einsum('bqhd,bthd->bhqt', q_blk, k).astype(jnp.float32) * SCALE
        q_pos = i * Q_BLOCK + jnp.arange(Q_BLOCK)
        s = jnp.where(key_pos[None, :] <= q_pos[:, None], s, NEG)
        pr = jax.nn.softmax(s, axis=-1).astype(v.dtype)
        return jnp.einsum('bhqt,bthd->bqhd', pr, v)

    o = lax.map(block, jnp.arange(S // Q_BLOCK))
    return o.transpose(1, 0, 2, 3, 4).reshape(B, S, ATTN_DIM)

def online_update(m, l, acc, s, c):
    m_new = jnp.maximum(m, jnp.max(s, axis=-1))
    corr = jnp.exp(m - m_new)
    pr = jnp.exp(s - m_new[..., None])
    l_new = l * corr + jnp.sum(pr, axis=-1)
    acc_new = acc * corr[..., None] + jnp.einsum('bhqt,btc->bhqc', pr, c.astype(jnp.float32))
    return m_new, l_new, acc_new

def sample_attention(q, c_new, kr_new, ckv_pages, kr_pages, page_table, p):
    DB, Q = q.shape[:2]

    def page_step(carry, phys):
        m, l, acc = carry
        c_pg = ckv_pages[phys]
        k_pg = mla_keys(c_pg, kr_pages[phys], p)
        s = jnp.einsum('bqhd,bthd->bhqt', q, k_pg).astype(jnp.float32) * SCALE
        return online_update(m, l, acc, s, c_pg), None

    init = (jnp.full((DB, N_HEADS, Q), NEG, jnp.float32),
            jnp.zeros((DB, N_HEADS, Q), jnp.float32),
            jnp.zeros((DB, N_HEADS, Q, KV_LORA), jnp.float32))
    (m, l, acc), _ = lax.scan(page_step, init, page_table.T)
    k_new = mla_keys(c_new, kr_new, p)
    s = jnp.einsum('bqhd,bthd->bhqt', q, k_new).astype(jnp.float32) * SCALE
    s = jnp.where(jnp.tril(jnp.ones((Q, Q), bool)), s, NEG)
    m, l, acc = online_update(m, l, acc, s, c_new)
    lat = (acc / l[..., None]).astype(c_new.dtype)
    o = jnp.einsum('bhqc,chd->bqhd', lat, p['w_uv'])
    return o.reshape(DB, Q, ATTN_DIM)

def pool_mix(u_full, n_new, p):
    B, L = u_full.shape[:2]
    u32 = u_full.astype(jnp.float32)
    cs = jnp.concatenate([jnp.zeros_like(u32[:, :1]), jnp.cumsum(u32, axis=1)], axis=1)
    rows = np.arange(L - n_new, L)
    outs = []
    for g, w in enumerate(POOL_WINDOWS):
        lo_c, hi_c = g * POOL_GROUP_DIM, (g + 1) * POOL_GROUP_DIM
        hi = rows + 1
        lo = np.maximum(hi - w, 0)
        cnt = (hi - lo).astype(np.float32)
        mean = (cs[:, hi, lo_c:hi_c] - cs[:, lo, lo_c:hi_c]) / cnt[None, :, None]
        outs.append(mean - u32[:, rows, lo_c:hi_c])
    z = jnp.stack(outs, axis=2).astype(u_full.dtype)
    z = jnp.einsum('bngc,gcd->bngd', z, p['pool_lin_w']).reshape(B, n_new, POOL_DIM)
    return z * p['pool_scale']

def peer(xn, p):
    B, T, D = xn.shape
    n_tok = B * T
    xt = xn.reshape(n_tok, D)
    q = jnp.einsum('nd,de->ne', xt, p['peer_w_q']).reshape(n_tok, PEER_HEADS, 2, PEER_HALF)
    s = jnp.einsum('nhpd,hpkd->nhpk', q, p['peer_keys']).astype(jnp.float32)
    s_top, i_top = lax.top_k(s, PEER_TOPK)
    cand = (s_top[:, :, 0, :, None] + s_top[:, :, 1, None, :]).reshape(n_tok, PEER_HEADS, PEER_TOPK * PEER_TOPK)
    cand_id = (i_top[:, :, 0, :, None] * PEER_NKEYS + i_top[:, :, 1, None, :]).reshape(n_tok, PEER_HEADS, PEER_TOPK * PEER_TOPK)
    best, pos = lax.top_k(cand, PEER_TOPK)
    expert = jnp.take_along_axis(cand_id, pos, axis=-1)
    gate = jax.nn.softmax(best, axis=-1).astype(xn.dtype)
    n_pad = (-n_tok) % PEER_BLOCK
    nb = (n_tok + n_pad) // PEER_BLOCK
    xb = jnp.pad(xt, ((0, n_pad), (0, 0))).reshape(nb, PEER_BLOCK, D)
    eb = jnp.pad(expert.reshape(n_tok, -1), ((0, n_pad), (0, 0))).reshape(nb, PEER_BLOCK, PEER_HEADS * PEER_TOPK)
    gb = jnp.pad(gate.reshape(n_tok, -1), ((0, n_pad), (0, 0))).reshape(nb, PEER_BLOCK, PEER_HEADS * PEER_TOPK)

    def block(args):
        xk, ek, gk = args
        u = p['peer_u'][ek]
        v = p['peer_v'][ek]
        a = jax.nn.gelu(jnp.einsum('td,ted->te', xk, u))
        return jnp.einsum('te,ted->td', gk * a, v)

    out = lax.map(block, (xb, eb, gb)).reshape(nb * PEER_BLOCK, D)[:n_tok]
    return out.reshape(B, T, D)

def merge_and_channel_mix(x, attn, pool, gates, p):
    br_attn = jnp.einsum('bte,ed->btd', attn, p['w_attn_br'])
    br_pool = jnp.einsum('btc,cd->btd', pool, p['w_pool_br'])
    mixed = jax.nn.sigmoid(gates[..., :D_MODEL]) * br_attn + jax.nn.sigmoid(gates[..., D_MODEL:]) * br_pool
    h = x + jnp.einsum('btd,de->bte', mixed, p['w_out'])
    return h + peer(rmsnorm(h, p['norm2_w']), p)

def setup_inputs(seed: int = 0) -> dict:
    key = jax.random.key(seed)
    ks = jax.random.split(key, 32)
    n_pages = PAST_LEN // PAGE_SIZE
    n_used = DEC_BATCH * n_pages
    n_phys = n_used + n_used // 4
    nrm = lambda k, shape, s: jax.random.normal(k, shape, jnp.float32) * s
    gain = lambda k, n: 1.0 + nrm(k, (DEPTH, n), 0.05)
    page_table = jax.random.permutation(ks[5], n_phys)[:n_used].reshape(DEC_BATCH, n_pages).astype(jnp.int32)
    return {
        'x_prompt': nrm(ks[0], (BATCH, SEQ, D_MODEL), 1.0),
        'x_sample': nrm(ks[1], (DEC_BATCH, DEC_SEQ, D_MODEL), 1.0),
        'cache_ckv': nrm(ks[2], (DEPTH, n_phys, PAGE_SIZE, KV_LORA), 1.0),
        'cache_krope': nrm(ks[3], (DEPTH, n_phys, PAGE_SIZE, QK_ROPE), 1.0),
        'state_pool': nrm(ks[4], (DEPTH, DEC_BATCH, POOL_STATE, POOL_DIM), 1.0),
        'page_table': page_table,
        'norm1_w': gain(ks[6], D_MODEL),
        'w_in': nrm(ks[7], (DEPTH, D_MODEL, IN_COLS), D_MODEL ** -0.5),
        'q_lat_norm_w': gain(ks[8], Q_LORA),
        'w_q_up': nrm(ks[9], (DEPTH, Q_LORA, N_HEADS, QK_HEAD), Q_LORA ** -0.5),
        'kv_lat_norm_w': gain(ks[10], KV_LORA),
        'w_uk': nrm(ks[11], (DEPTH, KV_LORA, N_HEADS, QK_NOPE), KV_LORA ** -0.5),
        'w_uv': nrm(ks[12], (DEPTH, KV_LORA, N_HEADS, V_HEAD), KV_LORA ** -0.5),
        'q_norm_w': gain(ks[13], QK_HEAD),
        'k_norm_w': gain(ks[14], QK_HEAD),
        'w_attn_br': nrm(ks[15], (DEPTH, ATTN_DIM, D_MODEL), ATTN_DIM ** -0.5),
        'pool_lin_w': nrm(ks[16], (DEPTH, POOL_GROUPS, POOL_GROUP_DIM, POOL_GROUP_DIM), POOL_GROUP_DIM ** -0.5),
        'pool_scale': 1.0 + nrm(ks[17], (DEPTH, POOL_DIM), 0.1),
        'w_pool_br': nrm(ks[18], (DEPTH, POOL_DIM, D_MODEL), POOL_DIM ** -0.5),
        'w_out': nrm(ks[19], (DEPTH, D_MODEL, D_MODEL), D_MODEL ** -0.5),
        'norm2_w': gain(ks[20], D_MODEL),
        'peer_w_q': nrm(ks[21], (DEPTH, D_MODEL, PEER_HEADS * PEER_QDIM), D_MODEL ** -0.5),
        'peer_keys': nrm(ks[22], (DEPTH, PEER_HEADS, 2, PEER_NKEYS, PEER_HALF), PEER_HALF ** -0.5),
        'peer_u': nrm(ks[23], (DEPTH, PEER_EXPERTS, D_MODEL), D_MODEL ** -0.5),
        'peer_v': nrm(ks[24], (DEPTH, PEER_EXPERTS, D_MODEL), PEER_HEADS ** -0.5),
    }

def reference(x_prompt, x_sample, cache_ckv, cache_krope, state_pool, page_table,
              norm1_w, w_in, q_lat_norm_w, w_q_up, kv_lat_norm_w, w_uk, w_uv, q_norm_w, k_norm_w,
              w_attn_br, pool_lin_w, pool_scale, w_pool_br, w_out, norm2_w,
              peer_w_q, peer_keys, peer_u, peer_v):
    B, S = x_prompt.shape[:2]
    DB, Q = x_sample.shape[:2]
    pos_p = jnp.arange(S)
    pos_s = PAST_LEN + jnp.arange(Q)
    xp, xs = x_prompt, x_sample
    ckv_p, kr_p, pool_p, ckv_s, kr_s, pool_s = [], [], [], [], [], []
    for l in range(DEPTH):
        p = dict(norm1_w=norm1_w[l], w_in=w_in[l], q_lat_norm_w=q_lat_norm_w[l], w_q_up=w_q_up[l],
                 kv_lat_norm_w=kv_lat_norm_w[l], w_uk=w_uk[l], w_uv=w_uv[l], q_norm_w=q_norm_w[l],
                 k_norm_w=k_norm_w[l], w_attn_br=w_attn_br[l], pool_lin_w=pool_lin_w[l],
                 pool_scale=pool_scale[l], w_pool_br=w_pool_br[l], w_out=w_out[l], norm2_w=norm2_w[l],
                 peer_w_q=peer_w_q[l], peer_keys=peer_keys[l], peer_u=peer_u[l], peer_v=peer_v[l])
        q, c, kr, u_pool, gates = mixer_projections(rmsnorm(xp, p['norm1_w']), pos_p, p)
        attn = prompt_attention(q, c, kr, p)
        pool = pool_mix(u_pool, S, p)
        xp = merge_and_channel_mix(xp, attn, pool, gates, p)
        ckv_p.append(c)
        kr_p.append(kr)
        pool_p.append(u_pool[:, S - POOL_STATE:])
        q, c, kr, u_pool, gates = mixer_projections(rmsnorm(xs, p['norm1_w']), pos_s, p)
        attn = sample_attention(q, c, kr, cache_ckv[l], cache_krope[l], page_table, p)
        u_full = jnp.concatenate([state_pool[l].astype(u_pool.dtype), u_pool], axis=1)
        pool = pool_mix(u_full, Q, p)
        xs = merge_and_channel_mix(xs, attn, pool, gates, p)
        ckv_s.append(c)
        kr_s.append(kr)
        pool_s.append(u_full[:, -POOL_STATE:])
    return (xp, xs, jnp.stack(ckv_p), jnp.stack(kr_p), jnp.stack(pool_p),
            jnp.stack(ckv_s), jnp.stack(kr_s), jnp.stack(pool_s))


_drawn_inputs = setup_inputs


def setup_inputs(seed=0):
    import zlib

    import numpy as np

    out = dict(_drawn_inputs(seed))
    spreads = {}
    factors = {'cache_krope': 3.771, 'q_lat_norm_w': 6.219, 'q_norm_w': 5.526, 'k_norm_w': 5.947}
    for name, (base, spread) in spreads.items():
        noise = np.random.default_rng([zlib.crc32(name.encode()), seed]).standard_normal(out[name].shape)
        drawn = base * np.exp(spread * noise) if base else spread * noise
        out[name] = __import__('jax').numpy.asarray(drawn.astype(out[name].dtype))
    for name, factor in factors.items():
        out[name] = (out[name] * factor).astype(out[name].dtype)
    return out
```

```python
from contextlib import ExitStack

import concourse.bass as bass
from concourse import mybir

F32 = mybir.dt.float32
U32 = mybir.dt.uint32
I32 = mybir.dt.int32
ALU = mybir.AluOpType
ACT = mybir.ActivationFunctionType
AX = mybir.AxisListType.X
ds = bass.ds

D, SEQ, DB, DQ = 1024, 1024, 8, 8
P = 128
KD = D // P
NS = DB * DQ
TOK = SEQ + 2 * NS
NT = TOK // P
PT = SEQ // P
NW = 384
NN = TOK // NW
H, DN, DR, DH = 8, 64, 32, 96
QL, KL = 384, 256
G, STATE = 4, 15
PAD = 16
PAGE, NPAGES, NPHYS = 128, 32, 320
GP = 4
GROUPS = NPAGES // GP
PGW = KL + 1 + DR
NK, TOPK = 128, 16
NEXP = NK * NK
ROUTES = PT * H + H // 2
NEG = -1e30
LOWEST = -3.0e38
EPS = 1e-6
RING = 8
W_FRONT = QL + KL + 4 * P + 2 * DR


class Arena:

    def __init__(self, tensor):
        self.tensor = tensor

    def at(self, word, parts, *dims):
        n = 1
        for d in dims:
            n *= d
        v = self.tensor[0:parts, word:word + n]
        if len(dims) == 2:
            return v.rearrange("p (a b) -> p a b", a=dims[0])
        if len(dims) == 3:
            return v.rearrange("p (a b c) -> p a b c", a=dims[0], b=dims[1])
        return v


def wait_apart(eng, sem, value, met):
    value = eng.compute_val(value)
    eng.wait_ge(*met)
    eng.wait_ge(sem, value)


def one(ap):
    return ap.rearrange("p a b -> p (a b)")


def build(nc, I, O):
    with ExitStack() as ctx:
        ar = Arena(ctx.enter_context(nc.sbuf_tensor("arena", [P, 51000], F32)))
        const = ctx.enter_context(nc.sbuf_tensor("const", [P, 1000], F32))
        xn_dram = nc.dram_tensor("xn_spill", [P, KD, TOK], F32, kind="Internal").ap()
        new_rows = nc.dram_tensor("new_rows", [P, KL + DR], F32, kind="Internal").ap()
        table = ctx.enter_context(nc.sbuf_tensor("page_ids", [1, DB * NPAGES], I32))
        qk_norms = ctx.enter_context(nc.sbuf_tensor("qk_norms", [DH, 2], F32))
        n_ids = ROUTES * TOPK

        names = {}
        col = 0
        for name, w in CONSTS:
            names[name] = const[:, col:col + w]
            col += w
        C = names
        env = dict(nc=nc, I=I, O=O, ar=ar, C=C, const=const, xn_dram=xn_dram, new_rows=new_rows,
                   table=table, qk_norms=qk_norms, ids=ar.at(TOP - 2 * n_ids, P, n_ids).bitcast(U32), gates=ar.at(TOP - n_ids, P, n_ids))
        project(env)
        pool_and_values(env)
        prompt_attention(env)
        sample_attention(env)
        merge(env)
        residual(env)
        peer_scores(env)
        route(env)
        peer(env)


CONSTS = [("ident", P), ("ones", P), ("causal", P), ("page_mask", NS), ("iota16", TOPK), ("w1", KD), ("wq_lat", 3),
          ("wkv", 2), ("wqk", 1), ("pool_scale", G), ("invcnt", G * PAD), ("eps", 1), ("fold", NS)]
CONST_COLS = sum(w for _, w in CONSTS)

TOP = 51000
QT = TOP - H * TOK
KT = QT - H * TOK
CT = KT - 2 * TOK
KRT = CT - TOK
UP = KRT - G * (PAD + TOK)
VV = 0
ZL = VV + PT * 512
AT = 17984
YALL = 0
XN2 = YALL + NT * D
XN2T = XN2 + NT * D
MT = XN2T + KD * TOK
SALL = XN2T + KD * TOK


def project(env):
    nc, I, ar, C = env["nc"], env["I"], env["ar"], env["C"]
    w = 0
    wfront = ar.at(w, P, KD, W_FRONT); w += KD * W_FRONT
    wqup = ar.at(w, P, 3, H * DH); w += 3 * H * DH
    wqsw = ar.at(w, P, 3, H * DR); w += 3 * H * DR
    wuk = ar.at(w, P, 2, H * DN); w += 2 * H * DN
    xt = ar.at(w, P, KD, NW); w += KD * NW
    sq = ar.at(w, P, 4, NW); w += 4 * NW
    qlat = ar.at(w, P, 3, NW); w += 3 * NW
    kv = ar.at(w, P, 2, NW); w += 2 * NW
    cos = ar.at(w, P, NW); w += NW
    sin = ar.at(w, P, NW); w += NW
    rr = ar.at(w, P, 2, NW); w += 2 * NW
    sqh = ar.at(w, P, 2, NW); w += 2 * NW
    kraw = ar.at(w, P, 2, NW); w += 2 * NW
    rot1 = ar.at(w, P, NW); w += NW
    rot2 = ar.at(w, P, NW); w += NW
    assert w <= UP
    qT, kT = ar.at(QT, P, H, TOK), ar.at(KT, P, H, TOK)
    cT, krT, uP = ar.at(CT, P, 2, TOK), ar.at(KRT, P, TOK), ar.at(UP, P, G, PAD + TOK)
    chunks = [(j * P, "q", j) for j in range(3)] + [(QL + j * P, "kv", j) for j in range(2)] \
        + [(QL + KL + j * P, "pool", j) for j in range(G)]
    KR0 = QL + KL + G * P
    NCH = len(chunks)
    units = [("q", h) for h in range(H)] + [("k", h) for h in range(H)]

    with ExitStack() as ctx:
        sem = lambda n: ctx.enter_context(nc.semaphore(n))
        ps = ctx.enter_context(nc.psum_tensor("ps_a", [P, 8, 512], F32))
        pj, ss, pa, pb = (ps[:, 2 * j:2 * j + 2, 0:NW] for j in range(4))
        loaded, x_in, xn_saved = sem("a_loaded"), sem("a_x_in"), sem("a_xn_saved")
        sq_done, sq_used = sem("a_sq_done"), sem("a_sq_used")
        std_done, tables_in = sem("a_std_done"), sem("a_tables_in")
        xn_done, chunk_done, chunk_out = sem("a_xn_done"), sem("a_chunk_done"), sem("a_chunk_out")
        kr_done, kr_out, lat_done = sem("a_kr_done"), sem("a_kr_out"), sem("a_lat_done")
        up_done, usq_done, uss_done, ustd_done, unit_out = (sem("a_" + n) for n in ("up", "usq", "uss", "ustd", "unit"))
        pads = sem("a_pads")
        block = ctx.enter_context(nc.Block())

        @block.sync
        def _(sp):
            sp.dma_start(env["const"][:, 0:CONST_COLS], I["consts"]).then_inc(loaded, 16)
            sp.dma_start(env["qk_norms"][:, :], I["qk_norms"]).then_inc(loaded, 16)
            sp.dma_start(wfront, I["w_front"]).then_inc(loaded, 16)
            sp.dma_start(wqup, I["w_q_up"]).then_inc(loaded, 16)
            sp.dma_start(wqsw, I["w_q_sw"]).then_inc(loaded, 16)
            sp.dma_start(wuk, I["w_uk"]).then_inc(loaded, 16)
            sp.wait_ge(loaded, 96)
            with sp.Fori(0, NN) as n:
                sp.wait_ge(xn_saved, n * 16)
                sp.wait_ge(kr_done, n)
                sp.dma_start(xt, I["xT"][:, :, ds(n * NW, NW)]).then_inc(x_in, 16)
                sp.wait_ge(unit_out, n * 16)
                sp.dma_start(cos[64:96, :], I["cos"][:, ds(n * NW, NW)]).then_inc(tables_in, 16)
                sp.dma_start(sin[64:96, :], I["sin"][:, ds(n * NW, NW)]).then_inc(tables_in, 16)
                sp.wait_ge(xn_done, n * KD + KD)
                sp.dma_start(env["xn_dram"][:, :, ds(n * NW, NW)], xt).then_inc(xn_saved, 16)
            sp.wait_ge(xn_saved, NN * 16)

        @block.gpsimd
        def _(pool):
            nc.gpsimd.memset(uP[:, :, 0:PAD], 0.0).then_inc(pads, 1)

        @block.scalar
        def _(act):
            act.wait_ge(loaded, 96)
            with act.Fori(0, NN) as n:
                act.wait_ge(x_in, n * 16 + 16)
                for half in range(2):
                    act.wait_ge(sq_used, n * 4 + half)
                    nc.scalar.activation(sq[:, :, :], xt[:, 4 * half:4 * half + 4, :], ACT.Square).then_inc(sq_done, 1)
                act.wait_ge(sq_used, n * 4 + 2)
                act.wait_ge(unit_out, n * 16)
                nc.scalar.activation(rr[:, 0, :], ss[:, 0, :], ACT.Sqrt, bias=C["eps"], scale=1.0 / D).then_inc(std_done, 1)
                for j, (_, what, at) in enumerate(chunks):
                    act.wait_ge(chunk_done, n * NCH + j + 1)
                    dst = {"q": lambda: qlat[:, at, :], "kv": lambda: kv[:, at, :],
                           "pool": lambda: uP[:, at, ds(PAD + n * NW, NW)]}[what]()
                    nc.scalar.activation(dst, pj[:, j % 2, :], ACT.Copy).then_inc(chunk_out, 1)
                    if j == 2:
                        nc.scalar.drain()
                        act.wait_ge(sq_used, n * 4 + 2)
                        nc.scalar.activation(sq[:, 0:3, :], qlat[:, :, :], ACT.Square).then_inc(sq_done, 1)
                    if j == 4:
                        nc.scalar.drain()
                        act.wait_ge(sq_used, n * 4 + 3)
                        nc.scalar.activation(rr[:, 1, :], ss[:, 1, :], ACT.Sqrt, bias=C["eps"], scale=1.0 / QL).then_inc(std_done, 1)
                        nc.scalar.activation(sq[:, 0:2, :], kv[:, :, :], ACT.Square).then_inc(sq_done, 1)
                act.wait_ge(sq_used, n * 4 + 4)
                act.wait_ge(xn_done, n * KD + KD)
                nc.scalar.activation(rr[:, 0, :], ss[:, 0, :], ACT.Sqrt, bias=C["eps"], scale=1.0 / KL).then_inc(std_done, 1)

                def unit_square(u):
                    kind, _ = units[u]
                    act.wait_ge(up_done, n * 16 + u + 1)
                    if kind == "q":
                        if u >= 2:
                            act.wait_ge(uss_done, n * 16 + u - 1)
                        nc.scalar.activation(sqh[0:DH, u % 2, :], pa[0:DH, u % 2, :], ACT.Square).then_inc(usq_done, 1)
                    else:
                        act.wait_ge(unit_out, n * 16 + u - 1)
                        nc.scalar.activation(kraw[0:DN, u % 2, :], pa[0:DN, u % 2, :], ACT.Copy)
                        nc.scalar.drain()
                        act.wait_ge(uss_done, n * 16 + u - 1)
                        nc.scalar.activation(sqh[0:DH, u % 2, :], kraw[0:DH, u % 2, :], ACT.Square).then_inc(usq_done, 1)

                def unit_std(u):
                    act.wait_ge(uss_done, n * 16 + u + 1)
                    if u < 2:
                        act.wait_ge(lat_done, n * 5 + 5)
                    else:
                        act.wait_ge(unit_out, n * 16 + u - 1)
                    nc.scalar.activation(rr[0:DH, u % 2, :], ss[0:DH, u % 2, :], ACT.Sqrt, bias=C["eps"][0:DH],
                                         scale=1.0 / DH).then_inc(ustd_done, 1)

                act.wait_ge(kr_out, n + 1)
                unit_square(0)
                for u in range(1, 16):
                    unit_square(u)
                    unit_std(u - 1)
                unit_std(15)

        @block.tensor
        def _(pe):
            pe.wait_ge(loaded, 96)
            ones = C["ones"]
            with pe.Fori(0, NN) as n:
                pe.wait_ge(ustd_done, n * 16)
                for half in range(2):
                    pe.wait_ge(sq_done, n * 4 + half + 1)
                    for k in range(4):
                        last = nc.tensor.matmul(ss[:, 0, :], ones, sq[:, k, :], start=half + k == 0, stop=half + k == 4)
                    last.then_inc(sq_used, 1)

                def chunk(j):
                    c0 = chunks[j][0]
                    pe.wait_ge(chunk_out, n * NCH + max(j - 1, 0))
                    if j == 0:
                        pe.wait_ge(kr_out, n)
                    for k in range(KD):
                        if j == 0:
                            pe.wait_ge(xn_done, n * KD + k + 1)
                        last = nc.tensor.matmul(pj[:, j % 2, :], wfront[:, k, c0:c0 + P], xt[:, k, :],
                                                start=k == 0, stop=k == KD - 1)
                    last.then_inc(chunk_done, 1)

                for j in range(4):
                    chunk(j)
                pe.wait_ge(sq_done, n * 4 + 3)
                for k in range(3):
                    last = nc.tensor.matmul(ss[:, 1, :], ones, sq[:, k, :], start=k == 0, stop=k == 2)
                last.then_inc(sq_used, 1)
                for j in range(4, 6):
                    chunk(j)
                pe.wait_ge(sq_done, n * 4 + 4)
                pe.wait_ge(std_done, n * 3 + 1)
                for k in range(2):
                    last = nc.tensor.matmul(ss[:, 0, :], ones, sq[:, k, :], start=k == 0, stop=k == 1)
                last.then_inc(sq_used, 1)
                for j in range(6, NCH):
                    chunk(j)
                pe.wait_ge(chunk_out, n * NCH + NCH)
                for s in range(2):
                    for k in range(KD):
                        last = nc.tensor.matmul(pj[64:96, s, :], wfront[:, k, KR0 + s * DR:KR0 + (s + 1) * DR], xt[:, k, :],
                                                start=k == 0, stop=k == KD - 1)
                last.then_inc(kr_done, 1)

                def up(u):
                    kind, h = units[u]
                    if u < 2:
                        pe.wait_ge(lat_done, n * 5 + 5)
                    wait_apart(pe, unit_out, n * 16 + max(u - 1, 0), (loaded, 96))
                    if kind == "q":
                        for k in range(3):
                            nc.tensor.matmul(pa[0:DH, u % 2, :], wqup[:, k, h * DH:(h + 1) * DH], qlat[:, k, :],
                                             start=k == 0, stop=k == 2)
                        for k in range(3):
                            last = nc.tensor.matmul(pb[64:96, u % 2, :], wqsw[:, k, h * DR:(h + 1) * DR], qlat[:, k, :],
                                                    start=k == 0, stop=k == 2)
                    else:
                        for k in range(2):
                            last = nc.tensor.matmul(pa[0:DN, u % 2, :], wuk[:, k, h * DN:(h + 1) * DN], cT[:, k, ds(n * NW, NW)],
                                                    start=k == 0, stop=k == 1)
                    last.then_inc(up_done, 1)

                def total(u):
                    pe.wait_ge(usq_done, n * 16 + u + 1)
                    if u < 2:
                        pe.wait_ge(std_done, n * 3 + 3)
                    else:
                        pe.wait_ge(ustd_done, n * 16 + u - 1)
                    nc.tensor.matmul(ss[0:DH, u % 2, :], ones[0:DH, 0:DH], sqh[0:DH, u % 2, :],
                                     start=True, stop=True).then_inc(uss_done, 1)

                up(0)
                for u in range(1, 16):
                    up(u)
                    total(u - 1)
                total(15)

        @block.vector
        def _(dve):
            dve.wait_ge(loaded, 96)
            mul, add = ALU.mult, ALU.add
            nc.vector.scalar_tensor_tensor(out=C["wqk"][0:DH], in0=env["qk_norms"][:, 0:1], scalar=DH ** -0.5,
                                           in1=env["qk_norms"][:, 1:2], op0=mul, op1=mul)
            nc.vector.drain()
            with dve.Fori(0, NN) as n:
                dve.wait_ge(std_done, n * 3 + 1)
                nc.vector.reciprocal(rr[:, 0, :], rr[:, 0, :])
                nc.vector.drain()
                for k in range(KD):
                    nc.vector.scalar_tensor_tensor(out=xt[:, k, :], in0=xt[:, k, :], scalar=C["w1"][:, k:k + 1],
                                                   in1=rr[:, 0, :], op0=mul, op1=mul).then_inc(xn_done, 1)
                dve.wait_ge(std_done, n * 3 + 2)
                nc.vector.reciprocal(rr[:, 1, :], rr[:, 1, :])
                nc.vector.drain()
                for k in range(3):
                    nc.vector.scalar_tensor_tensor(out=qlat[:, k, :], in0=qlat[:, k, :], scalar=C["wq_lat"][:, k:k + 1],
                                                   in1=rr[:, 1, :], op0=mul, op1=mul).then_inc(lat_done, 1)
                dve.wait_ge(std_done, n * 3 + 3)
                nc.vector.reciprocal(rr[:, 0, :], rr[:, 0, :])
                nc.vector.drain()
                for k in range(2):
                    nc.vector.scalar_tensor_tensor(out=cT[:, k, ds(n * NW, NW)], in0=kv[:, k, :], scalar=C["wkv"][:, k:k + 1],
                                                   in1=rr[:, 0, :], op0=mul, op1=mul).then_inc(lat_done, 1)
                dve.wait_ge(kr_done, n + 1)
                dve.wait_ge(tables_in, n * 32 + 32)
                dve.wait_ge(usq_done, n * 16)
                nc.vector.tensor_tensor(rot1[64:96, :], pj[64:96, 0, :], cos[64:96, :], mul)
                nc.vector.tensor_tensor(rot2[64:96, :], pj[64:96, 1, :], sin[64:96, :], mul)
                nc.vector.drain()
                nc.vector.tensor_tensor(kraw[64:96, 0, :], rot1[64:96, :], rot2[64:96, :], add)
                nc.vector.drain()
                nc.vector.tensor_copy(kraw[64:96, 1, :], kraw[64:96, 0, :])
                nc.vector.tensor_copy(krT[64:96, ds(n * NW, NW)], kraw[64:96, 0, :]).then_inc(kr_out, 1)
                for u, (kind, h) in enumerate(units):
                    dve.wait_ge(ustd_done, n * 16 + u + 1)
                    r = rr[:, u % 2, :]
                    nc.vector.reciprocal(r[0:DH], r[0:DH])
                    if kind == "q":
                        nc.vector.tensor_tensor(rot1[64:96, :], pa[64:96, u % 2, :], cos[64:96, :], mul)
                        nc.vector.tensor_tensor(rot2[64:96, :], pb[64:96, u % 2, :], sin[64:96, :], mul)
                        nc.vector.drain()
                        nc.vector.tensor_tensor(rot1[64:96, :], rot1[64:96, :], rot2[64:96, :], add)
                        nc.vector.scalar_tensor_tensor(out=qT[0:DN, h, ds(n * NW, NW)], in0=pa[0:DN, u % 2, :],
                                                       scalar=C["wqk"][0:DN], in1=r[0:DN], op0=mul, op1=mul)
                        nc.vector.drain()
                        nc.vector.scalar_tensor_tensor(out=qT[64:96, h, ds(n * NW, NW)], in0=rot1[64:96, :],
                                                       scalar=C["wqk"][64:96], in1=r[64:96], op0=mul, op1=mul).then_inc(unit_out, 1)
                    else:
                        nc.vector.drain()
                        nc.vector.tensor_tensor(kT[0:DH, h, ds(n * NW, NW)], kraw[0:DH, u % 2, :], r[0:DH], mul).then_inc(unit_out, 1)


def pool_and_values(env):
    nc, I, O, ar, C = (env[k] for k in ("nc", "I", "O", "ar", "C"))
    cT, krT, uP = ar.at(CT, P, 2, TOK), ar.at(KRT, P, TOK), ar.at(UP, P, G, PAD + TOK)
    vv, zl = ar.at(VV, P, PT, 512), ar.at(ZL, P, G, TOK)
    w = ZL + G * TOK
    z = ar.at(w, P, G, TOK); w += G * TOK
    part = [ar.at(w + s * (PAD + SEQ), P, PAD + SEQ) for s in range(2)]; w += 2 * (PAD + SEQ)
    wuv = ar.at(w, P, 2, 512); w += 1024
    wlin = ar.at(w, P, G, P); w += G * P
    us = ar.at(w, P, G, DB * (STATE + DQ)); w += G * DB * (STATE + DQ)
    uspart = [ar.at(w + s * DB * 23, P, DB, STATE + DQ) for s in range(2)]; w += 2 * DB * 23
    rows = ar.at(w, P, KL + DR); w += KL + DR
    assert w <= UP
    us4 = [us[:, g, :].rearrange("p (b t) -> p b t", b=DB) for g in range(G)]
    NZ = 3
    with ExitStack() as ctx:
        sem = lambda n: ctx.enter_context(nc.semaphore(n))
        ps = ctx.enter_context(nc.psum_tensor("ps_b", [P, 8, 512], F32))
        loaded, stored, v_done, v_out = sem("b_loaded"), sem("b_stored"), sem("b_v_done"), sem("b_v_out")
        us_ready, window, z_done, lin_done, zl_done = (sem("b_" + n) for n in ("us", "window", "z", "lin", "zl"))
        rows_done, rows_out, z_started = sem("b_rows_done"), sem("b_rows_out"), sem("b_z_started")
        block = ctx.enter_context(nc.Block())

        @block.sync
        def _(sp):
            sp.dma_start(wuv, I["w_uv"]).then_inc(loaded, 16)
            sp.dma_start(wlin, I["pool_lin"]).then_inc(loaded, 16)
            for g in range(G):
                sp.dma_start(us4[g][:, :, 0:STATE], I["stateT"][:, g, :, :]).then_inc(loaded, 16)
            sp.dma_start(O["ckvT"], cT).then_inc(stored, 16)
            sp.dma_start(O["kropeT"], krT[64:96, :]).then_inc(stored, 16)
            sp.dma_start(O["poolT"], uP[:, :, PAD + SEQ - STATE:PAD + SEQ]).then_inc(stored, 16)
            sp.wait_ge(us_ready, 1)
            for g in range(G):
                sp.dma_start(O["poolsT"][:, g, :, :], us4[g][:, :, DQ:DQ + STATE]).then_inc(stored, 16)
            sp.wait_ge(rows_out, 2)
            sp.dma_start(env["new_rows"], rows).then_inc(stored, 16)
            sp.wait_ge(stored, 8 * 16)

        @block.tensor
        def _(pe):
            pe.wait_ge(loaded, 96)
            for t in range(PT):
                if t >= 2:
                    pe.wait_ge(v_out, t - 1)
                for k in range(2):
                    last = nc.tensor.matmul(ps[:, t % 2, :], cT[:, k, t * P:(t + 1) * P], wuv[:, k, :], start=k == 0, stop=k == 1)
                last.then_inc(v_done, 1)
            for k in range(2):
                nc.tensor.transpose(ps[:, 2, k * P:(k + 1) * P], cT[:, k, SEQ:TOK], C["ident"])
            nc.tensor.transpose(ps[:, 3, 0:DR], krT[64:96, SEQ:TOK], C["ident"][64:96, 64:96]).then_inc(rows_done, 1)
            for g in range(G):
                pe.wait_ge(z_done, g + 1)
                for n in range(NZ):
                    i = g * NZ + n
                    if i >= 4:
                        pe.wait_ge(zl_done, i - 3)
                    nc.tensor.matmul(ps[:, 4 + i % 4, 0:NW], wlin[:, g, :], z[:, g, n * NW:(n + 1) * NW],
                                     start=True, stop=True).then_inc(lin_done, 1)

        @block.scalar
        def _(act):
            for t in range(PT):
                act.wait_ge(v_done, t + 1)
                nc.scalar.activation(vv[:, t, :], ps[:, t % 2, :], ACT.Copy).then_inc(v_out, 1)
            act.wait_ge(rows_done, 1)
            nc.scalar.activation(rows[:, 0:KL], ps[:, 2, 0:KL], ACT.Copy).then_inc(rows_out, 1)
            nc.scalar.activation(rows[:, KL:KL + DR], ps[:, 3, 0:DR], ACT.Copy).then_inc(rows_out, 1)
            for g in range(G):
                for n in range(NZ):
                    i = g * NZ + n
                    act.wait_ge(lin_done, i + 1)
                    nc.scalar.activation(zl[:, g, n * NW:(n + 1) * NW], ps[:, 4 + i % 4, 0:NW], ACT.Copy,
                                         scale=C["pool_scale"][:, g:g + 1]).then_inc(zl_done, 1)

        @block.gpsimd
        def _(pool):
            pool.wait_ge(loaded, 96)
            for g in range(G):
                last = nc.gpsimd.tensor_copy(us4[g][:, :, STATE:], uP[:, g, PAD + SEQ:PAD + SEQ + NS].rearrange("p (b q) -> p b q", b=DB))
            last.then_inc(us_ready, 1)
            pool.wait_ge(us_ready, 1)
            step = 0
            for g in range(G):
                src, ssrc = uP[:, g, 0:PAD + SEQ], us4[g]
                for lv in range(g + 1):
                    lo, sh = (2 << lv) - 1, 1 << lv
                    dst, sdst = part[(step) % 2], uspart[(step) % 2]
                    if lv == 0 and g:
                        pool.wait_ge(z_started, g)
                    nc.gpsimd.tensor_tensor(dst[:, lo:], src[:, lo:], src[:, lo - sh:PAD + SEQ - sh], ALU.add)
                    nc.gpsimd.tensor_tensor(sdst[:, :, lo:], ssrc[:, :, lo:], ssrc[:, :, lo - sh:STATE + DQ - sh], ALU.add).then_inc(window, 1)
                    step += 1
                    pool.wait_ge(window, step)
                    src, ssrc = dst, sdst

        @block.vector
        def _(dve):
            step = 0
            for g in range(G):
                step += g + 1
                dve.wait_ge(window, step)
                s, t = part[(step - 1) % 2], uspart[(step - 1) % 2]
                width = 2 << g
                nc.vector.scalar_tensor_tensor(out=z[:, g, PAD:SEQ], in0=s[:, 2 * PAD:], scalar=1.0 / width,
                                               in1=uP[:, g, 2 * PAD:PAD + SEQ], op0=ALU.mult, op1=ALU.subtract)
                nc.vector.tensor_tensor(z[:, g, 0:PAD], s[:, PAD:2 * PAD], C["invcnt"][:, g * PAD:(g + 1) * PAD], ALU.mult)
                nc.vector.drain()
                nc.vector.tensor_tensor(z[:, g, 0:PAD], z[:, g, 0:PAD], uP[:, g, PAD:2 * PAD], ALU.subtract)
                zs = z[:, g, SEQ:SEQ + NS].rearrange("p (b q) -> p b q", b=DB)
                nc.vector.scalar_tensor_tensor(out=zs, in0=t[:, :, STATE:], scalar=1.0 / width, in1=us4[g][:, :, STATE:],
                                               op0=ALU.mult, op1=ALU.subtract).then_inc(z_started, 1)
                nc.vector.drain()
                nc.vector.tensor_copy(z[:, g, SEQ + NS:TOK], z[:, g, SEQ:SEQ + NS]).then_inc(z_done, 1)


def prompt_attention(env):
    nc, ar, C = env["nc"], env["ar"], env["C"]
    qT, kT, vv = ar.at(QT, P, H, TOK), ar.at(KT, P, H, TOK), ar.at(VV, P, PT, 512)
    w = ZL + G * TOK
    attn = ar.at(w, P, PT, 512); w += PT * 512
    qh = ar.at(w, P, SEQ); w += SEQ
    pr = ar.at(w, P, 2, SEQ); w += 2 * SEQ
    prT = ar.at(w, P, 2, SEQ); w += 2 * SEQ
    negm = ar.at(w, P, 2); w += 2
    l = ar.at(w, P, 2); w += 2
    rl = ar.at(w, P, 1); w += 1
    assert w <= AT
    attnT = ar.at(AT, P, 4, TOK)
    with ExitStack() as ctx:
        sem = lambda n: ctx.enter_context(nc.semaphore(n))
        S = ctx.enter_context(nc.psum_tensor("ps_s", [P, 2, SEQ], F32))
        PTp = ctx.enter_context(nc.psum_tensor("ps_pt", [P, SEQ], F32))
        Op = ctx.enter_context(nc.psum_tensor("ps_o", [P, 512], F32))
        q_copied, s_done, max_done, exp_done, t_done, t_out, pv_done, o_out = (
            sem("c_" + n) for n in ("q_copied", "s", "max", "exp", "t", "t_out", "pv", "o_out"))
        at_done, at_out = sem("c_at_done"), sem("c_at_out")
        block = ctx.enter_context(nc.Block())

        @block.gpsimd
        def _(pool):
            with pool.Fori(0, H) as h:
                pool.wait_ge(s_done, h * PT)
                nc.gpsimd.tensor_copy(qh[0:DH, :], one(qT[0:DH, ds(h, 1), 0:SEQ])).then_inc(q_copied, 1)

        @block.tensor
        def _(pe):
            with pe.Fori(0, H) as h:
                def scores(i):
                    pe.wait_ge(q_copied, h + 1)
                    pe.wait_ge(exp_done, h * PT + max(i - 1, 0))
                    for c in range(0, (i + 1) * P, 512):
                        n = min(512, (i + 1) * P - c)
                        last = nc.tensor.matmul(S[:, i % 2, c:c + n], qh[0:DH, i * P:(i + 1) * P], one(kT[0:DH, ds(h, 1), c:c + n]),
                                                start=True, stop=True)
                    last.then_inc(s_done, 1)

                scores(0)
                for i in range(PT):
                    if i + 1 < PT:
                        scores(i + 1)
                    pe.wait_ge(exp_done, h * PT + i + 1)
                    pe.wait_ge(t_out, h * PT + i)
                    for j in range(i + 1):
                        last = nc.tensor.transpose(PTp[:, j * P:(j + 1) * P], pr[:, i % 2, j * P:(j + 1) * P], C["ident"])
                    last.then_inc(t_done, 1)
                    pe.wait_ge(t_out, h * PT + i + 1)
                    pe.wait_ge(o_out, h * PT + i)
                    for j in range(i + 1):
                        last = nc.tensor.matmul(Op[:, 0:DN], prT[:, i % 2, j * P:(j + 1) * P], vv[:, j, ds(h * DN, DN)],
                                                start=j == 0, stop=j == i)
                    last.then_inc(pv_done, 1)
            for i in range(PT):
                if i >= 2:
                    pe.wait_ge(at_out, i - 1)
                else:
                    pe.wait_ge(o_out, H * PT)
                for k in range(4):
                    last = nc.tensor.transpose(S[:, i % 2, k * P:(k + 1) * P], attn[:, i, k * P:(k + 1) * P], C["ident"])
                last.then_inc(at_done, 1)

        @block.scalar
        def _(act):
            with act.Fori(0, H) as h:
                def exps(i):
                    act.wait_ge(max_done, h * PT + i + 1)
                    if i >= 2:
                        act.wait_ge(t_done, h * PT + i - 1)
                        act.wait_ge(o_out, h * PT + i - 1)
                    else:
                        act.wait_ge(t_done, h * PT)
                        act.wait_ge(o_out, h * PT)
                    W = (i + 1) * P
                    nc.scalar.activation(pr[:, i % 2, 0:W], S[:, i % 2, 0:W], ACT.Exp, bias=negm[:, i % 2:i % 2 + 1],
                                         accum_out=l[:, i % 2:i % 2 + 1]).then_inc(exp_done, 1)

                exps(0)
                for i in range(PT):
                    if i + 1 < PT:
                        exps(i + 1)
                    act.wait_ge(t_done, h * PT + i + 1)
                    act.wait_ge(pv_done, h * PT + max(i - 1, 0))
                    nc.scalar.activation(prT[:, i % 2, 0:(i + 1) * P], PTp[:, 0:(i + 1) * P], ACT.Copy).then_inc(t_out, 1)
            for i in range(PT):
                act.wait_ge(at_done, i + 1)
                nc.scalar.activation(attnT[:, :, i * P:(i + 1) * P], S[:, i % 2, 0:512].rearrange("p (k t) -> p k t", k=4),
                                     ACT.Copy).then_inc(at_out, 1)

        @block.vector
        def _(dve):
            with dve.Fori(0, H) as h:
                def maxima(i):
                    dve.wait_ge(s_done, h * PT + i + 1)
                    W = (i + 1) * P
                    nc.vector.tensor_tensor(S[:, i % 2, W - P:W], S[:, i % 2, W - P:W], C["causal"], ALU.add)
                    nc.vector.drain()
                    nc.vector.tensor_reduce(out=negm[:, i % 2:i % 2 + 1], in_=S[:, i % 2, 0:W], axis=AX, op=ALU.max,
                                            negate=True).then_inc(max_done, 1)

                maxima(0)
                for i in range(PT):
                    if i + 1 < PT:
                        maxima(i + 1)
                    dve.wait_ge(pv_done, h * PT + i + 1)
                    nc.vector.reciprocal(rl, l[:, i % 2:i % 2 + 1])
                    nc.vector.drain()
                    nc.vector.tensor_scalar(attn[:, i, ds(h * DN, DN)], Op[:, 0:DN], rl, None, ALU.mult).then_inc(o_out, 1)


def sample_attention(env):
    nc, I, ar, C = env["nc"], env["I"], env["ar"], env["C"]
    qT, cT = ar.at(QT, P, H, TOK), ar.at(CT, P, 2, TOK)
    attnT = ar.at(AT, P, 4, TOK)
    w = VV
    pages = ar.at(w, P, GP, PGW); w += GP * PGW
    new_page = ar.at(w, P, PGW); w += PGW
    wuk = ar.at(w, P, 2, 512); w += 1024
    assert w <= ZL
    w = ZL + G * TOK
    wukT = ar.at(w, P, H, KL); w += H * KL
    wuv = ar.at(w, P, 2, 512); w += 1024
    qlat = ar.at(w, P, 2, H * NS); w += 2 * H * NS
    qrope = ar.at(w, P, H * NS); w += H * NS
    cTp = ar.at(w, P, 2, KL + P); w += 2 * (KL + P)
    sqp = ar.at(w, P, 2, 512); w += 1024
    assert w <= AT
    w = AT + 4 * TOK
    krsq = ar.at(w, P, GP, DR); w += GP * DR
    sskr = ar.at(w, P, GP); w += GP
    ssn = ar.at(w, P, GP, H); w += GP * H
    rk = ar.at(w, P, GP, H); w += GP * H
    sc = ar.at(w, P, GP, NS); w += GP * NS
    prob = ar.at(w, P, GP, NS); w += GP * NS
    pmax = ar.at(w, P, NS); w += NS
    small = ar.at(w, NS, 4); w += 4
    m, mnew, negm, corr = (small[:, j:j + 1] for j in range(4))
    gmax = ar.at(w, NS, 1); w += 1
    diag = ar.at(w, NS, NS); w += NS
    acc = ar.at(w, NS, KL + 1); w += KL + 1
    rl = ar.at(w, NS, 1); w += 1
    lat = ar.at(w, NS, KL); w += KL
    latT = ar.at(w, P, 2, H * NS); w += 2 * H * NS
    assert w <= QT, (w, QT)
    table = env["table"]
    GB = GROUPS + 1

    def by_batch(ap, h):
        return ap.rearrange("p (b h q) -> p h b q", b=DB, h=H)[:, h, :, :]

    with ExitStack() as ctx:
        sem = lambda n: ctx.enter_context(nc.semaphore(n))
        ps = ctx.enter_context(nc.psum_tensor("ps_d", [P, 8, 512], F32))
        loaded, shifted, qn_done = sem("d_loaded"), sem("d_shifted"), sem("d_qn_done")
        ql_done, ql_out, qr_done, qr_seen = sem("d_ql_done"), sem("d_ql_out"), sem("d_qr_done"), sem("d_qr_seen")
        page_in = [sem(f"d_page_in{j}") for j in range(GP)]
        new_in, zeroed = sem("d_new_in"), sem("d_zeroed")
        t_done, t_out, key_done, s_done, ksq_done, ks_done, kr_sq = (
            sem("d_" + n) for n in ("t_done", "t_out", "key", "s", "ksq", "ks", "kr_sq"))
        norm_in, norm_root, scaled, pm_done, pmT_done, m_done, corr_done, mb_done, shift_done, exp_done, pv_done, acc_out = (
            sem("d_" + n) for n in ("norm_in", "norm_root", "scaled", "pm", "pmT", "m", "corr", "mb", "sub", "exp", "pv", "acc_out"))
        lat_done, latT_done, latT_out, o_done, o_out = (sem("d_" + n) for n in ("lat", "latT", "latT_out", "o", "o_out"))
        block = ctx.enter_context(nc.Block())
        PPB = NPAGES + 1

        @block.sync
        def _(sp):
            sp.dma_start(table[:, :], I["page_table"]).then_inc(loaded, 16)
            sp.dma_start(wuk, I["w_uk"]).then_inc(loaded, 16)
            sp.dma_start(wukT[0:DN], I["w_ukT"]).then_inc(loaded, 16)
            sp.dma_start(wuv, I["w_uv"]).then_inc(loaded, 16)
            sp.wait_ge(qr_done, 1)
            sp.dma_start(qrope[0:DR, :], qrope[64:96, :]).then_inc(shifted, 16)
            sp.wait_ge(loaded, 64)
            sp.wait_ge(zeroed, 1)
            with sp.Fori(0, DB) as b:
                sp.wait_ge(pv_done, b * GB)
                sp.dma_start(new_page[0:DQ, 0:KL], env["new_rows"][ds(b * DQ, DQ), 0:KL]).then_inc(new_in, 16)
                sp.dma_start(new_page[0:DQ, KL + 1:PGW], env["new_rows"][ds(b * DQ, DQ), KL:KL + DR]).then_inc(new_in, 16)
                with sp.Fori(0, GROUPS) as g:
                    sp.wait_ge(pv_done, b * GB + g)
                    for j in range(GP):
                        page = sp.value_load(table[0:1, ds(b * NPAGES + g * GP + j, 1)], min_val=0, max_val=NPHYS - 1)
                        sp.dma_start(pages[:, j, 0:KL], I["cache_ckv"][ds(page, 1)].rearrange("a p c -> (a p) c")).then_inc(page_in[j], 16)
                        sp.dma_start(pages[:, j, KL + 1:PGW], I["cache_krope"][ds(page, 1)].rearrange("a p c -> (a p) c")).then_inc(page_in[j], 16)

        @block.gpsimd
        def _(pool):
            nc.gpsimd.memset(new_page, 0.0)
            nc.gpsimd.drain()
            nc.gpsimd.memset(new_page[:, KL:KL + 1], 1.0)
            for j in range(GP):
                nc.gpsimd.memset(pages[:, j, KL:KL + 1], 1.0)
            nc.gpsimd.drain().then_inc(zeroed, 1)

        @block.tensor
        def _(pe):
            pe.wait_ge(loaded, 64)
            for h in range(H):
                for k in range(2):
                    last = nc.tensor.matmul(ps[:, k, h * NS:(h + 1) * NS], wukT[0:DN, h, k * P:(k + 1) * P], qT[0:DN, h, SEQ:SEQ + NS],
                                            start=True, stop=True)
            last.then_inc(ql_done, 1)
            pe.wait_ge(ql_out, 2)
            pe.wait_ge(shifted, 16)

            def page(src, j, at, qcol):
                pe.wait_ge(t_out, at if j < 2 else at - 1)
                for k in range(2):
                    nc.tensor.transpose(ps[:, j % 2, k * P:(k + 1) * P], src[:, k * P:(k + 1) * P], C["ident"])
                nc.tensor.transpose(ps[0:DR, j % 2, KL:KL + P], src[:, KL + 1:PGW], C["ident"]).then_inc(t_done, 1)

            def keys(j, at, qcol):
                pe.wait_ge(t_out, at + 1)
                pe.wait_ge(ksq_done, at if j < 2 else at - 1)
                for k in range(2):
                    last = nc.tensor.matmul(ps[:, 2 + j % 2, :], cTp[:, j % 2, k * P:(k + 1) * P], wuk[:, k, :], start=k == 0, stop=k == 1)
                last.then_inc(key_done, 1)
                if j == 0:
                    pe.wait_ge(scaled, qcol[1])
                for k in range(2):
                    nc.tensor.matmul(ps[:, 4, j * NS:(j + 1) * NS], cTp[:, j % 2, k * P:(k + 1) * P], qlat[:, k, ds(qcol[0], NS)],
                                     start=k == 0, stop=False)
                nc.tensor.matmul(ps[:, 4, j * NS:(j + 1) * NS], cTp[0:DR, j % 2, KL:KL + P], qrope[0:DR, ds(qcol[0], NS)],
                                 start=False, stop=True).then_inc(s_done, 1)

            def group(srcs, at, gi, b):
                qcol = (b * H * DQ, gi)
                page(srcs[0], 0, at, qcol)
                for j in range(1, len(srcs)):
                    page(srcs[j], j, at + j, qcol)
                    keys(j - 1, at + j - 1, qcol)
                keys(len(srcs) - 1, at + len(srcs) - 1, qcol)
                wait_apart(pe, pm_done, gi + 1, (loaded, 64))
                nc.tensor.transpose(ps[0:NS, 5, 0:P], pmax, C["ident"]).then_inc(pmT_done, 1)
                pe.wait_ge(m_done, gi + 1)
                nc.tensor.matmul(ps[:, 5, 256:256 + NS], C["ones"][0:NS, :], diag, start=True, stop=True).then_inc(mb_done, 1)
                pe.wait_ge(exp_done, gi + 1)
                pe.wait_ge(acc_out, gi)
                for j, src in enumerate(srcs):
                    last = nc.tensor.matmul(ps[0:NS, 6, 0:KL + 1], prob[:, j, :], src[:, 0:KL + 1], start=j == 0, stop=j == len(srcs) - 1)
                last.then_inc(pv_done, 1)

            with pe.Fori(0, DB) as b:
                with pe.Fori(0, GROUPS) as g:
                    for j in range(GP):
                        pe.wait_ge(page_in[j], (b * GROUPS + g) * 32 + 32)
                    group([pages[:, j, :] for j in range(GP)], b * PPB + g * GP, b * GB + g, b)
                pe.wait_ge(new_in, b * 32 + 32)
                group([new_page], b * PPB + NPAGES, b * GB + GROUPS, b)
                pe.wait_ge(latT_out, b)
                wait_apart(pe, lat_done, b + 1, (loaded, 64))
                for k in range(2):
                    last = nc.tensor.transpose(ps[:, 7, k * NS:(k + 1) * NS], lat[:, k * P:(k + 1) * P], C["ident"][0:NS, 0:NS])
                last.then_inc(latT_done, 1)
            pe.wait_ge(latT_out, DB)
            for h in range(H):
                c = (h // 2) * NS
                for k in range(2):
                    last = nc.tensor.matmul(ps[(h % 2) * DN:(h % 2) * DN + DN, h % 2, c:c + NS], wuv[:, k, h * DN:(h + 1) * DN],
                                            latT[:, k, h * NS:(h + 1) * NS], start=k == 0, stop=k == 1)
            last.then_inc(o_done, 1)

        @block.scalar
        def _(act):
            act.wait_ge(ql_done, 1)
            for k in range(2):
                for h in range(H):
                    last = nc.scalar.activation(by_batch(qlat[:, k, :], h),
                                                ps[:, k, h * NS:(h + 1) * NS].rearrange("p (b q) -> p b q", b=DB), ACT.Copy)
                last.then_inc(ql_out, 1)

            def group(n, srcs, at, gi):
                for j in range(n):
                    act.wait_ge(t_done, at + j + 1)
                    act.wait_ge(s_done, at + j if j < 2 else at + j - 1)
                    nc.scalar.activation(cTp[:, j % 2, 0:KL], ps[:, j % 2, 0:KL], ACT.Copy)
                    nc.scalar.activation(cTp[0:DR, j % 2, KL:], ps[0:DR, j % 2, KL:KL + P], ACT.Copy)
                    nc.scalar.drain().then_inc(t_out, 1)
                    if j:
                        square(j - 1, at + j - 1)
                square(n - 1, at + n - 1)
                act.wait_ge(norm_in, gi)
                nc.scalar.activation(krsq[:, 0:n, :], srcs, ACT.Square).then_inc(kr_sq, 1)
                act.wait_ge(norm_in, gi + 1)
                nc.scalar.activation(rk[:, 0:n, :], rk[:, 0:n, :], ACT.Sqrt, bias=C["eps"], scale=1.0 / DH).then_inc(norm_root, 1)
                act.wait_ge(m_done, gi + 1)
                nc.scalar.activation(corr, m, ACT.Exp, bias=negm).then_inc(corr_done, 1)
                act.wait_ge(shift_done, gi + 1)
                nc.scalar.activation(prob[:, 0:n, :], sc[:, 0:n, :], ACT.Exp).then_inc(exp_done, 1)

            def square(j, at):
                act.wait_ge(key_done, at + 1)
                act.wait_ge(ks_done, at if j < 2 else at - 1)
                nc.scalar.activation(sqp[:, j % 2, :], ps[:, 2 + j % 2, :], ACT.Square).then_inc(ksq_done, 1)

            with act.Fori(0, DB) as b:
                with act.Fori(0, GROUPS) as g:
                    group(GP, pages[:, :, KL + 1:PGW], b * PPB + g * GP, b * GB + g)
                group(1, new_page[:, KL + 1:PGW].rearrange("p (a c) -> p a c", a=1), b * PPB + NPAGES, b * GB + GROUPS)
                act.wait_ge(latT_done, b + 1)
                for k in range(2):
                    dst = latT[:, k, :].rearrange("p (h t) -> p h t", h=H)[:, :, ds(b * DQ, DQ)]
                    last = nc.scalar.activation(dst, ps[:, 7, k * NS:(k + 1) * NS].rearrange("p (h q) -> p h q", h=H), ACT.Copy)
                nc.scalar.drain().then_inc(latT_out, 1)
            act.wait_ge(o_done, 1)
            for odd in range(2):
                rows = slice(odd * DN, odd * DN + DN)
                src = ps[rows, odd, 0:4 * NS].rearrange("p (k t) -> p k t", k=4)
                nc.scalar.activation(attnT[rows, :, SEQ:SEQ + NS], src, ACT.Copy)
                nc.scalar.activation(attnT[rows, :, SEQ + NS:TOK], src, ACT.Copy)

        @block.vector
        def _(dve):
            for h in range(H):
                last = nc.vector.tensor_copy(by_batch(qrope, h)[64:96], qT[64:96, h, SEQ:SEQ + NS].rearrange("p (b q) -> p b q", b=DB))
            last.then_inc(qr_done, 1)

            def group(n, at, gi, masked):
                for j in range(n):
                    dve.wait_ge(ksq_done, at + j + 1)
                    nc.vector.tensor_reduce(out=ssn[:, j, :], in_=sqp[:, j % 2, :].rearrange("p (h d) -> p h d", h=H), axis=AX,
                                            op=ALU.add).then_inc(ks_done, 1)
                dve.wait_ge(kr_sq, gi + 1)
                nc.vector.tensor_reduce(out=sskr[:, 0:n], in_=krsq[:, 0:n, :], axis=AX, op=ALU.add)
                nc.vector.drain()
                nc.vector.tensor_tensor(rk[:, 0:n, :], ssn[:, 0:n, :], sskr[:, 0:n].unsqueeze(2).to_broadcast([P, n, H]),
                                        ALU.add).then_inc(norm_in, 1)
                dve.wait_ge(norm_root, gi + 1)
                nc.vector.reciprocal(rk[:, 0:n, :], rk[:, 0:n, :])
                nc.vector.drain()
                dve.wait_ge(s_done, at + n)
                s4 = sc[:, 0:n, :].rearrange("p a (h q) -> p (a h) q", h=H)
                rkb = rk[:, 0:n, :].rearrange("p a h -> p (a h)").unsqueeze(2).to_broadcast([P, n * H, DQ])
                nc.vector.tensor_tensor(s4, ps[:, 4, 0:n * NS].rearrange("p (a q) -> p a q", q=DQ), rkb, ALU.mult).then_inc(scaled, 1)
                nc.vector.drain()
                if masked:
                    nc.vector.tensor_tensor(sc[:, 0, :], sc[:, 0, :], C["page_mask"], ALU.add)
                    nc.vector.drain()
                nc.vector.tensor_reduce(out=pmax, in_=sc[:, 0:n, :].rearrange("p a c -> p c a"), axis=AX, op=ALU.max).then_inc(pm_done, 1)
                dve.wait_ge(pmT_done, gi + 1)
                nc.vector.tensor_reduce(out=gmax, in_=ps[0:NS, 5, 0:P], axis=AX, op=ALU.max)
                nc.vector.drain()
                nc.vector.tensor_tensor(mnew, m, gmax, ALU.max)
                nc.vector.drain()
                nc.vector.tensor_scalar(diag, C["ident"][0:NS, 0:NS], mnew, None, ALU.mult)
                nc.vector.tensor_scalar(negm, mnew, -1.0, None, ALU.mult)
                nc.vector.drain().then_inc(m_done, 1)
                dve.wait_ge(mb_done, gi + 1)
                nc.vector.tensor_tensor(sc[:, 0:n, :], sc[:, 0:n, :], ps[:, 5, 256:256 + NS].unsqueeze(1).to_broadcast([P, n, NS]),
                                        ALU.subtract).then_inc(shift_done, 1)
                dve.wait_ge(corr_done, gi + 1)
                nc.vector.tensor_copy(m, mnew)
                dve.wait_ge(pv_done, gi + 1)
                nc.vector.scalar_tensor_tensor(out=acc, in0=acc, scalar=corr, in1=ps[0:NS, 6, 0:KL + 1], op0=ALU.mult,
                                               op1=ALU.add).then_inc(acc_out, 1)
                nc.vector.drain()

            with dve.Fori(0, DB) as b:
                nc.vector.memset(m, NEG)
                nc.vector.memset(acc, 0.0)
                nc.vector.drain()
                with dve.Fori(0, GROUPS) as g:
                    group(GP, b * PPB + g * GP, b * GB + g, False)
                group(1, b * PPB + NPAGES, b * GB + GROUPS, True)
                nc.vector.reciprocal(rl, acc[:, KL:KL + 1])
                nc.vector.drain()
                dve.wait_ge(latT_done, b)
                nc.vector.tensor_scalar(lat, acc[:, 0:KL], rl, None, ALU.mult).then_inc(lat_done, 1)
                nc.vector.drain()


def merge(env):
    nc, I, ar = env["nc"], env["I"], env["ar"]
    zl, attnT, mixed = ar.at(ZL, P, G, TOK), ar.at(AT, P, 4, TOK), ar.at(MT, P, KD, TOK)
    w = ZL + G * TOK
    ring = [ar.at(w + s * 24 * P, P, 24, P) for s in range(2)]; w += 48 * P
    sig = ar.at(w, P, 4, NW); w += 4 * NW
    assert w <= AT
    xnT = ar.at(MT + KD * TOK, P, KD, TOK)
    prod = ar.at(MT - 4 * NW, P, 4, NW)
    assert MT + 2 * KD * TOK <= TOP and MT - 4 * NW >= AT + 4 * TOK
    with ExitStack() as ctx:
        sem = lambda n: ctx.enter_context(nc.semaphore(n))
        ps = ctx.enter_context(nc.psum_tensor("ps_e", [P, 8, 512], F32))
        xn_in, w_in = sem("e_xn_in"), [sem(f"e_w_in{s}") for s in range(2)]
        gate_done, branch_done, sig_done, mix_done = (sem("e_" + n) for n in ("gate", "branch", "sig", "mix"))
        block = ctx.enter_context(nc.Block())

        @block.sync
        def _(sp):
            sp.dma_start(xnT, env["xn_dram"]).then_inc(xn_in, 16)
            for s in range(2):
                sp.dma_start(ring[s], I["w_merge"][s]).then_inc(w_in[s], 16)
            with sp.Fori(0, KD // 2 - 1) as dd:
                for s in range(2):
                    sp.wait_ge(branch_done, dd * 2 * NN + NN * (s + 1))
                    sp.dma_start(ring[s], I["w_merge"][ds(dd * 2 + 2 + s, 1)].rearrange("a p k c -> (a p) k c")).then_inc(w_in[s], 16)

        @block.tensor
        def _(pe):
            pe.wait_ge(xn_in, 16)
            with pe.Fori(0, KD // 2) as dd:
                for s in range(2):
                    pe.wait_ge(w_in[s], dd * 16 + 16)
                    for n in range(NN):
                        i = s * NN + n
                        c = slice(n * NW, (n + 1) * NW)
                        B = 4 * (i % 2)
                        pe.wait_ge(mix_done, dd * 2 * NN + max(i - 1, 0))
                        for a in range(2):
                            for k in range(KD):
                                last = nc.tensor.matmul(ps[:, B + a, 0:NW], ring[s][:, a * KD + k, :], xnT[:, k, c], start=k == 0, stop=k == KD - 1)
                        last.then_inc(gate_done, 1)
                        for a, src in enumerate((attnT, zl)):
                            for k in range(4):
                                last = nc.tensor.matmul(ps[:, B + 2 + a, 0:NW], ring[s][:, 16 + 4 * a + k, :], src[:, k, c], start=k == 0, stop=k == 3)
                        last.then_inc(branch_done, 1)

        @block.scalar
        def _(act):
            with act.Fori(0, KD // 2) as dd:
                for i in range(2 * NN):
                    act.wait_ge(gate_done, dd * 2 * NN + i + 1)
                    act.wait_ge(mix_done, dd * 2 * NN + max(i - 1, 0))
                    nc.scalar.activation(sig[:, 2 * (i % 2):2 * (i % 2) + 2, :], ps[:, 4 * (i % 2):4 * (i % 2) + 2, 0:NW],
                                         ACT.Sigmoid).then_inc(sig_done, 1)

        @block.vector
        def _(dve):
            with dve.Fori(0, KD // 2) as dd:
                for i in range(2 * NN):
                    s, n, h = i // NN, i % NN, 2 * (i % 2)
                    dve.wait_ge(sig_done, dd * 2 * NN + i + 1)
                    dve.wait_ge(branch_done, dd * 2 * NN + i + 1)
                    nc.vector.tensor_tensor(prod[:, h:h + 2, :], sig[:, h:h + 2, :], ps[:, 2 * h + 2:2 * h + 4, 0:NW], ALU.mult)
                    nc.vector.drain()
                    nc.vector.tensor_tensor(one(mixed[:, ds(dd * 2 + s, 1), n * NW:(n + 1) * NW]), prod[:, h, :], prod[:, h + 1, :],
                                            ALU.add).then_inc(mix_done, 1)


def residual(env):
    nc, I, ar, C = env["nc"], env["I"], env["ar"], env["C"]
    mixed = ar.at(MT, P, KD, TOK)
    yall, xn2, xn2T = ar.at(YALL, P, NT, D), ar.at(XN2, P, NT, D), ar.at(XN2T, P, KD, TOK)
    w = MT + KD * TOK
    wout = ar.at(w, P, KD, D); w += KD * D
    mt = ar.at(w, P, KD, P); w += D
    xt = ar.at(w, P, D); w += D
    w2 = ar.at(w, P, D); w += D
    xn = ar.at(w, P, D); w += D
    hh = ar.at(w, P, D); w += D
    st = ar.at(w, P, 2); w += 2
    assert w <= TOP, (w, TOP)
    with ExitStack() as ctx:
        sem = lambda n: ctx.enter_context(nc.semaphore(n))
        ps = ctx.enter_context(nc.psum_tensor("ps_f", [P, 8, 512], F32))
        loaded, x_in = sem("f_loaded"), sem("f_x_in")
        m_copied, h_done, h_out, ss_done, std_done, xn_done, xn_copied, t_done, t_out = (
            sem("f_" + n) for n in ("m_copied", "h", "h_out", "ss", "std", "xn", "xn_copied", "t", "t_out"))
        block = ctx.enter_context(nc.Block())

        @block.sync
        def _(sp):
            sp.dma_start(wout, I["w_out"]).then_inc(loaded, 16)
            sp.dma_start(w2, I["norm2"]).then_inc(loaded, 16)
            with sp.Fori(0, NT) as t:
                sp.wait_ge(h_out, t)
                sp.dma_start(xt, I["x_tok"][ds(t, 1)].rearrange("a p c -> (a p) c")).then_inc(x_in, 16)

        @block.gpsimd
        def _(pool):
            with pool.Fori(0, NT) as t:
                pool.wait_ge(h_done, t)
                nc.gpsimd.tensor_copy(mt, mixed[:, :, ds(t * P, P)]).then_inc(m_copied, 1)

        @block.tensor
        def _(pe):
            pe.wait_ge(loaded, 32)
            with pe.Fori(0, NT) as t:
                pe.wait_ge(m_copied, t + 1)
                pe.wait_ge(h_out, t)
                for c in range(2):
                    for k in range(KD):
                        last = nc.tensor.matmul(ps[:, c, :], mt[:, k, :], wout[:, k, c * 512:(c + 1) * 512], start=k == 0, stop=k == KD - 1)
                last.then_inc(h_done, 1)
                pe.wait_ge(xn_done, t + 1)
                pe.wait_ge(t_out, t)
                for k in range(KD):
                    last = nc.tensor.transpose(ps[:, 2 + k // 4, (k % 4) * P:(k % 4 + 1) * P], xn[:, k * P:(k + 1) * P], C["ident"])
                last.then_inc(t_done, 1)

        @block.scalar
        def _(act):
            with act.Fori(0, NT) as t:
                act.wait_ge(h_out, t + 1)
                act.wait_ge(t_done, t)
                act.wait_ge(xn_copied, t)
                nc.scalar.activation(xn, hh, ACT.Square, accum_out=st[:, 0:1])
                nc.scalar.drain()
                nc.scalar.activation(st[:, 1:2], st[:, 0:1], ACT.Sqrt, bias=C["eps"], scale=1.0 / D).then_inc(std_done, 1)
                act.wait_ge(xn_done, t + 1)
                nc.scalar.activation(one(xn2[:, ds(t, 1), :]), xn, ACT.Copy).then_inc(xn_copied, 1)
                act.wait_ge(t_done, t + 1)
                nc.scalar.activation(xn2T[:, :, ds(t * P, P)], ps[:, 2:4, :].rearrange("p a (b c) -> p (a b) c", b=4), ACT.Copy).then_inc(t_out, 1)

        @block.vector
        def _(dve):
            with dve.Fori(0, NT) as t:
                dve.wait_ge(h_done, t + 1)
                dve.wait_ge(x_in, t * 16 + 16)
                nc.vector.tensor_tensor(hh, ps[:, 0:2, :].rearrange("p a b -> p (a b)"), xt, ALU.add).then_inc(h_out, 1)
                nc.vector.drain()
                nc.vector.tensor_copy(one(yall[:, ds(t, 1), :]), hh)
                dve.wait_ge(std_done, t + 1)
                nc.vector.reciprocal(st[:, 1:2], st[:, 1:2])
                nc.vector.drain()
                nc.vector.scalar_tensor_tensor(out=xn, in0=hh, scalar=st[:, 1:2], in1=w2, op0=ALU.mult, op1=ALU.mult).then_inc(xn_done, 1)
            nc.vector.drain()
            nc.vector.memset(yall[NS:P, NT - 1, :], 0.0)


def peer_scores(env):
    nc, I, ar = env["nc"], env["I"], env["ar"]
    xn2T, s_all = ar.at(XN2T, P, KD, TOK), ar.at(SALL_AT, P, NT * H * 2, NK)
    w = RING_AT
    ring = [ar.at(w + s * 9 * P, P, 9, P) for s in range(2)]; w += 18 * P
    qb = [ar.at(w + s * TOK, P, TOK) for s in range(2)]; w += 2 * TOK
    assert w <= TOP, (w, TOP)
    with ExitStack() as ctx:
        sem = lambda n: ctx.enter_context(nc.semaphore(n))
        pq = ctx.enter_context(nc.psum_tensor("ps_g", [P, 4, 512], F32))
        pk = ctx.enter_context(nc.psum_tensor("ps_g2", [P, 3, 512], F32))
        w_in = [sem(f"g_w_in{s}") for s in range(2)]
        q_done, q_out, k_done, k_out = (sem("g_" + n) for n in ("q", "q_out", "k", "k_out"))
        block = ctx.enter_context(nc.Block())

        @block.sync
        def _(sp):
            for s in range(2):
                sp.dma_start(ring[s], I["w_peer"][s]).then_inc(w_in[s], 16)
            with sp.Fori(0, H - 1) as h:
                for s in range(2):
                    sp.wait_ge(k_done, h * 6 + 3 * (s + 1))
                    sp.dma_start(ring[s], I["w_peer"][ds(h * 2 + 2 + s, 1)].rearrange("a p k c -> (a p) k c")).then_inc(w_in[s], 16)

        @block.tensor
        def _(pe):
            with pe.Fori(0, H) as h:
                for s in range(2):
                    pe.wait_ge(w_in[s], h * 16 + 16)
                    for n in range(NN):
                        i = s * NN + n
                        pe.wait_ge(q_out, h * 6 + max(i - 2, 0))
                        for k in range(KD):
                            last = nc.tensor.matmul(pq[:, i % 3, 0:NW], ring[s][:, k, :], xn2T[:, k, n * NW:(n + 1) * NW], start=k == 0, stop=k == KD - 1)
                        last.then_inc(q_done, 1)
                    for n in range(NN):
                        i = s * NN + n
                        pe.wait_ge(q_out, h * 6 + i + 1)
                        pe.wait_ge(k_out, h * 6 + max(i - 2, 0))
                        for t in range(3):
                            last = nc.tensor.matmul(pk[:, n, t * P:(t + 1) * P], qb[s][:, (3 * n + t) * P:(3 * n + t + 1) * P], ring[s][:, 8, :],
                                                    start=True, stop=True)
                        last.then_inc(k_done, 1)

        @block.scalar
        def _(act):
            with act.Fori(0, H) as h:
                for i in range(6):
                    act.wait_ge(q_done, h * 6 + i + 1)
                    act.wait_ge(k_done, h * 6)
                    nc.scalar.activation(qb[i // 3][:, (i % 3) * NW:(i % 3 + 1) * NW], pq[:, i % 3, 0:NW], ACT.Copy).then_inc(q_out, 1)

        @block.vector
        def _(dve):
            sv = s_all.rearrange("p (t x) k -> p t x k", t=NT)
            with dve.Fori(0, H) as h:
                for i in range(6):
                    s, n = i // 3, i % 3
                    dve.wait_ge(k_done, h * 6 + i + 1)
                    for t in range(3):
                        last = nc.vector.tensor_copy(one(s_all[:, ds((3 * n + t) * 2 * H + h * 2 + s, 1), :]), pk[:, n, t * P:(t + 1) * P])
                    nc.vector.drain().then_inc(k_out, 1)
            nc.vector.tensor_copy(sv[NS:P, NT - 1, 0:H, :], sv[NS:P, NT - 1, H:2 * H, :])


def route(env):
    nc, ar, C = env["nc"], env["ar"], env["C"]
    s_all = ar.at(SALL_AT, P, NT * H * 2 * NK)
    ids, gates = env["ids"], env["gates"]
    w = RING_AT
    s = ar.at(w, P, 2, NK); w += 2 * NK
    s2 = ar.at(w, P, 2, NK); w += 2 * NK
    top = ar.at(w, P, 2, TOPK); w += 2 * TOPK
    topi = ar.at(w, P, 2, TOPK).bitcast(U32); w += 2 * TOPK
    topf = ar.at(w, P, 2, TOPK); w += 2 * TOPK
    cand = ar.at(w, P, TOPK, TOPK); w += TOPK * TOPK
    cand2 = ar.at(w, P, TOPK * TOPK); w += TOPK * TOPK
    best = ar.at(w, P, TOPK); w += TOPK
    pos = ar.at(w, P, TOPK).bitcast(U32); w += TOPK
    hilo = ar.at(w, P, 2, TOPK).bitcast(U32); w += 2 * TOPK
    hilof = ar.at(w, P, 2, TOPK); w += 2 * TOPK
    hit = ar.at(w, P, 2 * TOPK, TOPK); w += 2 * TOPK * TOPK
    e2 = ar.at(w, P, 2, TOPK); w += 2 * TOPK
    ef = ar.at(w, P, TOPK); w += TOPK
    negb = ar.at(w, P, 1); w += 1
    sm = ar.at(w, P, 1); w += 1
    ex = ar.at(w, P, TOPK); w += TOPK
    candf = cand.rearrange("p a b -> p (a b)")
    with ExitStack() as ctx:
        sem = lambda n: ctx.enter_context(nc.semaphore(n))
        s_in, s_used, b_done, e_done, g_done = (sem("h_" + n) for n in ("s_in", "s_used", "best", "exp", "gates"))
        block = ctx.enter_context(nc.Block())

        @block.gpsimd
        def _(pool):
            with pool.Fori(0, ROUTES) as r:
                pool.wait_ge(s_used, r)
                nc.gpsimd.tensor_copy(s.rearrange("p a b -> p (a b)"), s_all[:, ds(r * 2 * NK, 2 * NK)]).then_inc(s_in, 1)

        @block.scalar
        def _(act):
            with act.Fori(0, ROUTES) as r:
                act.wait_ge(b_done, r + 1)
                act.wait_ge(g_done, r)
                nc.scalar.activation(ex, best, ACT.Exp, bias=negb, accum_out=sm).then_inc(e_done, 1)

        @block.vector
        def _(dve):
            v, fence = nc.vector, nc.vector.drain
            with dve.Fori(0, ROUTES) as r:
                wait_apart(dve, s_in, r + 1, (s_in, 1))
                for p in range(2):
                    v.max(out=top[:, p, 0:8], in_=s[:, p, :])
                fence()
                for p in range(2):
                    v.max_index(out=topi[:, p, 0:8], in_max=top[:, p, 0:8], in_values=s[:, p, :])
                    v.match_replace(out=s2[:, p, :], in_to_replace=top[:, p, 0:8], in_values=s[:, p, :], imm_value=LOWEST)
                fence().then_inc(s_used, 1)
                for p in range(2):
                    v.max(out=top[:, p, 8:16], in_=s2[:, p, :])
                fence()
                for p in range(2):
                    v.max_index(out=topi[:, p, 8:16], in_max=top[:, p, 8:16], in_values=s2[:, p, :])
                v.tensor_tensor(cand, top[:, 0, :].unsqueeze(2).to_broadcast([P, TOPK, TOPK]),
                                top[:, 1, :].unsqueeze(1).to_broadcast([P, TOPK, TOPK]), ALU.add)
                fence()
                v.tensor_copy(topf, topi)
                v.max(out=best[:, 0:8], in_=candf)
                fence()
                v.tensor_scalar(topf[:, 0, :], topf[:, 0, :], float(NK), None, ALU.mult)
                v.max_index(out=pos[:, 0:8], in_max=best[:, 0:8], in_values=candf)
                v.match_replace(out=cand2, in_to_replace=best[:, 0:8], in_values=candf, imm_value=LOWEST)
                v.tensor_scalar(negb, best[:, 0:1], -1.0, None, ALU.mult)
                fence()
                v.max(out=best[:, 8:16], in_=cand2)
                fence().then_inc(b_done, 1)
                v.max_index(out=pos[:, 8:16], in_max=best[:, 8:16], in_values=cand2)
                fence()
                v.tensor_scalar(hilo[:, 0, :], pos, 4, None, ALU.logical_shift_right)
                v.tensor_scalar(hilo[:, 1, :], pos, TOPK - 1, None, ALU.bitwise_and)
                fence()
                v.tensor_copy(hilof, hilo)
                fence()
                v.tensor_tensor(hit, hilof.rearrange("p a b -> p (a b)").unsqueeze(2).to_broadcast([P, 2 * TOPK, TOPK]),
                                C["iota16"].unsqueeze(1).to_broadcast([P, 2 * TOPK, TOPK]), ALU.is_equal)
                fence()
                h4 = hit.rearrange("p (a b) c -> p a b c", a=2)
                v.tensor_tensor(h4, h4, topf.unsqueeze(2).to_broadcast([P, 2, TOPK, TOPK]), ALU.mult)
                fence()
                v.tensor_reduce(out=e2, in_=h4, axis=AX, op=ALU.add)
                fence()
                v.tensor_tensor(ef, e2[:, 0, :], e2[:, 1, :], ALU.add)
                fence()
                v.tensor_copy(ids[:, ds(r * TOPK, TOPK)], ef)
                dve.wait_ge(e_done, r + 1)
                v.reciprocal(sm, sm)
                fence()
                v.tensor_scalar(gates[:, ds(r * TOPK, TOPK)], ex, sm, None, ALU.mult)
                fence().then_inc(g_done, 1)


def peer(env):
    nc, I, O, ar, C = (env[k] for k in ("nc", "I", "O", "ar", "C"))
    yall, xn2 = ar.at(YALL, P, NT, D), ar.at(XN2, P, NT, D)
    ids, gates = env["ids"], env["gates"]
    w = XN2 + NT * D
    u_ring = ar.at(w, P, RING, D); w += RING * D
    v_ring = ar.at(w, P, RING, D); w += RING * D
    diag = ar.at(w, P, TOPK, P); w += TOPK * P
    xcur = ar.at(w, P, D); w += D
    scratch = ar.at(w, P, D); w += D
    uid = [ar.at(w + 8 * j, P, 8).bitcast(U32) for j in range(2)]; w += 16
    vid = [ar.at(w + 8 * j, P, 8).bitcast(U32) for j in range(2)]; w += 16
    a, a2, th, wt = (ar.at(w + 16 * j, P, TOPK) for j in range(4)); w += 64
    assert w <= TOP, (w, TOP)
    with ExitStack() as ctx:
        sem = lambda n: ctx.enter_context(nc.semaphore(n))
        acc = ctx.enter_context(nc.psum_tensor("ps_acc", [P, 2, 512], F32))
        fold_ps = ctx.enter_context(nc.psum_tensor("ps_fold", [NS, 2, 512], F32))
        u_in, v_in = [sem(f"i_u_in{j}") for j in range(RING)], [sem(f"i_v_in{j}") for j in range(RING)]
        uid_set, vid_set, u_used, v_used = (sem("i_" + n) for n in ("uid", "vid", "u_used", "v_used"))
        x_set, act_in, tanh_done, w_done, diag_done, acc_done, acc_out = (
            sem("i_" + n) for n in ("x_set", "act_in", "tanh", "w", "diag", "acc", "acc_out"))
        fold_done, fold_out, stored = sem("i_fold"), sem("i_fold_out"), sem("i_stored")
        block = ctx.enter_context(nc.Block())

        def gather(ring, j, idx, table, done):
            nc.gpsimd.indirect_dma_start(out=ring[:, j, :], out_offset=None, in_=I[table],
                                         in_offset=bass.IndirectOffsetOnAxis(ap=idx, axis=0)).then_inc(done[j], 16)

        @block.gpsimd
        def _(pool):
            for half in range(2):
                nc.gpsimd.tensor_copy(uid[half], ids[:, half * 8:half * 8 + 8]).then_inc(uid_set, 1)
                pool.wait_ge(uid_set, half + 1)
                for j in range(RING):
                    if half:
                        pool.wait_ge(u_used, j + 1)
                    gather(u_ring, j, uid[half][:, j:j + 1], "peer_u", u_in)

            def step(r, more, first=False):
                for half in range(2):
                    if more:
                        pool.wait_ge(u_used, r * 16 + half * 8 + 8)
                        nc.gpsimd.tensor_copy(uid[half], ids[:, ds((r + 1) * TOPK + half * 8, 8)]).then_inc(uid_set, 1)
                        pool.wait_ge(uid_set, r * 2 + half + 3)
                    if half or not first:
                        pool.wait_ge(v_used, r * 16 + half * 8 - 8)
                    nc.gpsimd.tensor_copy(vid[half], ids[:, ds(r * TOPK + half * 8, 8)]).then_inc(vid_set, 1)
                    pool.wait_ge(vid_set, r * 2 + half + 1)
                    for j in range(RING):
                        if more:
                            wait_apart(pool, u_used, r * 16 + half * 8 + 8 + j + 1, (uid_set, 1))
                            gather(u_ring, j, uid[half][:, j:j + 1], "peer_u", u_in)
                        if half or not first:
                            wait_apart(pool, v_used, r * 16 + half * 8 - 8 + j + 1, (vid_set, 1))
                        gather(v_ring, j, vid[half][:, j:j + 1], "peer_v", v_in)

            step(0, True, first=True)
            with pool.Fori(1, ROUTES - 1) as r:
                step(r, True)
            step(ROUTES - 1, False)

        @block.scalar
        def _(act):
            def set_x(t):
                nc.scalar.activation(xcur, t, ACT.Copy).then_inc(x_set, 1)

            def tanh(n):
                act.wait_ge(act_in, n)
                nc.scalar.activation(th, th, ACT.Tanh, scale=0.7978845608028654).then_inc(tanh_done, 1)

            set_x(xn2[:, 0, :])
            tanh(1)

            def step(r, more):
                if more:
                    act.wait_ge(u_used, r * 16 + 16)
                    set_x(one(xn2[:, ds((r + 1) // H, 1), :]))
                act.wait_ge(w_done, r + 1)
                act.wait_ge(v_used, r * 16)
                for s in range(TOPK):
                    nc.scalar.activation(diag[:, s, :], C["ident"], ACT.Copy, scale=wt[:, s:s + 1]).then_inc(diag_done, 1)
                if more:
                    tanh(r + 2)

            with act.Fori(0, ROUTES - 1) as r:
                step(r, True)
            step(ROUTES - 1, False)

        @block.tensor
        def _(pe):
            def step(r):
                pe.wait_ge(acc_out, r)
                for s in range(TOPK):
                    pe.wait_ge(diag_done, r * 16 + s + 1)
                    pe.wait_ge(v_in[s % RING], (r * 2 + s // RING) * 16 + 16)
                    for c in range(2):
                        last = nc.tensor.matmul(acc[:, c, :], diag[:, s, :], v_ring[:, s % RING, c * 512:(c + 1) * 512],
                                                start=s == 0, stop=s == TOPK - 1)
                    last.then_inc(v_used, 1)

            with pe.Fori(0, ROUTES) as r:
                step(r)
            pe.wait_ge(acc_out, ROUTES)
            for c in range(2):
                last = nc.tensor.matmul(fold_ps[:, c, :], C["fold"], yall[:, NT - 1, c * 512:(c + 1) * 512], start=True, stop=True)
            last.then_inc(fold_done, 1)

        @block.vector
        def _(dve):
            v, fence = nc.vector, nc.vector.drain

            def dots(r, at, after=None):
                for s in range(TOPK):
                    if s == 0:
                        dve.wait_ge(x_set, at + 1)
                    dve.wait_ge(u_in[s % RING], (at * 2 + s // RING) * 16 + 16)
                    v.tensor_tensor_reduce(out=u_ring[:, s % RING, :], in0=u_ring[:, s % RING, :], in1=xcur, scale=1.0, scalar=0.0,
                                           op0=ALU.mult, op1=ALU.add, accum_out=a[:, s:s + 1]).then_inc(u_used, 1)
                    if after and s == 3:
                        after()
                fence()
                v.tensor_tensor(a2, a, a, ALU.mult)
                fence()
                v.tensor_scalar(a2, a2, 0.044715, 1.0, ALU.mult, ALU.add)
                fence()
                v.tensor_tensor(th, a2, a, ALU.mult)
                fence().then_inc(act_in, 1)
                v.scalar_tensor_tensor(out=a2, in0=a, scalar=0.5, in1=gates[:, ds(r * TOPK, TOPK)], op0=ALU.mult, op1=ALU.mult)
                fence()
                dve.wait_ge(tanh_done, at + 1)
                dve.wait_ge(diag_done, at * 16)
                v.scalar_tensor_tensor(out=wt, in0=th, scalar=1.0, in1=a2, op0=ALU.add, op1=ALU.mult).then_inc(w_done, 1)

            def collect(r):
                dve.wait_ge(v_used, r * 16 + 16)
                y = one(yall[:, ds(r // H, 1), :])
                v.tensor_tensor(y, y, acc[:, :, :].rearrange("p a b -> p (a b)"), ALU.add).then_inc(acc_out, 1)
                fence()

            dots(0, 0)
            with dve.Fori(0, ROUTES - 1) as r:
                dots(r + 1, r + 1)
                collect(r)
            collect(ROUTES - 1)
            dve.wait_ge(fold_done, 1)
            v.tensor_copy(scratch[0:NS, :], fold_ps[:, :, :].rearrange("p a b -> p (a b)")).then_inc(fold_out, 1)

        @block.sync
        def _(sp):
            sp.wait_ge(acc_out, ROUTES)
            sp.dma_start(O["y_prompt"].rearrange("(t p) d -> p t d", p=P), yall[:, 0:PT, :]).then_inc(stored, 16)
            sp.wait_ge(fold_out, 1)
            sp.dma_start(O["y_sample"], scratch[0:NS, :]).then_inc(stored, 16)
            sp.wait_ge(stored, 32)


SALL_AT = XN2T + KD * TOK
RING_AT = SALL_AT + NT * H * 2 * NK

_OUTS = {"y_prompt": (SEQ, D), "y_sample": (NS, D), "ckvT": (P, 2, TOK), "kropeT": (DR, TOK),
         "poolT": (P, G, STATE), "poolsT": (P, G, DB, STATE)}


def constants():
    import numpy as np
    ident = np.eye(P, dtype=np.float32)
    k, q = np.arange(P), np.arange(P)
    causal = np.where(k[None, :] <= q[:, None], 0.0, NEG)
    hq = np.arange(NS) % DQ
    page_mask = np.where((k[:, None] < DQ) & (k[:, None] <= hq[None, :]), 0.0, NEG)
    inv = np.zeros((G, PAD))
    for g in range(G):
        inv[g] = 1.0 / np.minimum(np.arange(PAD) + 1, 2 << g)
    half = DR // 2
    pos = np.concatenate([np.arange(SEQ), 4096 + np.tile(np.arange(DQ), 2 * DB)]).astype(np.float32)
    freq = np.float32(10000.0) ** (-np.arange(half, dtype=np.float32) / np.float32(half))
    ang = (pos[None, :] * freq[:, None]).astype(np.float32)
    cos = np.concatenate([np.cos(ang)] * 2).astype(np.float32)
    sin = np.concatenate([-np.sin(ang), np.sin(ang)]).astype(np.float32)
    return dict(ident=ident, causal=causal, page_mask=page_mask, iota16=np.tile(np.arange(TOPK), (P, 1)),
                invcnt=np.tile(inv.reshape(1, -1), (P, 1)), fold=ident[:, 0:NS] + ident[:, NS:P]), cos, sin


def kernel(**inp):
    import numpy as np
    import concourse.bacc as bacc
    from concourse.bass_utils import run_bass_kernel_spmd

    A = {k: np.asarray(v) for k, v in inp.items()}

    def chunked(w):
        return w.reshape(w.shape[0] // P, P, w.shape[1]).transpose(1, 0, 2)

    def cols(w):
        return w.reshape(-1, P).T

    xs = A["x_sample"].reshape(NS, D)
    x = np.concatenate([A["x_prompt"][0], xs, xs])
    win = A["w_in"][0]
    o_kr, o_pool, o_gate = QL + KL, QL + KL + DR, QL + KL + DR + G * P
    swap = np.r_[DR // 2:DR, 0:DR // 2]
    kr = win[:, o_kr:o_pool]
    front = np.concatenate([win[:, 0:o_kr], win[:, o_pool:o_gate], kr, kr[:, swap]], axis=1)
    wq = A["w_q_up"][0]
    tables, cos, sin = constants()
    norms = dict(ones=np.ones((P, P)), w1=cols(A["norm1_w"][0]), wq_lat=cols(A["q_lat_norm_w"][0]), wkv=cols(A["kv_lat_norm_w"][0]),
                 pool_scale=cols(A["pool_scale"][0]), eps=np.full((P, 1), EPS),
                 wqk=np.zeros((P, 1), np.float32))
    consts = np.concatenate([np.asarray({**tables, **norms}[n], np.float32) for n, _ in CONSTS], axis=1)
    merge_w = np.stack([np.concatenate([chunked(win[:, o_gate + a * D + d * P:o_gate + a * D + (d + 1) * P]) for a in range(2)]
                                       + [chunked(A[n][0][:, d * P:(d + 1) * P]) for n in ("w_attn_br", "w_pool_br")], axis=1)
                        for d in range(KD)])
    keys = A["peer_keys"][0].reshape(2 * H, NK, P).transpose(0, 2, 1)
    peer_w = np.stack([np.concatenate([chunked(A["peer_w_q"][0][:, j * P:(j + 1) * P]), keys[j][:, None, :]], axis=1) for j in range(2 * H)])
    arrays = {
        "consts": consts, "qk_norms": np.stack([A["q_norm_w"][0], A["k_norm_w"][0]], axis=1),
        "xT": chunked(x.T), "x_tok": x.reshape(NT, P, D), "cos": cos, "sin": sin,
        "w_front": chunked(front), "w_q_up": chunked(wq.reshape(QL, H * DH)), "w_q_sw": chunked(wq[:, :, DN + swap].reshape(QL, H * DR)),
        "w_uk": chunked(A["w_uk"][0].reshape(KL, H * DN)), "w_ukT": A["w_uk"][0].transpose(2, 1, 0),
        "w_uv": chunked(A["w_uv"][0].reshape(KL, H * DN)), "pool_lin": A["pool_lin_w"][0].transpose(1, 0, 2),
        "stateT": A["state_pool"][0].reshape(DB, STATE, G, P).transpose(3, 2, 0, 1),
        "page_table": A["page_table"].reshape(1, DB * NPAGES), "cache_ckv": A["cache_ckv"][0], "cache_krope": A["cache_krope"][0],
        "w_merge": merge_w, "w_out": chunked(A["w_out"][0]), "norm2": np.tile(A["norm2_w"], (P, 1)), "w_peer": peer_w,
        "peer_u": A["peer_u"][0], "peer_v": A["peer_v"][0],
    }
    nc = bacc.Bacc("TRN2", target_bir_lowering=False, num_devices=1)
    ins, feed = {}, {}
    for name, a in arrays.items():
        a = np.ascontiguousarray(a)
        feed["in_" + name] = a
        ins[name] = nc.dram_tensor("in_" + name, a.shape, mybir.dt.from_np(a.dtype), kind="ExternalInput").ap()
    outs = {name: nc.dram_tensor("out_" + name, shape, F32, kind="ExternalOutput").ap() for name, shape in _OUTS.items()}
    build(nc, ins, outs)
    res = run_bass_kernel_spmd(nc, [feed], core_ids=[0]).results[0]
    got = {name: np.asarray(res["out_" + name]) for name in _OUTS}
    ckv = got["ckvT"].transpose(2, 1, 0).reshape(TOK, KL)
    kro = got["kropeT"].T
    return (got["y_prompt"].reshape(1, SEQ, D), got["y_sample"].reshape(DB, DQ, D),
            ckv[0:SEQ].reshape(1, 1, SEQ, KL), kro[0:SEQ].reshape(1, 1, SEQ, DR),
            got["poolT"].transpose(2, 1, 0).reshape(1, 1, STATE, G * P),
            ckv[SEQ:SEQ + NS].reshape(1, DB, DQ, KL), kro[SEQ:SEQ + NS].reshape(1, DB, DQ, DR),
            got["poolsT"].transpose(2, 3, 1, 0).reshape(1, DB, STATE, G * P))
```

```python
from contextlib import ExitStack

import concourse.bass as bass
from concourse import mybir

F32 = mybir.dt.float32
U32 = mybir.dt.uint32
I32 = mybir.dt.int32
ALU = mybir.AluOpType
ACT = mybir.ActivationFunctionType
AX = mybir.AxisListType.X
ds = bass.ds

D, SEQ, DB, DQ = 1024, 1024, 8, 8
P = 128
KD = D // P
NS = DB * DQ
TOK = SEQ + 2 * NS
NT = TOK // P
PT = SEQ // P
NW = 384
NN = TOK // NW
H, DN, DR, DH = 8, 64, 32, 96
QL, KL = 384, 256
G, STATE = 4, 15
PAD = 16
PAGE, NPAGES, NPHYS = 128, 32, 320
GP = 4
GROUPS = NPAGES // GP
PGW = KL + 1 + DR
NK, TOPK = 128, 16
NEXP = NK * NK
ROUTES = PT * H + H // 2
NEG = -1e30
LOWEST = -3.0e38
EPS = 1e-6
RING = 8
W_FRONT = QL + KL + 4 * P + 2 * DR


class Arena:

    def __init__(self, tensor):
        self.tensor = tensor

    def at(self, word, parts, *dims):
        n = 1
        for d in dims:
            n *= d
        v = self.tensor[0:parts, word:word + n]
        if len(dims) == 2:
            return v.rearrange("p (a b) -> p a b", a=dims[0])
        if len(dims) == 3:
            return v.rearrange("p (a b c) -> p a b c", a=dims[0], b=dims[1])
        return v


def wait_apart(eng, sem, value, met):
    value = eng.compute_val(value)
    eng.wait_ge(*met)
    eng.wait_ge(sem, value)


def one(ap):
    return ap.rearrange("p a b -> p (a b)")


def build(nc, I, O):
    with ExitStack() as ctx:
        ar = Arena(ctx.enter_context(nc.sbuf_tensor("arena", [P, TOP], F32)))
        const = ctx.enter_context(nc.sbuf_tensor("const", [P, CONST_COLS], F32))
        xn_dram = nc.dram_tensor("xn_spill", [P, KD, TOK], F32, kind="Internal").ap()
        new_rows = nc.dram_tensor("new_rows", [P, KL + DR], F32, kind="Internal").ap()
        table = ctx.enter_context(nc.sbuf_tensor("page_ids", [1, DB * NPAGES], I32))
        qk_norms = ctx.enter_context(nc.sbuf_tensor("qk_norms", [DH, 2], F32))
        s_dram = nc.dram_tensor("key_scores", [P, NT * H, 2 * NK], F32, kind="Internal").ap()

        C = {}
        col = 0
        for name, w in CONSTS:
            C[name] = const[:, col:col + w]
            col += w
        env = dict(nc=nc, I=I, O=O, ar=ar, C=C, const=const, xn_dram=xn_dram, new_rows=new_rows, s_dram=s_dram,
                   table=table, qk_norms=qk_norms, ids=ar.at(LATE, P, N_IDS).bitcast(U32), gates=ar.at(LATE + N_IDS, P, N_IDS))
        early = []

        def early_sem(name):
            early.append(nc.alloc_semaphore(name))
            return early[-1]

        env["early_sem"] = early_sem
        project(env)
        pool_and_values(env)
        prompt_attention(env)
        nc.clear_and_free_semaphores(early)
        nc.all_engine_barrier()
        sample_queries(env)
        prompt = Part(env, "p", 0, PT, 512, ar.at(AT, P, 4, TOK), ar.at(ZL, P, G, TOK), (YALL + PT * D, XN2 + PT * D))
        merge(env, prompt)
        residual(env, prompt)
        peer_scores(env, prompt)
        peer(env, "p", 0, PT * H, True)
        sample_output(env)
        sample = Part(env, "s", PT, 1, P, ar.at(ATS, P, 4, P), ar.at(ZLS, P, G, P), (YALL, YALL + D))
        merge(env, sample)
        residual(env, sample)
        peer_scores(env, sample)
        peer(env, "s", PT * H, H // 2, False)


CONSTS = [("ident", P), ("ones", P), ("causal", P), ("page_mask", NS), ("iota16", TOPK), ("w1", KD), ("wq_lat", 3),
          ("wkv", 2), ("wqk", 1), ("pool_scale", G), ("invcnt", G * PAD), ("eps", 1), ("fold", NS)]
CONST_COLS = sum(w for _, w in CONSTS)

TOP = 52000
N_IDS = ROUTES * TOPK
ZLS = TOP - G * P
QROPE = ZLS - H * NS
QLAT = QROPE - 2 * H * NS
ATS = QLAT - 4 * P
LATT = ATS - 2 * H * NS
LATE = LATT - 2 * N_IDS
QT = TOP - H * TOK
KT = QT - H * TOK
CT = KT - 2 * TOK
KRT = CT - TOK
UP = KRT - G * (PAD + TOK)
VV = 0
ZL = VV + PT * 512
AT = 17984
YALL = 0
XN2 = YALL + NT * D
XN2T = XN2 + NT * D
MT = XN2T + KD * SEQ


def project(env):
    nc, I, ar, C = env["nc"], env["I"], env["ar"], env["C"]
    w = 0
    wfront = ar.at(w, P, KD, W_FRONT); w += KD * W_FRONT
    wqup = ar.at(w, P, 3, H * DH); w += 3 * H * DH
    wqsw = ar.at(w, P, 3, H * DR); w += 3 * H * DR
    wuk = ar.at(w, P, 2, H * DN); w += 2 * H * DN
    xt = ar.at(w, P, KD, NW); w += KD * NW
    sq = ar.at(w, P, 4, NW); w += 4 * NW
    qlat = ar.at(w, P, 3, NW); w += 3 * NW
    kv = ar.at(w, P, 2, NW); w += 2 * NW
    cos = ar.at(w, P, NW); w += NW
    sin = ar.at(w, P, NW); w += NW
    rr = ar.at(w, P, 2, NW); w += 2 * NW
    sqh = ar.at(w, P, 2, NW); w += 2 * NW
    kraw = ar.at(w, P, 2, NW); w += 2 * NW
    rot1 = ar.at(w, P, NW); w += NW
    rot2 = ar.at(w, P, NW); w += NW
    assert w <= UP
    qT, kT = ar.at(QT, P, H, TOK), ar.at(KT, P, H, TOK)
    cT, krT, uP = ar.at(CT, P, 2, TOK), ar.at(KRT, P, TOK), ar.at(UP, P, G, PAD + TOK)
    chunks = [(j * P, "q", j) for j in range(3)] + [(QL + j * P, "kv", j) for j in range(2)] \
        + [(QL + KL + j * P, "pool", j) for j in range(G)]
    KR0 = QL + KL + G * P
    NCH = len(chunks)
    units = [("q", h) for h in range(H)] + [("k", h) for h in range(H)]

    with ExitStack() as ctx:
        sem = env["early_sem"]
        ps = ctx.enter_context(nc.psum_tensor("ps_a", [P, 8, 512], F32))
        pj, ss, pa, pb = (ps[:, 2 * j:2 * j + 2, 0:NW] for j in range(4))
        loaded, x_in, xn_saved = sem("a_loaded"), sem("a_x_in"), sem("a_xn_saved")
        sq_done, sq_used = sem("a_sq_done"), sem("a_sq_used")
        std_done, tables_in = sem("a_std_done"), sem("a_tables_in")
        xn_done, chunk_done, chunk_out = sem("a_xn_done"), sem("a_chunk_done"), sem("a_chunk_out")
        kr_done, kr_out, lat_done = sem("a_kr_done"), sem("a_kr_out"), sem("a_lat_done")
        up_done, usq_done, uss_done, ustd_done, unit_out = (sem("a_" + n) for n in ("up", "usq", "uss", "ustd", "unit"))
        pads = sem("a_pads")
        block = ctx.enter_context(nc.Block())

        @block.sync
        def _(sp):
            sp.dma_start(env["const"][:, 0:CONST_COLS], I["consts"]).then_inc(loaded, 16)
            sp.dma_start(env["qk_norms"][:, :], I["qk_norms"]).then_inc(loaded, 16)
            sp.dma_start(wfront, I["w_front"]).then_inc(loaded, 16)
            sp.dma_start(wqup, I["w_q_up"]).then_inc(loaded, 16)
            sp.dma_start(wqsw, I["w_q_sw"]).then_inc(loaded, 16)
            sp.dma_start(wuk, I["w_uk"]).then_inc(loaded, 16)
            sp.wait_ge(loaded, 96)
            with sp.Fori(0, NN) as n:
                sp.wait_ge(xn_saved, n * 16)
                sp.wait_ge(kr_done, n)
                sp.dma_start(xt, I["xT"][:, :, ds(n * NW, NW)]).then_inc(x_in, 16)
                sp.wait_ge(unit_out, n * 16)
                sp.dma_start(cos[64:96, :], I["cos"][:, ds(n * NW, NW)]).then_inc(tables_in, 16)
                sp.dma_start(sin[64:96, :], I["sin"][:, ds(n * NW, NW)]).then_inc(tables_in, 16)
                sp.wait_ge(xn_done, n * KD + KD)
                sp.dma_start(env["xn_dram"][:, :, ds(n * NW, NW)], xt).then_inc(xn_saved, 16)
            sp.wait_ge(xn_saved, NN * 16)

        @block.gpsimd
        def _(pool):
            nc.gpsimd.memset(uP[:, :, 0:PAD], 0.0).then_inc(pads, 1)

        @block.scalar
        def _(act):
            act.wait_ge(loaded, 96)
            with act.Fori(0, NN) as n:
                act.wait_ge(x_in, n * 16 + 16)
                for half in range(2):
                    act.wait_ge(sq_used, n * 4 + half)
                    nc.scalar.activation(sq[:, :, :], xt[:, 4 * half:4 * half + 4, :], ACT.Square).then_inc(sq_done, 1)
                act.wait_ge(sq_used, n * 4 + 2)
                act.wait_ge(unit_out, n * 16)
                nc.scalar.activation(rr[:, 0, :], ss[:, 0, :], ACT.Sqrt, bias=C["eps"], scale=1.0 / D).then_inc(std_done, 1)
                for j, (_, what, at) in enumerate(chunks):
                    act.wait_ge(chunk_done, n * NCH + j + 1)
                    dst = {"q": lambda: qlat[:, at, :], "kv": lambda: kv[:, at, :],
                           "pool": lambda: uP[:, at, ds(PAD + n * NW, NW)]}[what]()
                    nc.scalar.activation(dst, pj[:, j % 2, :], ACT.Copy).then_inc(chunk_out, 1)
                    if j == 2:
                        nc.scalar.drain()
                        act.wait_ge(sq_used, n * 4 + 2)
                        nc.scalar.activation(sq[:, 0:3, :], qlat[:, :, :], ACT.Square).then_inc(sq_done, 1)
                    if j == 4:
                        nc.scalar.drain()
                        act.wait_ge(sq_used, n * 4 + 3)
                        nc.scalar.activation(rr[:, 1, :], ss[:, 1, :], ACT.Sqrt, bias=C["eps"], scale=1.0 / QL).then_inc(std_done, 1)
                        nc.scalar.activation(sq[:, 0:2, :], kv[:, :, :], ACT.Square).then_inc(sq_done, 1)
                act.wait_ge(sq_used, n * 4 + 4)
                act.wait_ge(xn_done, n * KD + KD)
                nc.scalar.activation(rr[:, 0, :], ss[:, 0, :], ACT.Sqrt, bias=C["eps"], scale=1.0 / KL).then_inc(std_done, 1)

                def unit_square(u):
                    kind, _ = units[u]
                    act.wait_ge(up_done, n * 16 + u + 1)
                    if kind == "q":
                        if u >= 2:
                            act.wait_ge(uss_done, n * 16 + u - 1)
                        nc.scalar.activation(sqh[0:DH, u % 2, :], pa[0:DH, u % 2, :], ACT.Square).then_inc(usq_done, 1)
                    else:
                        act.wait_ge(unit_out, n * 16 + u - 1)
                        nc.scalar.activation(kraw[0:DN, u % 2, :], pa[0:DN, u % 2, :], ACT.Copy)
                        nc.scalar.drain()
                        act.wait_ge(uss_done, n * 16 + u - 1)
                        nc.scalar.activation(sqh[0:DH, u % 2, :], kraw[0:DH, u % 2, :], ACT.Square).then_inc(usq_done, 1)

                def unit_std(u):
                    act.wait_ge(uss_done, n * 16 + u + 1)
                    if u < 2:
                        act.wait_ge(lat_done, n * 5 + 5)
                    else:
                        act.wait_ge(unit_out, n * 16 + u - 1)
                    nc.scalar.activation(rr[0:DH, u % 2, :], ss[0:DH, u % 2, :], ACT.Sqrt, bias=C["eps"][0:DH],
                                         scale=1.0 / DH).then_inc(ustd_done, 1)

                act.wait_ge(kr_out, n + 1)
                unit_square(0)
                for u in range(1, 16):
                    unit_square(u)
                    unit_std(u - 1)
                unit_std(15)

        @block.tensor
        def _(pe):
            pe.wait_ge(loaded, 96)
            ones = C["ones"]
            with pe.Fori(0, NN) as n:
                pe.wait_ge(ustd_done, n * 16)
                for half in range(2):
                    pe.wait_ge(sq_done, n * 4 + half + 1)
                    for k in range(4):
                        last = nc.tensor.matmul(ss[:, 0, :], ones, sq[:, k, :], start=half + k == 0, stop=half + k == 4)
                    last.then_inc(sq_used, 1)

                def chunk(j):
                    c0 = chunks[j][0]
                    pe.wait_ge(chunk_out, n * NCH + max(j - 1, 0))
                    if j == 0:
                        pe.wait_ge(kr_out, n)
                    for k in range(KD):
                        if j == 0:
                            pe.wait_ge(xn_done, n * KD + k + 1)
                        last = nc.tensor.matmul(pj[:, j % 2, :], wfront[:, k, c0:c0 + P], xt[:, k, :],
                                                start=k == 0, stop=k == KD - 1)
                    last.then_inc(chunk_done, 1)

                for j in range(4):
                    chunk(j)
                pe.wait_ge(sq_done, n * 4 + 3)
                for k in range(3):
                    last = nc.tensor.matmul(ss[:, 1, :], ones, sq[:, k, :], start=k == 0, stop=k == 2)
                last.then_inc(sq_used, 1)
                for j in range(4, 6):
                    chunk(j)
                pe.wait_ge(sq_done, n * 4 + 4)
                pe.wait_ge(std_done, n * 3 + 1)
                for k in range(2):
                    last = nc.tensor.matmul(ss[:, 0, :], ones, sq[:, k, :], start=k == 0, stop=k == 1)
                last.then_inc(sq_used, 1)
                for j in range(6, NCH):
                    chunk(j)
                pe.wait_ge(chunk_out, n * NCH + NCH)
                for s in range(2):
                    for k in range(KD):
                        last = nc.tensor.matmul(pj[64:96, s, :], wfront[:, k, KR0 + s * DR:KR0 + (s + 1) * DR], xt[:, k, :],
                                                start=k == 0, stop=k == KD - 1)
                last.then_inc(kr_done, 1)

                def up(u):
                    kind, h = units[u]
                    if u < 2:
                        pe.wait_ge(lat_done, n * 5 + 5)
                    wait_apart(pe, unit_out, n * 16 + max(u - 1, 0), (loaded, 96))
                    if kind == "q":
                        for k in range(3):
                            nc.tensor.matmul(pa[0:DH, u % 2, :], wqup[:, k, h * DH:(h + 1) * DH], qlat[:, k, :],
                                             start=k == 0, stop=k == 2)
                        for k in range(3):
                            last = nc.tensor.matmul(pb[64:96, u % 2, :], wqsw[:, k, h * DR:(h + 1) * DR], qlat[:, k, :],
                                                    start=k == 0, stop=k == 2)
                    else:
                        for k in range(2):
                            last = nc.tensor.matmul(pa[0:DN, u % 2, :], wuk[:, k, h * DN:(h + 1) * DN], cT[:, k, ds(n * NW, NW)],
                                                    start=k == 0, stop=k == 1)
                    last.then_inc(up_done, 1)

                def total(u):
                    pe.wait_ge(usq_done, n * 16 + u + 1)
                    if u < 2:
                        pe.wait_ge(std_done, n * 3 + 3)
                    else:
                        pe.wait_ge(ustd_done, n * 16 + u - 1)
                    nc.tensor.matmul(ss[0:DH, u % 2, :], ones[0:DH, 0:DH], sqh[0:DH, u % 2, :],
                                     start=True, stop=True).then_inc(uss_done, 1)

                up(0)
                for u in range(1, 16):
                    up(u)
                    total(u - 1)
                total(15)

        @block.vector
        def _(dve):
            dve.wait_ge(loaded, 96)
            mul, add = ALU.mult, ALU.add
            nc.vector.scalar_tensor_tensor(out=C["wqk"][0:DH], in0=env["qk_norms"][:, 0:1], scalar=DH ** -0.5,
                                           in1=env["qk_norms"][:, 1:2], op0=mul, op1=mul)
            nc.vector.drain()
            with dve.Fori(0, NN) as n:
                dve.wait_ge(std_done, n * 3 + 1)
                nc.vector.reciprocal(rr[:, 0, :], rr[:, 0, :])
                nc.vector.drain()
                for k in range(KD):
                    nc.vector.scalar_tensor_tensor(out=xt[:, k, :], in0=xt[:, k, :], scalar=C["w1"][:, k:k + 1],
                                                   in1=rr[:, 0, :], op0=mul, op1=mul).then_inc(xn_done, 1)
                dve.wait_ge(std_done, n * 3 + 2)
                nc.vector.reciprocal(rr[:, 1, :], rr[:, 1, :])
                nc.vector.drain()
                for k in range(3):
                    nc.vector.scalar_tensor_tensor(out=qlat[:, k, :], in0=qlat[:, k, :], scalar=C["wq_lat"][:, k:k + 1],
                                                   in1=rr[:, 1, :], op0=mul, op1=mul).then_inc(lat_done, 1)
                dve.wait_ge(std_done, n * 3 + 3)
                nc.vector.reciprocal(rr[:, 0, :], rr[:, 0, :])
                nc.vector.drain()
                for k in range(2):
                    nc.vector.scalar_tensor_tensor(out=cT[:, k, ds(n * NW, NW)], in0=kv[:, k, :], scalar=C["wkv"][:, k:k + 1],
                                                   in1=rr[:, 0, :], op0=mul, op1=mul).then_inc(lat_done, 1)
                dve.wait_ge(kr_done, n + 1)
                dve.wait_ge(tables_in, n * 32 + 32)
                dve.wait_ge(usq_done, n * 16)
                nc.vector.tensor_tensor(rot1[64:96, :], pj[64:96, 0, :], cos[64:96, :], mul)
                nc.vector.tensor_tensor(rot2[64:96, :], pj[64:96, 1, :], sin[64:96, :], mul)
                nc.vector.drain()
                nc.vector.tensor_tensor(kraw[64:96, 0, :], rot1[64:96, :], rot2[64:96, :], add)
                nc.vector.drain()
                nc.vector.tensor_copy(kraw[64:96, 1, :], kraw[64:96, 0, :])
                nc.vector.tensor_copy(krT[64:96, ds(n * NW, NW)], kraw[64:96, 0, :]).then_inc(kr_out, 1)
                for u, (kind, h) in enumerate(units):
                    dve.wait_ge(ustd_done, n * 16 + u + 1)
                    r = rr[:, u % 2, :]
                    nc.vector.reciprocal(r[0:DH], r[0:DH])
                    if kind == "q":
                        nc.vector.tensor_tensor(rot1[64:96, :], pa[64:96, u % 2, :], cos[64:96, :], mul)
                        nc.vector.tensor_tensor(rot2[64:96, :], pb[64:96, u % 2, :], sin[64:96, :], mul)
                        nc.vector.drain()
                        nc.vector.tensor_tensor(rot1[64:96, :], rot1[64:96, :], rot2[64:96, :], add)
                        nc.vector.scalar_tensor_tensor(out=qT[0:DN, h, ds(n * NW, NW)], in0=pa[0:DN, u % 2, :],
                                                       scalar=C["wqk"][0:DN], in1=r[0:DN], op0=mul, op1=mul)
                        nc.vector.drain()
                        nc.vector.scalar_tensor_tensor(out=qT[64:96, h, ds(n * NW, NW)], in0=rot1[64:96, :],
                                                       scalar=C["wqk"][64:96], in1=r[64:96], op0=mul, op1=mul).then_inc(unit_out, 1)
                    else:
                        nc.vector.drain()
                        nc.vector.tensor_tensor(kT[0:DH, h, ds(n * NW, NW)], kraw[0:DH, u % 2, :], r[0:DH], mul).then_inc(unit_out, 1)


def pool_and_values(env):
    nc, I, O, ar, C = (env[k] for k in ("nc", "I", "O", "ar", "C"))
    cT, krT, uP = ar.at(CT, P, 2, TOK), ar.at(KRT, P, TOK), ar.at(UP, P, G, PAD + TOK)
    vv, zl = ar.at(VV, P, PT, 512), ar.at(ZL, P, G, TOK)
    w = ZL + G * TOK
    z = ar.at(w, P, G, TOK); w += G * TOK
    part = [ar.at(w + s * (PAD + SEQ), P, PAD + SEQ) for s in range(2)]; w += 2 * (PAD + SEQ)
    wuv = ar.at(w, P, 2, 512); w += 1024
    wlin = ar.at(w, P, G, P); w += G * P
    us = ar.at(w, P, G, DB * (STATE + DQ)); w += G * DB * (STATE + DQ)
    uspart = [ar.at(w + s * DB * 23, P, DB, STATE + DQ) for s in range(2)]; w += 2 * DB * 23
    rows = ar.at(w, P, KL + DR); w += KL + DR
    assert w <= UP
    us4 = [us[:, g, :].rearrange("p (b t) -> p b t", b=DB) for g in range(G)]
    NZ = 3
    with ExitStack() as ctx:
        sem = env["early_sem"]
        ps = ctx.enter_context(nc.psum_tensor("ps_b", [P, 8, 512], F32))
        loaded, stored, v_done, v_out = sem("b_loaded"), sem("b_stored"), sem("b_v_done"), sem("b_v_out")
        us_ready, window, z_done, lin_done, zl_done = (sem("b_" + n) for n in ("us", "window", "z", "lin", "zl"))
        rows_done, rows_out, z_started = sem("b_rows_done"), sem("b_rows_out"), sem("b_z_started")
        block = ctx.enter_context(nc.Block())

        @block.sync
        def _(sp):
            sp.dma_start(wuv, I["w_uv"]).then_inc(loaded, 16)
            sp.dma_start(wlin, I["pool_lin"]).then_inc(loaded, 16)
            for g in range(G):
                sp.dma_start(us4[g][:, :, 0:STATE], I["stateT"][:, g, :, :]).then_inc(loaded, 16)
            sp.dma_start(O["ckvT"], cT).then_inc(stored, 16)
            sp.dma_start(O["kropeT"], krT[64:96, :]).then_inc(stored, 16)
            sp.dma_start(O["poolT"], uP[:, :, PAD + SEQ - STATE:PAD + SEQ]).then_inc(stored, 16)
            sp.wait_ge(us_ready, 1)
            for g in range(G):
                sp.dma_start(O["poolsT"][:, g, :, :], us4[g][:, :, DQ:DQ + STATE]).then_inc(stored, 16)
            sp.wait_ge(rows_out, 2)
            sp.dma_start(env["new_rows"], rows).then_inc(stored, 16)
            sp.wait_ge(stored, 8 * 16)

        @block.tensor
        def _(pe):
            pe.wait_ge(loaded, 96)
            for t in range(PT):
                if t >= 2:
                    pe.wait_ge(v_out, t - 1)
                for k in range(2):
                    last = nc.tensor.matmul(ps[:, t % 2, :], cT[:, k, t * P:(t + 1) * P], wuv[:, k, :], start=k == 0, stop=k == 1)
                last.then_inc(v_done, 1)
            for k in range(2):
                nc.tensor.transpose(ps[:, 2, k * P:(k + 1) * P], cT[:, k, SEQ:TOK], C["ident"])
            nc.tensor.transpose(ps[:, 3, 0:DR], krT[64:96, SEQ:TOK], C["ident"][64:96, 64:96]).then_inc(rows_done, 1)
            for g in range(G):
                pe.wait_ge(z_done, g + 1)
                for n in range(NZ):
                    i = g * NZ + n
                    if i >= 4:
                        pe.wait_ge(zl_done, i - 3)
                    nc.tensor.matmul(ps[:, 4 + i % 4, 0:NW], wlin[:, g, :], z[:, g, n * NW:(n + 1) * NW],
                                     start=True, stop=True).then_inc(lin_done, 1)

        @block.scalar
        def _(act):
            for t in range(PT):
                act.wait_ge(v_done, t + 1)
                nc.scalar.activation(vv[:, t, :], ps[:, t % 2, :], ACT.Copy).then_inc(v_out, 1)
            act.wait_ge(rows_done, 1)
            nc.scalar.activation(rows[:, 0:KL], ps[:, 2, 0:KL], ACT.Copy).then_inc(rows_out, 1)
            nc.scalar.activation(rows[:, KL:KL + DR], ps[:, 3, 0:DR], ACT.Copy).then_inc(rows_out, 1)
            for g in range(G):
                for n in range(NZ):
                    i = g * NZ + n
                    act.wait_ge(lin_done, i + 1)
                    nc.scalar.activation(zl[:, g, n * NW:(n + 1) * NW], ps[:, 4 + i % 4, 0:NW], ACT.Copy,
                                         scale=C["pool_scale"][:, g:g + 1]).then_inc(zl_done, 1)

        @block.gpsimd
        def _(pool):
            pool.wait_ge(loaded, 96)
            for g in range(G):
                last = nc.gpsimd.tensor_copy(us4[g][:, :, STATE:], uP[:, g, PAD + SEQ:PAD + SEQ + NS].rearrange("p (b q) -> p b q", b=DB))
            last.then_inc(us_ready, 1)
            pool.wait_ge(us_ready, 1)
            step = 0
            for g in range(G):
                src, ssrc = uP[:, g, 0:PAD + SEQ], us4[g]
                for lv in range(g + 1):
                    lo, sh = (2 << lv) - 1, 1 << lv
                    dst, sdst = part[(step) % 2], uspart[(step) % 2]
                    if lv == 0 and g:
                        pool.wait_ge(z_started, g)
                    nc.gpsimd.tensor_tensor(dst[:, lo:], src[:, lo:], src[:, lo - sh:PAD + SEQ - sh], ALU.add)
                    nc.gpsimd.tensor_tensor(sdst[:, :, lo:], ssrc[:, :, lo:], ssrc[:, :, lo - sh:STATE + DQ - sh], ALU.add).then_inc(window, 1)
                    step += 1
                    pool.wait_ge(window, step)
                    src, ssrc = dst, sdst

        @block.vector
        def _(dve):
            step = 0
            for g in range(G):
                step += g + 1
                dve.wait_ge(window, step)
                s, t = part[(step - 1) % 2], uspart[(step - 1) % 2]
                width = 2 << g
                nc.vector.scalar_tensor_tensor(out=z[:, g, PAD:SEQ], in0=s[:, 2 * PAD:], scalar=1.0 / width,
                                               in1=uP[:, g, 2 * PAD:PAD + SEQ], op0=ALU.mult, op1=ALU.subtract)
                nc.vector.tensor_tensor(z[:, g, 0:PAD], s[:, PAD:2 * PAD], C["invcnt"][:, g * PAD:(g + 1) * PAD], ALU.mult)
                nc.vector.drain()
                nc.vector.tensor_tensor(z[:, g, 0:PAD], z[:, g, 0:PAD], uP[:, g, PAD:2 * PAD], ALU.subtract)
                zs = z[:, g, SEQ:SEQ + NS].rearrange("p (b q) -> p b q", b=DB)
                nc.vector.scalar_tensor_tensor(out=zs, in0=t[:, :, STATE:], scalar=1.0 / width, in1=us4[g][:, :, STATE:],
                                               op0=ALU.mult, op1=ALU.subtract).then_inc(z_started, 1)
                nc.vector.drain()
                nc.vector.tensor_copy(z[:, g, SEQ + NS:TOK], z[:, g, SEQ:SEQ + NS]).then_inc(z_done, 1)


def prompt_attention(env):
    nc, ar, C = env["nc"], env["ar"], env["C"]
    qT, kT, vv = ar.at(QT, P, H, TOK), ar.at(KT, P, H, TOK), ar.at(VV, P, PT, 512)
    w = ZL + G * TOK
    attn = ar.at(w, P, PT, 512); w += PT * 512
    qh = ar.at(w, P, SEQ); w += SEQ
    pr = ar.at(w, P, 2, SEQ); w += 2 * SEQ
    prT = ar.at(w, P, 2, SEQ); w += 2 * SEQ
    negm = ar.at(w, P, 2); w += 2
    l = ar.at(w, P, 2); w += 2
    rl = ar.at(w, P, 1); w += 1
    assert w <= AT
    attnT = ar.at(AT, P, 4, TOK)
    with ExitStack() as ctx:
        sem = env["early_sem"]
        S = ctx.enter_context(nc.psum_tensor("ps_s", [P, 2, SEQ], F32))
        PTp = ctx.enter_context(nc.psum_tensor("ps_pt", [P, SEQ], F32))
        Op = ctx.enter_context(nc.psum_tensor("ps_o", [P, 512], F32))
        q_copied, s_done, max_done, exp_done, t_done, t_out, pv_done, o_out = (
            sem("c_" + n) for n in ("q_copied", "s", "max", "exp", "t", "t_out", "pv", "o_out"))
        at_done, at_out = sem("c_at_done"), sem("c_at_out")
        block = ctx.enter_context(nc.Block())

        @block.gpsimd
        def _(pool):
            with pool.Fori(0, H) as h:
                pool.wait_ge(s_done, h * PT)
                nc.gpsimd.tensor_copy(qh[0:DH, :], one(qT[0:DH, ds(h, 1), 0:SEQ])).then_inc(q_copied, 1)

        @block.tensor
        def _(pe):
            with pe.Fori(0, H) as h:
                def scores(i):
                    pe.wait_ge(q_copied, h + 1)
                    pe.wait_ge(exp_done, h * PT + max(i - 1, 0))
                    for c in range(0, (i + 1) * P, 512):
                        n = min(512, (i + 1) * P - c)
                        last = nc.tensor.matmul(S[:, i % 2, c:c + n], qh[0:DH, i * P:(i + 1) * P], one(kT[0:DH, ds(h, 1), c:c + n]),
                                                start=True, stop=True)
                    last.then_inc(s_done, 1)

                scores(0)
                for i in range(PT):
                    if i + 1 < PT:
                        scores(i + 1)
                    pe.wait_ge(exp_done, h * PT + i + 1)
                    pe.wait_ge(t_out, h * PT + i)
                    for j in range(i + 1):
                        last = nc.tensor.transpose(PTp[:, j * P:(j + 1) * P], pr[:, i % 2, j * P:(j + 1) * P], C["ident"])
                    last.then_inc(t_done, 1)
                    pe.wait_ge(t_out, h * PT + i + 1)
                    pe.wait_ge(o_out, h * PT + i)
                    for j in range(i + 1):
                        last = nc.tensor.matmul(Op[:, 0:DN], prT[:, i % 2, j * P:(j + 1) * P], vv[:, j, ds(h * DN, DN)],
                                                start=j == 0, stop=j == i)
                    last.then_inc(pv_done, 1)
            for i in range(PT):
                if i >= 2:
                    pe.wait_ge(at_out, i - 1)
                else:
                    pe.wait_ge(o_out, H * PT)
                for k in range(4):
                    last = nc.tensor.transpose(S[:, i % 2, k * P:(k + 1) * P], attn[:, i, k * P:(k + 1) * P], C["ident"])
                last.then_inc(at_done, 1)

        @block.scalar
        def _(act):
            with act.Fori(0, H) as h:
                def exps(i):
                    act.wait_ge(max_done, h * PT + i + 1)
                    if i >= 2:
                        act.wait_ge(t_done, h * PT + i - 1)
                        act.wait_ge(o_out, h * PT + i - 1)
                    else:
                        act.wait_ge(t_done, h * PT)
                        act.wait_ge(o_out, h * PT)
                    W = (i + 1) * P
                    nc.scalar.activation(pr[:, i % 2, 0:W], S[:, i % 2, 0:W], ACT.Exp, bias=negm[:, i % 2:i % 2 + 1],
                                         accum_out=l[:, i % 2:i % 2 + 1]).then_inc(exp_done, 1)

                exps(0)
                for i in range(PT):
                    if i + 1 < PT:
                        exps(i + 1)
                    act.wait_ge(t_done, h * PT + i + 1)
                    act.wait_ge(pv_done, h * PT + max(i - 1, 0))
                    nc.scalar.activation(prT[:, i % 2, 0:(i + 1) * P], PTp[:, 0:(i + 1) * P], ACT.Copy).then_inc(t_out, 1)
            for i in range(PT):
                act.wait_ge(at_done, i + 1)
                nc.scalar.activation(attnT[:, :, i * P:(i + 1) * P], S[:, i % 2, 0:512].rearrange("p (k t) -> p k t", k=4),
                                     ACT.Copy).then_inc(at_out, 1)

        @block.vector
        def _(dve):
            with dve.Fori(0, H) as h:
                def maxima(i):
                    dve.wait_ge(s_done, h * PT + i + 1)
                    W = (i + 1) * P
                    nc.vector.tensor_tensor(S[:, i % 2, W - P:W], S[:, i % 2, W - P:W], C["causal"], ALU.add)
                    nc.vector.drain()
                    nc.vector.tensor_reduce(out=negm[:, i % 2:i % 2 + 1], in_=S[:, i % 2, 0:W], axis=AX, op=ALU.max,
                                            negate=True).then_inc(max_done, 1)

                maxima(0)
                for i in range(PT):
                    if i + 1 < PT:
                        maxima(i + 1)
                    dve.wait_ge(pv_done, h * PT + i + 1)
                    nc.vector.reciprocal(rl, l[:, i % 2:i % 2 + 1])
                    nc.vector.drain()
                    nc.vector.tensor_scalar(attn[:, i, ds(h * DN, DN)], Op[:, 0:DN], rl, None, ALU.mult).then_inc(o_out, 1)


def sample_queries(env):
    nc, I, ar, C = env["nc"], env["I"], env["ar"], env["C"]
    qT, zl = ar.at(QT, P, H, TOK), ar.at(ZL, P, G, TOK)
    wukT = ar.at(KT, P, H, KL)
    qlat0, qrope0 = ar.at(KT + H * KL, P, 2, H * NS), ar.at(KT + H * KL + 2 * H * NS, P, H * NS)
    qlat, qrope, zls = ar.at(QLAT, P, 2 * H * NS), ar.at(QROPE, P, H * NS), ar.at(ZLS, P, G, P)

    def by_batch(ap, h):
        return ap.rearrange("p (b h q) -> p h b q", b=DB, h=H)[:, h, :, :]

    with ExitStack() as ctx:
        sem = lambda n: ctx.enter_context(nc.semaphore(n))
        ps = ctx.enter_context(nc.psum_tensor("ps_q", [P, 2, 512], F32))
        loaded, ql_done, ql_out, qr_done, shifted = (sem("q_" + n) for n in ("loaded", "ql", "ql_out", "qr", "shifted"))
        block = ctx.enter_context(nc.Block())

        @block.sync
        def _(sp):
            sp.dma_start(wukT[0:DN], I["w_ukT"]).then_inc(loaded, 16)
            sp.wait_ge(qr_done, 1)
            sp.wait_ge(ql_done, 1)
            sp.dma_start(qrope[0:DR, :], qrope0[64:96, :]).then_inc(shifted, 16)
            sp.wait_ge(shifted, 16)

        @block.tensor
        def _(pe):
            pe.wait_ge(loaded, 16)
            for h in range(H):
                for k in range(2):
                    last = nc.tensor.matmul(ps[:, k, h * NS:(h + 1) * NS], wukT[0:DN, h, k * P:(k + 1) * P], qT[0:DN, h, SEQ:SEQ + NS],
                                            start=True, stop=True)
            last.then_inc(ql_done, 1)

        @block.vector
        def _(dve):
            for h in range(H):
                last = nc.vector.tensor_copy(by_batch(qrope0, h)[64:96], qT[64:96, h, SEQ:SEQ + NS].rearrange("p (b q) -> p b q", b=DB))
            last.then_inc(qr_done, 1)

        @block.scalar
        def _(act):
            act.wait_ge(ql_done, 1)
            for k in range(2):
                for h in range(H):
                    last = nc.scalar.activation(by_batch(qlat0[:, k, :], h),
                                                ps[:, k, h * NS:(h + 1) * NS].rearrange("p (b q) -> p b q", b=DB), ACT.Copy)
            act.wait_ge(qr_done, 1)
            nc.scalar.drain()
            nc.scalar.activation(qlat, qlat0.rearrange("p a b -> p (a b)"), ACT.Copy)
            nc.scalar.activation(zls, zl[:, :, SEQ:TOK], ACT.Copy)


class Part:

    def __init__(self, env, tag, first, tiles, width, attnT, zl, x_free):
        ar = env["ar"]
        self.tag, self.first, self.tiles, self.width, self.x_free = tag, first, tiles, width, x_free
        self.cols = tiles * P
        self.steps = self.cols // width
        self.attnT, self.zl = attnT, zl
        self.mixed, self.xn2T = ar.at(MT, P, KD, self.cols), ar.at(XN2T, P, KD, self.cols)


def merge(env, part):
    nc, I, ar = env["nc"], env["I"], env["ar"]
    zl, attnT, mixed = part.zl, part.attnT, part.mixed
    W, N = part.width, part.steps
    w = ZL + G * TOK
    ring = [ar.at(w + s * 24 * P, P, 24, P) for s in range(2)]; w += 48 * P
    sig = ar.at(w, P, 4, W); w += 4 * W
    assert w <= AT
    xnT = ar.at(MT + KD * SEQ, P, KD, part.cols)
    prod = ar.at(MT - 4 * W, P, 4, W)
    assert MT + 2 * KD * SEQ <= LATE and MT - 4 * W >= AT + 4 * TOK
    with ExitStack() as ctx:
        sem = lambda n: ctx.enter_context(nc.semaphore("e_" + n + part.tag))
        ps = ctx.enter_context(nc.psum_tensor("ps_e" + part.tag, [P, 8, 512], F32))
        xn_in, w_in = sem("xn_in"), [sem(f"w_in{s}") for s in range(2)]
        gate_done, branch_done, sig_done, mix_done = (sem(n) for n in ("gate", "branch", "sig", "mix"))
        block = ctx.enter_context(nc.Block())

        @block.sync
        def _(sp):
            sp.dma_start(xnT, env["xn_dram"][:, :, part.first * P:part.first * P + part.cols]).then_inc(xn_in, 16)
            for s in range(2):
                sp.dma_start(ring[s], I["w_merge"][s]).then_inc(w_in[s], 16)
            with sp.Fori(0, KD // 2 - 1) as dd:
                for s in range(2):
                    sp.wait_ge(branch_done, dd * 2 * N + N * (s + 1))
                    sp.dma_start(ring[s], I["w_merge"][ds(dd * 2 + 2 + s, 1)].rearrange("a p k c -> (a p) k c")).then_inc(w_in[s], 16)

        @block.tensor
        def _(pe):
            pe.wait_ge(xn_in, 16)
            with pe.Fori(0, KD // 2) as dd:
                for s in range(2):
                    pe.wait_ge(w_in[s], dd * 16 + 16)
                    for n in range(N):
                        i = s * N + n
                        c = slice(n * W, (n + 1) * W)
                        B = 4 * (i % 2)
                        pe.wait_ge(mix_done, dd * 2 * N + i + 1)
                        for a in range(2):
                            for k in range(KD):
                                last = nc.tensor.matmul(ps[:, B + a, 0:W], ring[s][:, a * KD + k, :], xnT[:, k, c], start=k == 0, stop=k == KD - 1)
                        last.then_inc(gate_done, 1)
                        for a, src in enumerate((attnT, zl)):
                            for k in range(4):
                                last = nc.tensor.matmul(ps[:, B + 2 + a, 0:W], ring[s][:, 16 + 4 * a + k, :], src[:, k, c], start=k == 0, stop=k == 3)
                        last.then_inc(branch_done, 1)

        @block.scalar
        def _(act):
            with act.Fori(0, KD // 2) as dd:
                for i in range(2 * N):
                    act.wait_ge(gate_done, dd * 2 * N + i + 1)
                    act.wait_ge(mix_done, dd * 2 * N + i + 1)
                    nc.scalar.activation(sig[:, 2 * (i % 2):2 * (i % 2) + 2, :], ps[:, 4 * (i % 2):4 * (i % 2) + 2, 0:W],
                                         ACT.Sigmoid).then_inc(sig_done, 1)

        @block.vector
        def _(dve):
            nc.vector.drain().then_inc(mix_done, 2)
            with dve.Fori(0, KD // 2) as dd:
                for i in range(2 * N):
                    s, n, h = i // N, i % N, 2 * (i % 2)
                    dve.wait_ge(sig_done, dd * 2 * N + i + 1)
                    dve.wait_ge(branch_done, dd * 2 * N + i + 1)
                    nc.vector.tensor_tensor(prod[:, h:h + 2, :], sig[:, h:h + 2, :], ps[:, 2 * h + 2:2 * h + 4, 0:W], ALU.mult)
                    nc.vector.drain()
                    nc.vector.tensor_tensor(one(mixed[:, ds(dd * 2 + s, 1), n * W:(n + 1) * W]), prod[:, h, :], prod[:, h + 1, :],
                                            ALU.add).then_inc(mix_done, 1)


def residual(env, part):
    nc, I, ar, C = env["nc"], env["I"], env["ar"], env["C"]
    mixed, xn2T = part.mixed, part.xn2T
    yall, xn2 = ar.at(YALL, P, NT, D), ar.at(XN2, P, NT, D)
    T, T0 = part.tiles, part.first
    w = MT + KD * SEQ
    wout = ar.at(w, P, KD, D); w += KD * D
    mt = [ar.at(w + s * D, P, KD, P) for s in range(2)]; w += 2 * D
    xt = [ar.at(a, P, D) for a in part.x_free]
    w2 = ar.at(w, P, D); w += D
    xn = ar.at(w, P, D); w += D
    st = ar.at(w, P, 2); w += 2
    assert w <= LATT, (w, LATT)
    with ExitStack() as ctx:
        sem = lambda n: ctx.enter_context(nc.semaphore("f_" + n + part.tag))
        ps = ctx.enter_context(nc.psum_tensor("ps_f" + part.tag, [P, 8, 512], F32))
        loaded, x_in = sem("loaded"), [sem(f"x_in{s}") for s in range(2)]
        m_copied, h_done, h_out, std_done, xn_done, t_done, t_out = (
            sem(n) for n in ("m_copied", "h", "h_out", "std", "xn", "t", "t_out"))
        block = ctx.enter_context(nc.Block())

        def ahead(eng, get):
            for s in range(min(2, T)):
                get(s, s, 0)
            if T > 2:
                with eng.Fori(0, T // 2 - 1) as tt:
                    for s in range(2):
                        get(tt * 2 + 2 + s, s, tt + 1)

        def each(eng, body):
            if T == 1:
                return body(0, 0, 0)
            with eng.Fori(0, T // 2) as tt:
                for s in range(2):
                    body(tt * 2 + s, s, tt)

        @block.sync
        def _(sp):
            sp.dma_start(wout, I["w_out"]).then_inc(loaded, 16)
            sp.dma_start(w2, I["norm2"]).then_inc(loaded, 16)

            def get(t, s, i):
                if not isinstance(t, int):
                    sp.wait_ge(h_out, t - 1)
                sp.dma_start(xt[s], I["x_tok"][ds(t + T0, 1)].rearrange("a p c -> (a p) c")).then_inc(x_in[s], 16)

            ahead(sp, get)

        @block.gpsimd
        def _(pool):
            def get(t, s, i):
                if not isinstance(t, int):
                    pool.wait_ge(h_done, t - 1)
                nc.gpsimd.tensor_copy(mt[s], mixed[:, :, ds(t * P, P)]).then_inc(m_copied, 1)

            ahead(pool, get)

        @block.tensor
        def _(pe):
            def product(t, s):
                pe.wait_ge(m_copied, t + 1)
                if not isinstance(t, int) or t >= 2:
                    pe.wait_ge(h_out, t - 1)
                for c in range(2):
                    for k in range(KD):
                        last = nc.tensor.matmul(ps[:, 2 * s + c, :], mt[s][:, k, :], wout[:, k, c * 512:(c + 1) * 512], start=k == 0, stop=k == KD - 1)
                last.then_inc(h_done, 1)

            def transposed(t):
                pe.wait_ge(xn_done, t + 1)
                pe.wait_ge(t_out, t)
                for k in range(KD):
                    last = nc.tensor.transpose(ps[:, 4 + k // 4, (k % 4) * P:(k % 4 + 1) * P], xn[:, k * P:(k + 1) * P], C["ident"])
                last.then_inc(t_done, 1)

            pe.wait_ge(loaded, 32)
            product(0, 0)
            if T > 1:
                with pe.Fori(0, T // 2 - 1) as tt:
                    product(tt * 2 + 1, 1)
                    transposed(tt * 2)
                    product(tt * 2 + 2, 0)
                    transposed(tt * 2 + 1)
                product(T - 1, 1)
                transposed(T - 2)
            transposed(T - 1)

        @block.scalar
        def _(act):
            def body(t, s, i):
                act.wait_ge(h_out, t + 1)
                act.wait_ge(t_done, t)
                nc.scalar.activation(xn, one(yall[:, ds(t + T0, 1), :]), ACT.Square, accum_out=st[:, 0:1])
                nc.scalar.drain()
                nc.scalar.activation(st[:, 1:2], st[:, 0:1], ACT.Sqrt, bias=C["eps"], scale=1.0 / D).then_inc(std_done, 1)
                act.wait_ge(xn_done, t + 1)
                nc.scalar.activation(one(xn2[:, ds(t + T0, 1), :]), xn, ACT.Copy)
                act.wait_ge(t_done, t + 1)
                nc.scalar.activation(xn2T[:, :, ds(t * P, P)], ps[:, 4:6, :].rearrange("p a (b c) -> p (a b) c", b=4), ACT.Copy).then_inc(t_out, 1)
                nc.scalar.drain()

            each(act, body)

        @block.vector
        def _(dve):
            def body(t, s, i):
                y = one(yall[:, ds(t + T0, 1), :])
                dve.wait_ge(h_done, t + 1)
                dve.wait_ge(x_in[s], i * 16 + 16)
                nc.vector.tensor_tensor(y, ps[:, 2 * s:2 * s + 2, :].rearrange("p a b -> p (a b)"), xt[s], ALU.add).then_inc(h_out, 1)
                dve.wait_ge(std_done, t + 1)
                nc.vector.reciprocal(st[:, 1:2], st[:, 1:2])
                nc.vector.drain()
                nc.vector.scalar_tensor_tensor(out=xn, in0=y, scalar=st[:, 1:2], in1=w2, op0=ALU.mult, op1=ALU.mult).then_inc(xn_done, 1)

            each(dve, body)
            if T0:
                nc.vector.drain()
                nc.vector.memset(yall[NS:P, NT - 1, :], 0.0)


def peer_scores(env, part):
    nc, I, ar = env["nc"], env["I"], env["ar"]
    xn2T = part.xn2T
    W, N, T = part.width, part.steps, part.tiles
    TW = W // P
    w = XN2T + KD * SEQ
    ring = [ar.at(w + s * 9 * P, P, 9, P) for s in range(2)]; w += 18 * P
    qb = [ar.at(w + s * part.cols, P, part.cols) for s in range(2)]; w += 2 * part.cols
    out = ar.at(w, P, T, 2, NK); w += T * 2 * NK
    assert w <= LATE
    by_head = env["s_dram"][:, part.first * H:(part.first + T) * H, :].rearrange("p (t h) c -> p t h c", t=T)
    with ExitStack() as ctx:
        sem = lambda n: ctx.enter_context(nc.semaphore("g_" + n + part.tag))
        pq = ctx.enter_context(nc.psum_tensor("ps_g" + part.tag, [P, 4, 512], F32))
        pk = ctx.enter_context(nc.psum_tensor("ps_g2" + part.tag, [P, 4, 512], F32))
        w_in = [sem(f"w_in{s}") for s in range(2)]
        q_done, q_out, k_done, k_out, stored = (sem(n) for n in ("q", "q_out", "k", "k_out", "stored"))
        block = ctx.enter_context(nc.Block())

        @block.sync
        def _(sp):
            def store(h):
                sp.wait_ge(k_out, h * 2 * N + 2 * N)
                if T == 1:
                    dst, src = by_head[:, 0, ds(h, 1), :].rearrange("p a c -> p (a c)"), out.rearrange("p t s k -> p (t s k)")
                else:
                    dst, src = by_head[:, :, ds(h, 1), :].rearrange("p t a c -> p t (a c)"), out.rearrange("p t s k -> p t (s k)")
                sp.dma_start(dst, src).then_inc(stored, 16)

            for s in range(2):
                sp.dma_start(ring[s], I["w_peer"][s]).then_inc(w_in[s], 16)
            with sp.Fori(0, H - 1) as h:
                for s in range(2):
                    sp.wait_ge(k_done, h * 2 * N + N * (s + 1))
                    sp.dma_start(ring[s], I["w_peer"][ds(h * 2 + 2 + s, 1)].rearrange("a p k c -> (a p) k c")).then_inc(w_in[s], 16)
                store(h)
            store(H - 1)
            sp.wait_ge(stored, H * 16)

        @block.tensor
        def _(pe):
            with pe.Fori(0, H) as h:
                for s in range(2):
                    pe.wait_ge(w_in[s], h * 16 + 16)
                    for n in range(N):
                        for k in range(KD):
                            last = nc.tensor.matmul(pq[:, s * N + n, 0:W], ring[s][:, k, :], xn2T[:, k, n * W:(n + 1) * W], start=k == 0, stop=k == KD - 1)
                        last.then_inc(q_done, 1)
                    for n in range(N):
                        pe.wait_ge(q_out, h * 2 * N + s * N + n + 1)
                        pe.wait_ge(k_out, h * 2 * N)
                        for t in range(TW):
                            last = nc.tensor.matmul(pk[:, s * N + n, t * P:(t + 1) * P], qb[s][:, (TW * n + t) * P:(TW * n + t + 1) * P], ring[s][:, 8, :],
                                                    start=True, stop=True)
                        last.then_inc(k_done, 1)

        @block.scalar
        def _(act):
            with act.Fori(0, H) as h:
                for i in range(2 * N):
                    act.wait_ge(q_done, h * 2 * N + i + 1)
                    act.wait_ge(k_done, h * 2 * N)
                    nc.scalar.activation(qb[i // N][:, (i % N) * W:(i % N + 1) * W], pq[:, i, 0:W], ACT.Copy).then_inc(q_out, 1)

        @block.vector
        def _(dve):
            with dve.Fori(0, H) as h:
                for i in range(2 * N):
                    s, n = i // N, i % N
                    dve.wait_ge(k_done, h * 2 * N + i + 1)
                    dve.wait_ge(stored, h * 16)
                    nc.vector.tensor_copy(out[:, n * TW:(n + 1) * TW, s, :], pk[:, i, 0:W].rearrange("p (t k) -> p t k", t=TW)).then_inc(k_out, 1)


def sample_output(env):
    nc, I, ar = env["nc"], env["I"], env["ar"]
    latT, attnT = ar.at(LATT, P, 2, H * NS), ar.at(ATS, P, 4, P)
    wuv = ar.at(0, P, 2, 512)
    with ExitStack() as ctx:
        sem = lambda n: ctx.enter_context(nc.semaphore("o_" + n))
        ps = ctx.enter_context(nc.psum_tensor("ps_uv", [P, 4, 512], F32))
        loaded, done = sem("loaded"), sem("done")
        block = ctx.enter_context(nc.Block())

        @block.sync
        def _(sp):
            sp.dma_start(wuv, I["w_uv"]).then_inc(loaded, 16)

        @block.tensor
        def _(pe):
            pe.wait_ge(loaded, 16)
            for h in range(H):
                o = (h % 2) * DN
                for k in range(2):
                    last = nc.tensor.matmul(ps[o:o + DN, h // 2, 0:NS], wuv[:, k, h * DN:(h + 1) * DN], latT[:, k, h * NS:(h + 1) * NS],
                                            start=k == 0, stop=k == 1)
            last.then_inc(done, 1)

        @block.scalar
        def _(act):
            act.wait_ge(done, 1)
            for r in range(2):
                nc.scalar.activation(attnT[:, :, r * NS:(r + 1) * NS], ps[:, :, 0:NS], ACT.Copy)


class Route:

    def __init__(self, env, w, sem, by_halves):
        self.by_halves, self.unit = by_halves, 32 if by_halves else 16
        self.nc, self.C, self.ids, self.gates, ar = env["nc"], env["C"], env["ids"], env["gates"], env["ar"]

        def take(*dims):
            nonlocal w
            n = 1
            for d in dims:
                n *= d
            w += n
            return ar.at(w - n, P, *dims)

        self.s, self.s2 = take(2, NK), take(2, NK)
        self.top, self.topi, self.topf = take(2, TOPK), take(2, TOPK).bitcast(U32), take(2, TOPK)
        self.cand, self.best, self.pos = take(TOPK, TOPK), take(TOPK), take(TOPK).bitcast(U32)
        self.hilo, self.hilof, self.hit = take(2, TOPK).bitcast(U32), take(2, TOPK), take(2 * TOPK, TOPK)
        self.e2, self.ef, self.ex = take(2, TOPK), take(TOPK), take(TOPK)
        self.negb, self.sm = take(1), take(1)
        self.end = w
        self.s_in, self.s_used, self.b_done, self.e_done, self.done = (sem("h_" + n) for n in ("s_in", "s_used", "best", "exp", "done"))

    def load(self, sp, c, r, src):
        sp.wait_ge(self.s_used, c)
        if self.by_halves:
            for rows, head in ((slice(0, NS), r), (slice(NS, P), r + H // 2)):
                sp.dma_start(self.s[rows].rearrange("p a b -> p (a b)"), one(src[rows, ds(head, 1), :])).then_inc(self.s_in, 16)
        else:
            sp.dma_start(self.s.rearrange("p a b -> p (a b)"), one(src[:, ds(r, 1), :])).then_inc(self.s_in, 16)

    def softmax(self, act, c):
        act.wait_ge(self.b_done, c + 1)
        act.wait_ge(self.done, c)
        self.nc.scalar.activation(self.ex, self.best, ACT.Exp, bias=self.negb, accum_out=self.sm).then_inc(self.e_done, 1)

    def top_eight(self, dve, c):
        v = self.nc.vector
        wait_apart(dve, self.s_in, c * self.unit + self.unit, (self.s_in, self.unit))
        for p in range(2):
            v.max(out=self.top[:, p, 0:8], in_=self.s[:, p, :])
        v.drain()
        for p in range(2):
            v.max_index(out=self.topi[:, p, 0:8], in_max=self.top[:, p, 0:8], in_values=self.s[:, p, :])
            v.match_replace(out=self.s2[:, p, :], in_to_replace=self.top[:, p, 0:8], in_values=self.s[:, p, :], imm_value=LOWEST)
        v.drain().then_inc(self.s_used, 1)

    def top_sixteen(self):
        v = self.nc.vector
        for p in range(2):
            v.max(out=self.top[:, p, 8:16], in_=self.s2[:, p, :])
        v.drain()
        for p in range(2):
            v.max_index(out=self.topi[:, p, 8:16], in_max=self.top[:, p, 8:16], in_values=self.s2[:, p, :])
        v.tensor_tensor(self.cand, self.top[:, 0, :].unsqueeze(2).to_broadcast([P, TOPK, TOPK]),
                        self.top[:, 1, :].unsqueeze(1).to_broadcast([P, TOPK, TOPK]), ALU.add)
        v.drain()

    def pairs(self):
        v = self.nc.vector
        candf, cand2 = self.cand.rearrange("p a b -> p (a b)"), self.s2.rearrange("p a b -> p (a b)")
        v.tensor_copy(self.topf, self.topi)
        v.max(out=self.best[:, 0:8], in_=candf)
        v.drain()
        v.tensor_scalar(self.topf[:, 0, :], self.topf[:, 0, :], float(NK), None, ALU.mult)
        v.max_index(out=self.pos[:, 0:8], in_max=self.best[:, 0:8], in_values=candf)
        v.match_replace(out=cand2, in_to_replace=self.best[:, 0:8], in_values=candf, imm_value=LOWEST)
        v.tensor_scalar(self.negb, self.best[:, 0:1], -1.0, None, ALU.mult)
        v.drain()
        v.max(out=self.best[:, 8:16], in_=cand2)
        v.drain().then_inc(self.b_done, 1)
        v.max_index(out=self.pos[:, 8:16], in_max=self.best[:, 8:16], in_values=cand2)
        v.drain()

    def experts(self, dve, c, r):
        v = self.nc.vector
        v.tensor_scalar(self.hilo[:, 0, :], self.pos, 4, None, ALU.logical_shift_right)
        v.tensor_scalar(self.hilo[:, 1, :], self.pos, TOPK - 1, None, ALU.bitwise_and)
        v.drain()
        v.tensor_copy(self.hilof, self.hilo)
        v.drain()
        v.tensor_tensor(self.hit, self.hilof.rearrange("p a b -> p (a b)").unsqueeze(2).to_broadcast([P, 2 * TOPK, TOPK]),
                        self.C["iota16"].unsqueeze(1).to_broadcast([P, 2 * TOPK, TOPK]), ALU.is_equal)
        v.drain()
        h4 = self.hit.rearrange("p (a b) c -> p a b c", a=2)
        v.tensor_tensor(h4, h4, self.topf.unsqueeze(2).to_broadcast([P, 2, TOPK, TOPK]), ALU.mult)
        v.drain()
        v.tensor_reduce(out=self.e2, in_=h4, axis=AX, op=ALU.add)
        v.drain()
        v.tensor_tensor(self.ef, self.e2[:, 0, :], self.e2[:, 1, :], ALU.add)
        v.drain()
        v.tensor_copy(self.ids[:, ds(r * TOPK, TOPK)], self.ef)
        dve.wait_ge(self.e_done, c + 1)
        v.reciprocal(self.sm, self.sm)
        v.drain()
        v.tensor_scalar(self.gates[:, ds(r * TOPK, TOPK)], self.ex, self.sm, None, ALU.mult)
        v.drain().then_inc(self.done, 1)


class Pages:

    PPB = NPAGES + 1
    GB = GROUPS + 1

    def __init__(self, env, w, sem, ps):
        self.nc, self.I, self.C, self.env, ar = env["nc"], env["I"], env["C"], env, env["ar"]

        def take(parts, *dims):
            nonlocal w
            n = 1
            for d in dims:
                n *= d
            w += n
            return ar.at(w - n, parts, *dims)

        self.pages, self.new_page, self.wuk = take(P, GP, PGW), take(P, PGW), take(P, 2, 512)
        self.cTp, self.sqp = take(P, 2, KL + P), take(P, 2, 512)
        self.krsq, self.sskr, self.ssn, self.rk = take(P, GP, DR), take(P, GP), take(P, GP, H), take(P, GP, H)
        self.sc, self.pmax = take(P, GP, NS), take(P, NS)
        self.prob = self.sc
        small = take(NS, 8)
        self.m, self.mnew, self.negm, self.corr, self.gmax, self.rl = (small[:, j:j + 1] for j in range(6))
        self.diag, self.acc, self.lat = take(NS, NS), take(NS, KL + 1), take(NS, KL)
        self.end = w
        self.qlat, self.qrope = ar.at(QLAT, P, 2, H * NS), ar.at(QROPE, P, H * NS)
        self.latT = ar.at(LATT, P, 2, H * NS)
        self.tp, self.key, self.small_ps, self.acc_ps = ps[:, 0:2, :], ps[:, 2:4, :], ps[:, 4, :], ps[:, 5, :]
        self.loaded, self.new_in, self.zeroed = sem("d_loaded"), sem("d_new_in"), sem("d_zeroed")
        self.page_in = [sem(f"d_page_in{j}") for j in range(GP)]
        (self.t_done, self.t_out, self.key_done, self.s_done, self.ksq_done, self.ks_done, self.kr_sq, self.norm_in, self.norm_root,
         self.scaled, self.pm_done, self.pmT_done, self.m_done, self.corr_done, self.mb_done, self.shift_done, self.exp_done,
         self.pv_done, self.acc_out, self.lat_done, self.latT_done, self.latT_out) = (sem("d_" + n) for n in (
             "t_done", "t_out", "key", "s", "ksq", "ks", "kr_sq", "norm_in", "norm_root", "scaled", "pm", "pmT", "m", "corr",
             "mb", "sub", "exp", "pv", "acc_out", "lat", "latT", "latT_out"))

    def load_first(self, sp):
        sp.dma_start(self.env["table"][:, :], self.I["page_table"]).then_inc(self.loaded, 16)
        sp.dma_start(self.wuk, self.I["w_uk"]).then_inc(self.loaded, 16)
        sp.wait_ge(self.loaded, 32)
        sp.wait_ge(self.zeroed, 1)

    def load_new(self, sp, b):
        sp.wait_ge(self.pv_done, b * self.GB)
        rows = self.env["new_rows"]
        sp.dma_start(self.new_page[0:DQ, 0:KL], rows[ds(b * DQ, DQ), 0:KL]).then_inc(self.new_in, 16)
        sp.dma_start(self.new_page[0:DQ, KL + 1:PGW], rows[ds(b * DQ, DQ), KL:KL + DR]).then_inc(self.new_in, 16)

    def load_group(self, sp, b, g):
        sp.wait_ge(self.pv_done, b * self.GB + g)
        for j in range(GP):
            page = sp.value_load(self.env["table"][0:1, ds(b * NPAGES + g * GP + j, 1)], min_val=0, max_val=NPHYS - 1)
            for cols, src in ((slice(0, KL), "cache_ckv"), (slice(KL + 1, PGW), "cache_krope")):
                sp.dma_start(self.pages[:, j, cols], self.I[src][ds(page, 1)].rearrange("a p c -> (a p) c")).then_inc(self.page_in[j], 16)

    def clear(self):
        g = self.nc.gpsimd
        g.memset(self.new_page, 0.0)
        g.drain()
        g.memset(self.new_page[:, KL:KL + 1], 1.0)
        for j in range(GP):
            g.memset(self.pages[:, j, KL:KL + 1], 1.0)
        g.drain().then_inc(self.zeroed, 1)

    def transposes(self, pe, src, j, at):
        t = self.nc.tensor
        pe.wait_ge(self.t_out, at + (j if j < 2 else j - 1))
        for k in range(2):
            t.transpose(self.tp[:, j % 2, k * P:(k + 1) * P], src[:, k * P:(k + 1) * P], self.C["ident"])
        t.transpose(self.tp[0:DR, j % 2, KL:KL + P], src[:, KL + 1:PGW], self.C["ident"]).then_inc(self.t_done, 1)

    def keys(self, pe, j, at, gi, b):
        t = self.nc.tensor
        pe.wait_ge(self.t_out, at + j + 1)
        pe.wait_ge(self.ksq_done, at + (j if j < 2 else j - 1))
        for k in range(2):
            last = t.matmul(self.key[:, j % 2, :], self.cTp[:, j % 2, k * P:(k + 1) * P], self.wuk[:, k, :], start=k == 0, stop=k == 1)
        last.then_inc(self.key_done, 1)
        if j == 0:
            pe.wait_ge(self.scaled, gi)
            pe.wait_ge(self.shift_done, gi)
        out = self.small_ps[:, j * NS:(j + 1) * NS]
        for k in range(2):
            t.matmul(out, self.cTp[:, j % 2, k * P:(k + 1) * P], self.qlat[:, k, ds(b * NS, NS)], start=k == 0, stop=False)
        t.matmul(out, self.cTp[0:DR, j % 2, KL:KL + P], self.qrope[0:DR, ds(b * NS, NS)], start=False, stop=True).then_inc(self.s_done, 1)

    def maxima(self, pe, gi):
        wait_apart(pe, self.pm_done, gi + 1, (self.loaded, 32))
        self.nc.tensor.transpose(self.small_ps[0:NS, 256:256 + P], self.pmax, self.C["ident"]).then_inc(self.pmT_done, 1)

    def spread_maxima(self, pe, gi):
        pe.wait_ge(self.m_done, gi + 1)
        self.nc.tensor.matmul(self.small_ps[:, 384:384 + NS], self.C["ones"][0:NS, :], self.diag, start=True, stop=True).then_inc(self.mb_done, 1)

    def weigh(self, pe, srcs, gi):
        pe.wait_ge(self.exp_done, gi + 1)
        pe.wait_ge(self.acc_out, gi)
        for j, src in enumerate(srcs):
            last = self.nc.tensor.matmul(self.acc_ps[0:NS, 0:KL + 1], self.prob[:, j, :], src[:, 0:KL + 1], start=j == 0, stop=j == len(srcs) - 1)
        last.then_inc(self.pv_done, 1)

    def group_arrived(self, pe, b, g):
        for j in range(GP):
            pe.wait_ge(self.page_in[j], (b * GROUPS + g) * 32 + 32)

    def finish_pe(self, pe, b):
        at, gi = b * self.PPB + NPAGES, b * self.GB + GROUPS
        pe.wait_ge(self.new_in, b * 32 + 32)
        self.transposes(pe, self.new_page, 0, at)
        self.keys(pe, 0, at, gi, b)
        self.maxima(pe, gi)
        self.spread_maxima(pe, gi)
        self.weigh(pe, [self.new_page], gi)
        wait_apart(pe, self.lat_done, b + 1, (self.loaded, 32))
        for k in range(2):
            last = self.nc.tensor.transpose(self.acc_ps[:, 320 + k * NS:320 + (k + 1) * NS], self.lat[:, k * P:(k + 1) * P], self.C["ident"][0:NS, 0:NS])
        last.then_inc(self.latT_done, 1)

    def copy_page(self, act, j, at):
        s = self.nc.scalar
        act.wait_ge(self.t_done, at + j + 1)
        act.wait_ge(self.s_done, at + (j if j < 2 else j - 1))
        s.activation(self.cTp[:, j % 2, 0:KL], self.tp[:, j % 2, 0:KL], ACT.Copy)
        s.activation(self.cTp[0:DR, j % 2, KL:], self.tp[0:DR, j % 2, KL:KL + P], ACT.Copy)
        s.drain().then_inc(self.t_out, 1)

    def square(self, act, j, at):
        act.wait_ge(self.key_done, at + j + 1)
        act.wait_ge(self.ks_done, at + (j if j < 2 else j - 1))
        self.nc.scalar.activation(self.sqp[:, j % 2, :], self.key[:, j % 2, :], ACT.Square).then_inc(self.ksq_done, 1)

    def square_rope(self, act, rope, n, gi):
        act.wait_ge(self.norm_in, gi)
        self.nc.scalar.activation(self.krsq[:, 0:n, :], rope, ACT.Square).then_inc(self.kr_sq, 1)

    def root(self, act, n, gi):
        act.wait_ge(self.norm_in, gi + 1)
        self.nc.scalar.activation(self.rk[:, 0:n, :], self.rk[:, 0:n, :], ACT.Sqrt, bias=self.C["eps"], scale=1.0 / DH).then_inc(self.norm_root, 1)

    def correct(self, act, gi):
        act.wait_ge(self.m_done, gi + 1)
        self.nc.scalar.activation(self.corr, self.m, ACT.Exp, bias=self.negm).then_inc(self.corr_done, 1)

    def exponentials(self, act, n, gi):
        act.wait_ge(self.shift_done, gi + 1)
        self.nc.scalar.activation(self.prob[:, 0:n, :], self.sc[:, 0:n, :], ACT.Exp).then_inc(self.exp_done, 1)

    def finish_act(self, act, b):
        at, gi = b * self.PPB + NPAGES, b * self.GB + GROUPS
        self.copy_page(act, 0, at)
        self.square(act, 0, at)
        self.square_rope(act, self.new_page[:, KL + 1:PGW].rearrange("p (a c) -> p a c", a=1), 1, gi)
        self.root(act, 1, gi)
        self.correct(act, gi)
        self.exponentials(act, 1, gi)
        act.wait_ge(self.latT_done, b + 1)
        for k in range(2):
            dst = self.latT[:, k, :].rearrange("p (h t) -> p h t", h=H)[:, :, ds(b * DQ, DQ)]
            self.nc.scalar.activation(dst, self.acc_ps[:, 320 + k * NS:320 + (k + 1) * NS].rearrange("p (h q) -> p h q", h=H), ACT.Copy)
        self.nc.scalar.drain().then_inc(self.latT_out, 1)

    def start_batch(self):
        v = self.nc.vector
        v.memset(self.m, NEG)
        v.memset(self.acc, 0.0)
        v.drain()

    def key_norm(self, dve, j, at):
        dve.wait_ge(self.ksq_done, at + j + 1)
        self.nc.vector.tensor_reduce(out=self.ssn[:, j, :], in_=self.sqp[:, j % 2, :].rearrange("p (h d) -> p h d", h=H), axis=AX,
                                     op=ALU.add).then_inc(self.ks_done, 1)

    def norm_sum(self, dve, n, gi):
        v = self.nc.vector
        dve.wait_ge(self.kr_sq, gi + 1)
        v.tensor_reduce(out=self.sskr[:, 0:n], in_=self.krsq[:, 0:n, :], axis=AX, op=ALU.add)
        v.drain()
        v.tensor_tensor(self.rk[:, 0:n, :], self.ssn[:, 0:n, :], self.sskr[:, 0:n].unsqueeze(2).to_broadcast([P, n, H]),
                        ALU.add).then_inc(self.norm_in, 1)

    def scale(self, dve, n, at, gi, masked=False):
        v = self.nc.vector
        dve.wait_ge(self.norm_root, gi + 1)
        v.reciprocal(self.rk[:, 0:n, :], self.rk[:, 0:n, :])
        v.drain()
        dve.wait_ge(self.s_done, at + n)
        rkb = self.rk[:, 0:n, :].rearrange("p a h -> p (a h)").unsqueeze(2).to_broadcast([P, n * H, DQ])
        v.tensor_tensor(self.sc[:, 0:n, :].rearrange("p a (h q) -> p (a h) q", h=H),
                        self.small_ps[:, 0:n * NS].rearrange("p (a q) -> p a q", q=DQ), rkb, ALU.mult).then_inc(self.scaled, 1)
        v.drain()
        if masked:
            v.tensor_tensor(self.sc[:, 0, :], self.sc[:, 0, :], self.C["page_mask"], ALU.add)
            v.drain()
        v.tensor_reduce(out=self.pmax, in_=self.sc[:, 0:n, :].rearrange("p a c -> p c a"), axis=AX, op=ALU.max).then_inc(self.pm_done, 1)

    def new_maximum(self, dve, gi):
        v = self.nc.vector
        dve.wait_ge(self.pmT_done, gi + 1)
        v.tensor_reduce(out=self.gmax, in_=self.small_ps[0:NS, 256:256 + P], axis=AX, op=ALU.max)
        v.drain()
        v.tensor_tensor(self.mnew, self.m, self.gmax, ALU.max)
        v.drain()
        v.tensor_scalar(self.diag, self.C["ident"][0:NS, 0:NS], self.mnew, None, ALU.mult)
        v.tensor_scalar(self.negm, self.mnew, -1.0, None, ALU.mult)
        v.drain().then_inc(self.m_done, 1)

    def subtract(self, dve, n, gi):
        dve.wait_ge(self.mb_done, gi + 1)
        self.nc.vector.tensor_tensor(self.sc[:, 0:n, :], self.sc[:, 0:n, :],
                                     self.small_ps[:, 384:384 + NS].unsqueeze(1).to_broadcast([P, n, NS]), ALU.subtract).then_inc(self.shift_done, 1)

    def accumulate(self, dve, gi):
        v = self.nc.vector
        dve.wait_ge(self.corr_done, gi + 1)
        v.tensor_copy(self.m, self.mnew)
        dve.wait_ge(self.pv_done, gi + 1)
        v.scalar_tensor_tensor(out=self.acc, in0=self.acc, scalar=self.corr, in1=self.acc_ps[0:NS, 0:KL + 1], op0=ALU.mult,
                               op1=ALU.add).then_inc(self.acc_out, 1)
        v.drain()

    def finish_dve(self, dve, b):
        at, gi = b * self.PPB + NPAGES, b * self.GB + GROUPS
        v = self.nc.vector
        self.key_norm(dve, 0, at)
        self.norm_sum(dve, 1, gi)
        self.scale(dve, 1, at, gi, masked=True)
        self.new_maximum(dve, gi)
        self.subtract(dve, 1, gi)
        self.accumulate(dve, gi)
        v.reciprocal(self.rl, self.acc[:, KL:KL + 1])
        v.drain()
        dve.wait_ge(self.latT_done, b)
        v.tensor_scalar(self.lat, self.acc[:, 0:KL], self.rl, None, ALU.mult).then_inc(self.lat_done, 1)
        v.drain()


def peer(env, tag, r0, nr, with_pages):
    nc, I, O, ar, C = (env[k] for k in ("nc", "I", "O", "ar", "C"))
    yall, xn2 = ar.at(YALL, P, NT, D), ar.at(XN2, P, NT, D)
    ids, gates, s_dram = env["ids"], env["gates"], env["s_dram"]
    w = XN2 + NT * D
    u_ring = ar.at(w, P, RING, D); w += RING * D
    v_ring = ar.at(w, P, RING, D); w += RING * D
    diag = ar.at(w, P, TOPK, P); w += TOPK * P
    xcur = ar.at(w, P, D); w += D
    uid = [ar.at(w + 8 * j, P, 8).bitcast(U32) for j in range(2)]; w += 16
    vid = [ar.at(w + 8 * j, P, 8).bitcast(U32) for j in range(2)]; w += 16
    a, a2, th, wt = (ar.at(w + 16 * j, P, TOPK) for j in range(4)); w += 64
    with ExitStack() as ctx:
        sem = lambda n: ctx.enter_context(nc.semaphore(tag + n))
        acc = ctx.enter_context(nc.psum_tensor("ps_acc" + tag, [P, 2, 512], F32))
        ps = ctx.enter_context(nc.psum_tensor("ps_pages" + tag, [P, 6, 512], F32))
        rt = Route(env, w, sem, not with_pages)
        pg = Pages(env, rt.end, sem, ps) if with_pages else None
        assert (pg or rt).end <= LATE, ((pg or rt).end, LATE)
        PPB, GB = Pages.PPB, Pages.GB
        u_in, v_in = [sem(f"i_u_in{j}") for j in range(RING)], [sem(f"i_v_in{j}") for j in range(RING)]
        uid_set, vid_set, u_used, v_used = (sem("i_" + n) for n in ("uid", "vid", "u_used", "v_used"))
        x_set, act_in, tanh_done, w_done, diag_done, acc_out = (
            sem("i_" + n) for n in ("x_set", "act_in", "tanh", "w", "diag", "acc_out"))
        fold_done, fold_out, stored = sem("i_fold"), sem("i_fold_out"), sem("i_stored")
        block = ctx.enter_context(nc.Block())

        def steps(eng, step, finish):
            if with_pages:
                with eng.Fori(0, DB - 1) as b:
                    with eng.Fori(0, GROUPS) as g:
                        step(b * GROUPS + g, b, g, True, True)
                    finish(b)
                b = DB - 1
                with eng.Fori(0, GROUPS - 2) as g:
                    step(g + b * GROUPS, b, g, True, True)
                step(nr - 2, b, GROUPS - 2, True, False)
                step(nr - 1, b, GROUPS - 1, False, False)
                finish(b)
            else:
                with eng.Fori(0, nr - 2) as c:
                    step(c, 0, 0, True, True)
                step(nr - 2, 0, 0, True, False)
                step(nr - 1, 0, 0, False, False)

        def gather(ring, j, idx, table, done):
            nc.gpsimd.indirect_dma_start(out=ring[:, j, :], out_offset=None, in_=I[table],
                                         in_offset=bass.IndirectOffsetOnAxis(ap=idx, axis=0)).then_inc(done[j], 16)

        @block.sync
        def _(sp):
            if pg:
                pg.load_first(sp)
                pg.load_new(sp, 0)
                pg.load_group(sp, 0, 0)
            for c in range(3):
                rt.load(sp, c, r0 + c, s_dram)
            if pg:
                with sp.Fori(0, GROUPS - 1) as g:
                    pg.load_group(sp, 0, g + 1)
                    rt.load(sp, g + 3, r0 + g + 3, s_dram)
                with sp.Fori(1, DB - 1) as b:
                    pg.load_new(sp, b)
                    with sp.Fori(0, GROUPS) as g:
                        pg.load_group(sp, b, g)
                        rt.load(sp, b * GROUPS + g + 2, r0 + b * GROUPS + g + 2, s_dram)
                pg.load_new(sp, DB - 1)
                with sp.Fori(0, GROUPS - 2) as g:
                    pg.load_group(sp, DB - 1, g)
                    rt.load(sp, g + (DB - 1) * GROUPS + 2, g + r0 + (DB - 1) * GROUPS + 2, s_dram)
                for g in range(GROUPS - 2, GROUPS):
                    pg.load_group(sp, DB - 1, g)
                sp.wait_ge(acc_out, nr)
                sp.dma_start(O["y_prompt"].rearrange("(t p) d -> p t d", p=P), yall[:, 0:PT, :]).then_inc(stored, 16)
                sp.wait_ge(stored, 16)
            else:
                rt.load(sp, 3, r0 + 3, s_dram)
                sp.wait_ge(fold_out, 1)
                sp.dma_start(O["y_sample"], xcur[0:NS, :]).then_inc(stored, 16)
                sp.wait_ge(stored, 16)

        @block.gpsimd
        def _(pool):
            if pg:
                pg.clear()
            pool.wait_ge(rt.done, 1)
            for half in range(2):
                nc.gpsimd.tensor_copy(uid[half], ids[:, r0 * TOPK + half * 8:r0 * TOPK + half * 8 + 8]).then_inc(uid_set, 1)
                pool.wait_ge(uid_set, half + 1)
                for j in range(RING):
                    if half:
                        pool.wait_ge(u_used, j + 1)
                    gather(u_ring, j, uid[half][:, j:j + 1], "peer_u", u_in)

            def step(c, more, first=False):
                for half in range(2):
                    if more:
                        pool.wait_ge(u_used, c * 16 + half * 8 + 8)
                        pool.wait_ge(rt.done, c + 2)
                        nc.gpsimd.tensor_copy(uid[half], ids[:, ds((c + r0 + 1) * TOPK + half * 8, 8)]).then_inc(uid_set, 1)
                        pool.wait_ge(uid_set, c * 2 + half + 3)
                    if half or not first:
                        pool.wait_ge(v_used, c * 16 + half * 8 - 8)
                    nc.gpsimd.tensor_copy(vid[half], ids[:, ds((c + r0) * TOPK + half * 8, 8)]).then_inc(vid_set, 1)
                    pool.wait_ge(vid_set, c * 2 + half + 1)
                    for j in range(RING):
                        if more:
                            wait_apart(pool, u_used, c * 16 + half * 8 + 8 + j + 1, (uid_set, 1))
                            gather(u_ring, j, uid[half][:, j:j + 1], "peer_u", u_in)
                        if half or not first:
                            wait_apart(pool, v_used, c * 16 + half * 8 - 8 + j + 1, (vid_set, 1))
                        gather(v_ring, j, vid[half][:, j:j + 1], "peer_v", v_in)

            step(0, True, first=True)
            with pool.Fori(1, nr - 1) as c:
                step(c, True)
            step(nr - 1, False)

        @block.scalar
        def _(act):
            def set_x(t):
                nc.scalar.activation(xcur, t, ACT.Copy).then_inc(x_set, 1)

            def tanh(n):
                act.wait_ge(act_in, n)
                nc.scalar.activation(th, th, ACT.Tanh, scale=0.7978845608028654).then_inc(tanh_done, 1)

            def step(c, b, g, more, ahead):
                if more:
                    act.wait_ge(u_used, c * 16 + 16)
                    set_x(one(xn2[:, ds((c + r0 + 1) // H, 1), :]))
                act.wait_ge(w_done, c + 1)
                act.wait_ge(v_used, c * 16)
                for s in range(TOPK):
                    nc.scalar.activation(diag[:, s, :], C["ident"], ACT.Copy, scale=wt[:, s:s + 1]).then_inc(diag_done, 1)
                if pg:
                    at, gi = b * PPB + g * GP, b * GB + g
                    pg.copy_page(act, 0, at)
                    for j in range(1, GP):
                        pg.copy_page(act, j, at)
                        pg.square(act, j - 1, at)
                    pg.square(act, GP - 1, at)
                    pg.square_rope(act, pg.pages[:, :, KL + 1:PGW], GP, gi)
                    pg.root(act, GP, gi)
                if ahead:
                    rt.softmax(act, c + 2)
                if pg:
                    pg.correct(act, gi)
                    pg.exponentials(act, GP, gi)
                if more:
                    tanh(c + 2)

            rt.softmax(act, 0)
            set_x(xn2[:, r0 // H, :])
            rt.softmax(act, 1)
            tanh(1)
            steps(act, step, lambda b: pg.finish_act(act, b))

        @block.tensor
        def _(pe):
            def add(c, s):
                pe.wait_ge(diag_done, c * 16 + s + 1)
                pe.wait_ge(v_in[s % RING], (c * 2 + s // RING) * 16 + 16)
                for n in range(2):
                    last = nc.tensor.matmul(acc[:, n, :], diag[:, s, :], v_ring[:, s % RING, n * 512:(n + 1) * 512],
                                            start=s == 0, stop=s == TOPK - 1)
                last.then_inc(v_used, 1)

            def step(c, b, g, more, ahead):
                pe.wait_ge(acc_out, c)
                if pg:
                    at, gi = b * PPB + g * GP, b * GB + g
                for s in range(TOPK):
                    add(c, s)
                    if not pg:
                        continue
                    if s == 3:
                        pg.group_arrived(pe, b, g)
                        pg.transposes(pe, pg.pages[:, 0, :], 0, at)
                    if s in (4, 6, 7):
                        j = {4: 1, 6: 2, 7: 3}[s]
                        pg.transposes(pe, pg.pages[:, j, :], j, at)
                        pg.keys(pe, j - 1, at, gi, b)
                    if s == 8:
                        pg.keys(pe, GP - 1, at, gi, b)
                    if s == 11:
                        pg.maxima(pe, gi)
                    if s == 13:
                        pg.spread_maxima(pe, gi)
                if pg:
                    pg.weigh(pe, [pg.pages[:, j, :] for j in range(GP)], gi)

            if pg:
                pe.wait_ge(pg.loaded, 32)
            steps(pe, step, lambda b: pg.finish_pe(pe, b))
            if not with_pages:
                pe.wait_ge(acc_out, nr)
                for n in range(2):
                    last = nc.tensor.matmul(ps[0:NS, n, :], C["fold"], yall[:, NT - 1, n * 512:(n + 1) * 512], start=True, stop=True)
                last.then_inc(fold_done, 1)

        @block.vector
        def _(dve):
            v, fence = nc.vector, nc.vector.drain

            def dot(c, s):
                if s == 0:
                    dve.wait_ge(x_set, c + 1)
                dve.wait_ge(u_in[s % RING], (c * 2 + s // RING) * 16 + 16)
                v.tensor_tensor_reduce(out=u_ring[:, s % RING, :], in0=u_ring[:, s % RING, :], in1=xcur, scale=1.0, scalar=0.0,
                                       op0=ALU.mult, op1=ALU.add, accum_out=a[:, s:s + 1]).then_inc(u_used, 1)

            def weights(c):
                fence()
                v.tensor_tensor(a2, a, a, ALU.mult)
                fence()
                v.tensor_scalar(a2, a2, 0.044715, 1.0, ALU.mult, ALU.add)
                fence()
                v.tensor_tensor(th, a2, a, ALU.mult)
                fence().then_inc(act_in, 1)
                v.scalar_tensor_tensor(out=a2, in0=a, scalar=0.5, in1=gates[:, ds((c + r0) * TOPK, TOPK)], op0=ALU.mult, op1=ALU.mult)
                fence()
                dve.wait_ge(tanh_done, c + 1)
                dve.wait_ge(diag_done, c * 16)
                v.scalar_tensor_tensor(out=wt, in0=th, scalar=1.0, in1=a2, op0=ALU.add, op1=ALU.mult).then_inc(w_done, 1)

            def collect(c):
                dve.wait_ge(v_used, c * 16 + 16)
                y = one(yall[:, ds((c + r0) // H, 1), :])
                v.tensor_tensor(y, y, acc[:, :, :].rearrange("p a b -> p (a b)"), ALU.add).then_inc(acc_out, 1)
                fence()

            def route(c):
                rt.top_eight(dve, c)
                rt.top_sixteen()
                rt.pairs()
                rt.experts(dve, c, c + r0)

            def step(c, b, g, more, ahead):
                if pg:
                    at, gi = b * PPB + g * GP, b * GB + g
                for s in range(TOPK):
                    if more:
                        dot(c + 1, s)
                    if ahead:
                        if s == 0:
                            rt.top_eight(dve, c + 2)
                        if s == 1:
                            rt.top_sixteen()
                        if s == 3:
                            rt.pairs()
                        if s == 11:
                            rt.experts(dve, c + 2, c + 2 + r0)
                    if pg:
                        if s in (5, 6, 8, 9):
                            pg.key_norm(dve, {5: 0, 6: 1, 8: 2, 9: 3}[s], at)
                        if s == 9:
                            pg.norm_sum(dve, GP, gi)
                        if s == 10:
                            pg.scale(dve, GP, at, gi)
                        if s == 12:
                            pg.new_maximum(dve, gi)
                        if s == 14:
                            pg.subtract(dve, GP, gi)
                if more:
                    weights(c + 1)
                collect(c)
                if pg:
                    pg.accumulate(dve, gi)

            route(0)
            route(1)
            for s in range(TOPK):
                dot(0, s)
            weights(0)
            if pg:
                pg.start_batch()

            def finish(b):
                pg.finish_dve(dve, b)
                pg.start_batch()

            steps(dve, step, finish)
            if not with_pages:
                dve.wait_ge(fold_done, 1)
                v.tensor_copy(xcur[0:NS, :], ps[0:NS, 0:2, :].rearrange("p a b -> p (a b)")).then_inc(fold_out, 1)


_OUTS = {"y_prompt": (SEQ, D), "y_sample": (NS, D), "ckvT": (P, 2, TOK), "kropeT": (DR, TOK),
         "poolT": (P, G, STATE), "poolsT": (P, G, DB, STATE)}


def constants():
    import numpy as np
    ident = np.eye(P, dtype=np.float32)
    k, q = np.arange(P), np.arange(P)
    causal = np.where(k[None, :] <= q[:, None], 0.0, NEG)
    hq = np.arange(NS) % DQ
    page_mask = np.where((k[:, None] < DQ) & (k[:, None] <= hq[None, :]), 0.0, NEG)
    inv = np.zeros((G, PAD))
    for g in range(G):
        inv[g] = 1.0 / np.minimum(np.arange(PAD) + 1, 2 << g)
    half = DR // 2
    pos = np.concatenate([np.arange(SEQ), 4096 + np.tile(np.arange(DQ), 2 * DB)]).astype(np.float32)
    freq = np.float32(10000.0) ** (-np.arange(half, dtype=np.float32) / np.float32(half))
    ang = (pos[None, :] * freq[:, None]).astype(np.float32)
    cos = np.concatenate([np.cos(ang)] * 2).astype(np.float32)
    sin = np.concatenate([-np.sin(ang), np.sin(ang)]).astype(np.float32)
    return dict(ident=ident, causal=causal, page_mask=page_mask, iota16=np.tile(np.arange(TOPK), (P, 1)),
                invcnt=np.tile(inv.reshape(1, -1), (P, 1)), fold=ident[:, 0:NS] + ident[:, NS:P]), cos, sin


def kernel(**inp):
    import numpy as np
    import concourse.bacc as bacc
    from concourse.bass_utils import run_bass_kernel_spmd

    A = {k: np.asarray(v) for k, v in inp.items()}

    def chunked(w):
        return w.reshape(w.shape[0] // P, P, w.shape[1]).transpose(1, 0, 2)

    def cols(w):
        return w.reshape(-1, P).T

    xs = A["x_sample"].reshape(NS, D)
    x = np.concatenate([A["x_prompt"][0], xs, xs])
    win = A["w_in"][0]
    o_kr, o_pool, o_gate = QL + KL, QL + KL + DR, QL + KL + DR + G * P
    swap = np.r_[DR // 2:DR, 0:DR // 2]
    kr = win[:, o_kr:o_pool]
    front = np.concatenate([win[:, 0:o_kr], win[:, o_pool:o_gate], kr, kr[:, swap]], axis=1)
    wq = A["w_q_up"][0]
    tables, cos, sin = constants()
    norms = dict(ones=np.ones((P, P)), w1=cols(A["norm1_w"][0]), wq_lat=cols(A["q_lat_norm_w"][0]), wkv=cols(A["kv_lat_norm_w"][0]),
                 pool_scale=cols(A["pool_scale"][0]), eps=np.full((P, 1), EPS),
                 wqk=np.zeros((P, 1), np.float32))
    consts = np.concatenate([np.asarray({**tables, **norms}[n], np.float32) for n, _ in CONSTS], axis=1)
    merge_w = np.stack([np.concatenate([chunked(win[:, o_gate + a * D + d * P:o_gate + a * D + (d + 1) * P]) for a in range(2)]
                                       + [chunked(A[n][0][:, d * P:(d + 1) * P]) for n in ("w_attn_br", "w_pool_br")], axis=1)
                        for d in range(KD)])
    keys = A["peer_keys"][0].reshape(2 * H, NK, P).transpose(0, 2, 1)
    peer_w = np.stack([np.concatenate([chunked(A["peer_w_q"][0][:, j * P:(j + 1) * P]), keys[j][:, None, :]], axis=1) for j in range(2 * H)])
    arrays = {
        "consts": consts, "qk_norms": np.stack([A["q_norm_w"][0], A["k_norm_w"][0]], axis=1),
        "xT": chunked(x.T), "x_tok": x.reshape(NT, P, D), "cos": cos, "sin": sin,
        "w_front": chunked(front), "w_q_up": chunked(wq.reshape(QL, H * DH)), "w_q_sw": chunked(wq[:, :, DN + swap].reshape(QL, H * DR)),
        "w_uk": chunked(A["w_uk"][0].reshape(KL, H * DN)), "w_ukT": A["w_uk"][0].transpose(2, 1, 0),
        "w_uv": chunked(A["w_uv"][0].reshape(KL, H * DN)), "pool_lin": A["pool_lin_w"][0].transpose(1, 0, 2),
        "stateT": A["state_pool"][0].reshape(DB, STATE, G, P).transpose(3, 2, 0, 1),
        "page_table": A["page_table"].reshape(1, DB * NPAGES), "cache_ckv": A["cache_ckv"][0], "cache_krope": A["cache_krope"][0],
        "w_merge": merge_w, "w_out": chunked(A["w_out"][0]), "norm2": np.tile(A["norm2_w"], (P, 1)), "w_peer": peer_w,
        "peer_u": A["peer_u"][0], "peer_v": A["peer_v"][0],
    }
    nc = bacc.Bacc("TRN2", target_bir_lowering=False, num_devices=1)
    ins, feed = {}, {}
    for name, a in arrays.items():
        a = np.ascontiguousarray(a)
        feed["in_" + name] = a
        ins[name] = nc.dram_tensor("in_" + name, a.shape, mybir.dt.from_np(a.dtype), kind="ExternalInput").ap()
    outs = {name: nc.dram_tensor("out_" + name, shape, F32, kind="ExternalOutput").ap() for name, shape in _OUTS.items()}
    build(nc, ins, outs)
    res = run_bass_kernel_spmd(nc, [feed], core_ids=[0]).results[0]
    got = {name: np.asarray(res["out_" + name]) for name in _OUTS}
    ckv = got["ckvT"].transpose(2, 1, 0).reshape(TOK, KL)
    kro = got["kropeT"].T
    return (got["y_prompt"].reshape(1, SEQ, D), got["y_sample"].reshape(DB, DQ, D),
            ckv[0:SEQ].reshape(1, 1, SEQ, KL), kro[0:SEQ].reshape(1, 1, SEQ, DR),
            got["poolT"].transpose(2, 1, 0).reshape(1, 1, STATE, G * P),
            ckv[SEQ:SEQ + NS].reshape(1, DB, DQ, KL), kro[SEQ:SEQ + NS].reshape(1, DB, DQ, DR),
            got["poolsT"].transpose(2, 3, 1, 0).reshape(1, DB, STATE, G * P))
```

```python
from contextlib import ExitStack

import concourse.bass as bass
from concourse import mybir

F32 = mybir.dt.float32
U32 = mybir.dt.uint32
I32 = mybir.dt.int32
ALU = mybir.AluOpType
ACT = mybir.ActivationFunctionType
AX = mybir.AxisListType.X
ds = bass.ds

D, SEQ, DB, DQ = 1024, 1024, 8, 8
P = 128
KD = D // P
NS = DB * DQ
TOK = SEQ + 2 * NS
NT = TOK // P
PT = SEQ // P
NW = 384
NN = TOK // NW
H, DN, DR, DH = 8, 64, 32, 96
QL, KL = 384, 256
G, STATE = 4, 15
PAD = 16
PAGE, NPAGES, NPHYS = 128, 32, 320
EARLY = 3
EARLY_AT = H // 2
GP = 4
GROUPS = NPAGES // GP
PGW = KL + 1 + DR
NK, TOPK = 128, 16
NEXP = NK * NK
ROUTES = PT * H + H // 2
NEG = -1e30
LOWEST = -3.0e38
EPS = 1e-6
RING = 8
LEAD = 3
KEYS_AT = (3, 5, 7, 8, 9)
SCORES_AT = KEYS_AT[-1] + 1
W_FRONT = QL + KL + 4 * P + 2 * DR


class Arena:

    def __init__(self, tensor):
        self.tensor = tensor

    def at(self, word, parts, *dims):
        n = 1
        for d in dims:
            n *= d
        v = self.tensor[0:parts, word:word + n]
        if len(dims) == 2:
            return v.rearrange("p (a b) -> p a b", a=dims[0])
        if len(dims) == 3:
            return v.rearrange("p (a b c) -> p a b c", a=dims[0], b=dims[1])
        return v


def wait_apart(eng, sem, value, met):
    value = eng.compute_val(value)
    eng.wait_ge(*met)
    eng.wait_ge(sem, value)


def one(ap):
    return ap.rearrange("p a b -> p (a b)")


def build(nc, I, O):
    with ExitStack() as ctx:
        ar = Arena(ctx.enter_context(nc.sbuf_tensor("arena", [P, TOP], F32)))
        const = ctx.enter_context(nc.sbuf_tensor("const", [P, CONST_COLS], F32))
        xn_dram = nc.dram_tensor("xn_spill", [P, KD, TOK], F32, kind="Internal").ap()
        new_rows = nc.dram_tensor("new_rows", [P, KL + DR], F32, kind="Internal").ap()
        table = ctx.enter_context(nc.sbuf_tensor("page_ids", [1, DB * NPAGES], I32))
        qk_norms = ctx.enter_context(nc.sbuf_tensor("qk_norms", [DH, 2], F32))
        s_dram = nc.dram_tensor("key_scores", [P, NT * H, 2 * NK], F32, kind="Internal").ap()

        C = {}
        col = 0
        for name, w in CONSTS:
            C[name] = const[:, col:col + w]
            col += w
        env = dict(nc=nc, I=I, O=O, ar=ar, C=C, const=const, xn_dram=xn_dram, new_rows=new_rows, s_dram=s_dram,
                   table=table, qk_norms=qk_norms, ids=ar.at(LATE, P, N_IDS).bitcast(U32), gates=ar.at(LATE + N_IDS, P, N_IDS))
        early = []

        def early_sem(name):
            early.append(nc.alloc_semaphore(name))
            return early[-1]

        env["early_sem"] = early_sem
        project(env)
        pool_and_values(env)
        prompt_attention(env)
        nc.clear_and_free_semaphores(early)
        nc.all_engine_barrier()
        late_sem = lambda n: ctx.enter_context(nc.semaphore(n))
        prompt = Part(env, "p", 0, PT, 512, ar.at(AT, P, 4, TOK), ar.at(ZL, P, G, TOK), (YALL + PT * D, XN2 + PT * D), late_sem)
        sample = Part(env, "s", PT, 1, P, ar.at(ATS, P, 4, P), ar.at(ZLS, P, G, P), (XN2, XN2 + D), late_sem)
        env["y_stored"] = late_sem("y_stored")
        sample_queries(env, prompt)
        merge(env, prompt)
        residual(env, prompt)
        peer_scores(env, prompt, Route(env, lambda n: late_sem("p" + n), False))
        peer(env, "p", 0, PT * H, prompt.rt)
        sample_output(env, sample)
        merge(env, sample)
        residual(env, sample)
        peer_scores(env, sample, Route(env, lambda n: late_sem("s" + n), True))
        peer(env, "s", PT * H, H // 2, sample.rt)


CONSTS = [("ident", P), ("ones", P), ("causal", P), ("page_mask", NS), ("iota16", TOPK), ("w1", KD), ("wq_lat", 3),
          ("wkv", 2), ("wqk", 1), ("pool_scale", G), ("invcnt", G * PAD), ("eps", 1), ("fold", NS), ("pick", 2 * H - 1)]
CONST_COLS = sum(w for _, w in CONSTS)

TOP = 51984
N_IDS = ROUTES * TOPK
ZLS = TOP - G * P
QROPE = ZLS - H * NS
QLAT = QROPE - 2 * H * NS
ATS = QLAT - 4 * P
LATT = ATS - 2 * H * NS
LATE = LATT - 2 * N_IDS
QT = TOP - H * TOK
KT = QT - H * TOK
CT = KT - 2 * TOK
KRT = CT - TOK
UP = KRT - G * (PAD + TOK)
VV = 0
ZL = VV + PT * 512
AT = 17984
YALL = 0
XN2 = YALL + NT * D
XN2T = XN2 + NT * D
MT = XN2T + KD * SEQ
XNT = MT + KD * SEQ
MERGE_RING = ZL + G * TOK
ROUTE_AT = XN2T + 2 * RING * D + TOPK * P + D + 32 + 64
WOUT_AHEAD = 6
WOUT = XNT + KD * SEQ
assert WOUT + WOUT_AHEAD * D <= QLAT


def project(env):
    nc, I, ar, C = env["nc"], env["I"], env["ar"], env["C"]
    w = 0

    def take(*dims):
        nonlocal w
        n = 1
        for d in dims:
            n *= d
        w += n
        return ar.at(w - n, P, *dims)

    wfront, wqup, wqsw, wuk = take(KD, W_FRONT), take(3, H * DH), take(3, H * DR), take(2, H * DN)
    spread = take(H, DH)
    xt, sq, qlat, kv = take(KD, NW), take(4, NW), take(3, NW), take(2, NW)
    cos, sin, rr, sqh = take(NW), take(NW), take(3, NW), take(2, NW)
    rot1, rot2, rh = take(NW), take(NW), take(2, NW)
    assert w <= UP, (w, UP)
    qT, kT = ar.at(QT, P, H, TOK), ar.at(KT, P, H, TOK)
    cT, krT, uP = ar.at(CT, P, 2, TOK), ar.at(KRT, P, TOK), ar.at(UP, P, G, PAD + TOK)
    chunks = [(j * P, "q", j) for j in range(3)] + [(QL + j * P, "kv", j) for j in range(2)] \
        + [(QL + KL + j * P, "pool", j) for j in range(G)]
    KR0 = QL + KL + G * P
    NCH = len(chunks)
    U = 2 * H

    with ExitStack() as ctx:
        sem = env["early_sem"]
        ps = ctx.enter_context(nc.psum_tensor("ps_a", [P, 8, 512], F32))
        pj, ss, pa, pb = (ps[:, 2 * j:2 * j + 2, 0:NW] for j in range(4))
        front_in, units_in = sem("a_front_in"), sem("a_units_in")
        loaded, x_in, xn_saved, tables_in = sem("a_loaded"), sem("a_x_in"), sem("a_xn_saved"), sem("a_tables_in")
        sq_done, sq_used, std_done, x_scaled, rr_done, xn_done = (
            sem("a_" + n) for n in ("sq_done", "sq_used", "std_done", "x_scaled", "rr_done", "xn_done"))
        chunk_done, chunk_out, kr_done, kr_out, lat_done = (
            sem("a_" + n) for n in ("chunk_done", "chunk_out", "kr_done", "kr_out", "lat_done"))
        up_done, up_squared, summed, root_done, inv_done, up_copied, rotated, spread_done, unit_out = (
            sem("a_" + n) for n in ("up", "up_squared", "summed", "root", "inv", "up_copied", "rotated", "spread", "unit_out"))
        pads = sem("a_pads")
        block = ctx.enter_context(nc.Block())

        @block.sync
        def _(sp):
            sp.dma_start(env["const"][:, 0:CONST_COLS], I["consts"]).then_inc(loaded, 16)
            sp.dma_start(env["qk_norms"][:, :], I["qk_norms"]).then_inc(loaded, 16)
            sp.dma_start(xt, I["xT"][:, :, 0:NW]).then_inc(x_in, 16)
            sp.dma_start(wfront, I["w_front"]).then_inc(front_in, 16)
            for dst, src in ((wqup, "w_q_up"), (wqsw, "w_q_sw"), (wuk, "w_uk"), (spread[0:H], "spread")):
                sp.dma_start(dst, I[src]).then_inc(units_in, 16)
            def step(n):
                sp.wait_ge(rotated, n * H)
                sp.dma_start(cos[64:96, :], I["cos"][:, ds(n * NW, NW)]).then_inc(tables_in, 16)
                sp.dma_start(sin[64:96, :], I["sin"][:, ds(n * NW, NW)]).then_inc(tables_in, 16)
                sp.wait_ge(xn_done, n + 1)
                sp.dma_start(env["xn_dram"][:, :, ds(n * NW, NW)], xt).then_inc(xn_saved, 16)

            with sp.Fori(0, NN - 1) as n:
                step(n)
                sp.wait_ge(xn_saved, n * 16 + 16)
                sp.dma_start(xt, I["xT"][:, :, ds(n * NW + NW, NW)]).then_inc(x_in, 16)
            step(NN - 1)
            sp.wait_ge(xn_saved, NN * 16)

        @block.gpsimd
        def _(pool):
            nc.gpsimd.memset(uP[:, :, 0:PAD], 0.0).then_inc(pads, 1)
            with pool.Fori(0, NN) as n:
                pool.wait_ge(rr_done, n + 1)
                pool.wait_ge(kr_done, n + 1)
                nc.gpsimd.tensor_tensor(xt, xt, rr[:, 0, :].unsqueeze(1).to_broadcast([P, KD, NW]), ALU.mult).then_inc(xn_done, 1)

        @block.scalar
        def _(act):
            act.wait_ge(loaded, 32)
            with act.Fori(0, NN) as n:
                act.wait_ge(x_in, n * 16 + 16)
                for half in range(2):
                    act.wait_ge(sq_used, n * 4 + half)
                    nc.scalar.activation(sq[:, :, :], xt[:, 4 * half:4 * half + 4, :], ACT.Square).then_inc(sq_done, 1)
                act.wait_ge(sq_used, n * 4 + 2)
                act.wait_ge(xn_done, n)
                nc.scalar.activation(rr[:, 0, :], ss[:, 0, :], ACT.Sqrt, bias=C["eps"], scale=1.0 / D).then_inc(std_done, 1)
                act.wait_ge(chunk_out, n * NCH + 3)
                nc.scalar.activation(sq[:, 0:3, :], qlat[:, :, :], ACT.Square).then_inc(sq_done, 1)
                act.wait_ge(sq_used, n * 4 + 3)
                act.wait_ge(lat_done, n * 5)
                nc.scalar.activation(rr[:, 1, :], ss[:, 1, :], ACT.Sqrt, bias=C["eps"], scale=1.0 / QL).then_inc(std_done, 1)
                act.wait_ge(chunk_out, n * NCH + 5)
                nc.scalar.activation(sq[:, 0:2, :], kv[:, :, :], ACT.Square).then_inc(sq_done, 1)
                act.wait_ge(sq_used, n * 4 + 4)
                nc.scalar.activation(rr[:, 2, :], ss[:, 0, :], ACT.Sqrt, bias=C["eps"], scale=1.0 / KL).then_inc(std_done, 1)

                def unit(u):
                    dst, h = (qT, u) if u < H else (kT, u - H)
                    act.wait_ge(up_done, n * U + u + 1)
                    act.wait_ge(summed, n * U + max(u - 1, 0))
                    rows = DH if u < H else DN
                    nc.scalar.activation(sqh[0:rows, u % 2, :], pa[0:rows, u % 2, :], ACT.Square)
                    if u in (H, H + 1):
                        nc.scalar.activation(sqh[64:96, u % 2, :], krT[64:96, ds(n * NW, NW)], ACT.Square)
                    nc.scalar.drain().then_inc(up_squared, 1)
                    nc.scalar.activation(dst[0:DN, h, ds(n * NW, NW)], pa[0:DN, u % 2, :], ACT.Copy).then_inc(up_copied, 1)

                def root(i):
                    act.wait_ge(summed, n * U + (i + 1) * H)
                    act.wait_ge(spread_done, n * U)
                    nc.scalar.activation(rh[0:H, i, :], ss[0:H, i, :], ACT.Sqrt, bias=C["eps"][0:H], scale=1.0 / DH).then_inc(root_done, 1)

                unit(0)
                act.wait_ge(kr_out, n + 1)
                for u in range(1, H + 1):
                    unit(u)
                root(0)
                for u in range(H + 1, U):
                    unit(u)
                root(1)

        @block.tensor
        def _(pe):
            pe.wait_ge(loaded, 32)
            with pe.Fori(0, NN) as n:
                pe.wait_ge(root_done, n * 2)
                for half in range(2):
                    pe.wait_ge(sq_done, n * 4 + half + 1)
                    for k in range(4):
                        last = nc.tensor.matmul(ss[:, 0, :], C["ones"], sq[:, k, :], start=half + k == 0, stop=half + k == 4)
                    last.then_inc(sq_used, 1)

                def chunk(j):
                    c0 = chunks[j][0]
                    if j < 2:
                        pe.wait_ge(unit_out, n * U)
                    else:
                        pe.wait_ge(chunk_out, n * NCH + j - 1)
                    if j == 0:
                        pe.wait_ge(front_in, 16)
                    for k in range(KD):
                        if j == 0:
                            pe.wait_ge(x_scaled, n * KD + k + 1)
                        last = nc.tensor.matmul(pj[:, j % 2, :], wfront[:, k, c0:c0 + P], xt[:, k, :],
                                                start=k == 0, stop=k == KD - 1)
                    last.then_inc(chunk_done, 1)

                for j in range(5):
                    chunk(j)
                pe.wait_ge(sq_done, n * 4 + 3)
                for k in range(3):
                    last = nc.tensor.matmul(ss[:, 1, :], C["ones"], sq[:, k, :], start=k == 0, stop=k == 2)
                last.then_inc(sq_used, 1)
                for j in range(5, 7):
                    chunk(j)
                pe.wait_ge(sq_done, n * 4 + 4)
                pe.wait_ge(std_done, n * 3 + 1)
                for k in range(2):
                    last = nc.tensor.matmul(ss[:, 0, :], C["ones"], sq[:, k, :], start=k == 0, stop=k == 1)
                last.then_inc(sq_used, 1)
                for j in range(7, NCH):
                    chunk(j)
                pe.wait_ge(chunk_out, n * NCH + NCH)
                for s in range(2):
                    for k in range(KD):
                        last = nc.tensor.matmul(pj[64:96, s, :], wfront[:, k, KR0 + s * DR:KR0 + (s + 1) * DR], xt[:, k, :],
                                                start=k == 0, stop=k == KD - 1)
                last.then_inc(kr_done, 1)

                def up(u):
                    if u in (0, H):
                        pe.wait_ge(lat_done, n * 5 + (3 if u == 0 else 5))
                    if u < H + 2:
                        wait_apart(pe, rotated, n * H + max(u - 1, 0), (loaded, 32))
                    wait_apart(pe, up_copied, n * U + max(u - 1, 0), (loaded, 32))
                    if u < H:
                        h = u
                        for k in range(3):
                            nc.tensor.matmul(pa[0:DH, u % 2, :], wqup[:, k, h * DH:(h + 1) * DH], qlat[:, k, :],
                                             start=k == 0, stop=k == 2)
                        for k in range(3):
                            last = nc.tensor.matmul(pb[64:96, u % 2, :], wqsw[:, k, h * DR:(h + 1) * DR], qlat[:, k, :],
                                                    start=k == 0, stop=k == 2)
                    else:
                        h = u - H
                        for k in range(2):
                            last = nc.tensor.matmul(pa[0:DN, u % 2, :], wuk[:, k, h * DN:(h + 1) * DN], cT[:, k, ds(n * NW, NW)],
                                                    start=k == 0, stop=k == 1)
                    last.then_inc(up_done, 1)

                def total(u):
                    h = u % H
                    pe.wait_ge(up_squared, n * U + u + 1)
                    if u == 0:
                        pe.wait_ge(std_done, n * 3 + 3)
                    nc.tensor.matmul(ss[0:H, u // H, :], C["pick"][0:DH, H - 1 - h:2 * H - 1 - h], sqh[0:DH, u % 2, :],
                                     start=h == 0, stop=h == H - 1).then_inc(summed, 1)

                def spread_root(u):
                    pe.wait_ge(inv_done, n * 2 + u // H + 1)
                    if u < 2:
                        pe.wait_ge(kr_out, n + 1)
                    else:
                        pe.wait_ge(unit_out, n * U + u - 1)
                    nc.tensor.matmul(pj[0:DH, u % 2, :], spread[0:H, u % H, :], rh[0:H, u // H, :], start=True, stop=True).then_inc(spread_done, 1)

                pe.wait_ge(units_in, 64)
                up(0)
                for u in range(1, U):
                    up(u)
                    total(u - 1)
                    if u >= H + 2:
                        spread_root(u - H - 2)
                total(U - 1)
                for u in range(H - 2, U):
                    spread_root(u)

        @block.vector
        def _(dve):
            dve.wait_ge(loaded, 32)
            mul, add = ALU.mult, ALU.add
            v = nc.vector
            v.scalar_tensor_tensor(out=C["wqk"][0:DH], in0=env["qk_norms"][:, 0:1], scalar=DH ** -0.5,
                                   in1=env["qk_norms"][:, 1:2], op0=mul, op1=mul)
            v.drain()
            with dve.Fori(0, NN) as n:
                now = ds(n * NW, NW)
                for k in range(KD):
                    dve.wait_ge(sq_done, n * 4 + k // 4 + 1)
                    v.tensor_scalar(xt[:, k, :], xt[:, k, :], C["w1"][:, k:k + 1], None, mul).then_inc(x_scaled, 1)
                dve.wait_ge(std_done, n * 3 + 1)
                v.reciprocal(rr[:, 0, :], rr[:, 0, :])
                v.drain().then_inc(rr_done, 1)
                for j, (_, what, at) in enumerate(chunks):
                    dve.wait_ge(chunk_done, n * NCH + j + 1)
                    if j == 0:
                        dve.wait_ge(up_done, n * U)
                    dst = {"q": lambda: qlat[:, at, :], "kv": lambda: kv[:, at, :],
                           "pool": lambda: uP[:, at, ds(PAD + n * NW, NW)]}[what]()
                    v.tensor_tensor(dst, pj[:, j % 2, :], rr[:, 0, :], mul).then_inc(chunk_out, 1)
                    if j == 6:
                        dve.wait_ge(std_done, n * 3 + 2)
                        v.reciprocal(rr[:, 1, :], rr[:, 1, :])
                        v.drain()
                        for k in range(3):
                            v.scalar_tensor_tensor(out=qlat[:, k, :], in0=qlat[:, k, :], scalar=C["wq_lat"][:, k:k + 1],
                                                   in1=rr[:, 1, :], op0=mul, op1=mul).then_inc(lat_done, 1)
                    if j == 8:
                        dve.wait_ge(std_done, n * 3 + 3)
                        v.reciprocal(rr[:, 2, :], rr[:, 2, :])
                        v.drain()
                        for k in range(2):
                            v.scalar_tensor_tensor(out=cT[:, k, now], in0=kv[:, k, :], scalar=C["wkv"][:, k:k + 1],
                                                   in1=rr[:, 2, :], op0=mul, op1=mul).then_inc(lat_done, 1)
                dve.wait_ge(kr_done, n + 1)
                dve.wait_ge(tables_in, n * 32 + 32)
                v.tensor_tensor(rot1[64:96, :], pj[64:96, 0, :], cos[64:96, :], mul)
                v.tensor_tensor(rot2[64:96, :], pj[64:96, 1, :], sin[64:96, :], mul)
                v.drain()
                v.tensor_tensor(rot1[64:96, :], rot1[64:96, :], rot2[64:96, :], add)
                v.drain()
                v.tensor_tensor(krT[64:96, now], rot1[64:96, :], rr[64:96, 0, :], mul)
                v.drain().then_inc(kr_out, 1)
                for h in range(H):
                    dve.wait_ge(up_squared, n * U + h + 1)
                    v.tensor_tensor(rot1[64:96, :], pa[64:96, h % 2, :], cos[64:96, :], mul)
                    v.tensor_tensor(rot2[64:96, :], pb[64:96, h % 2, :], sin[64:96, :], mul)
                    v.drain()
                    v.tensor_tensor(qT[64:96, h, now], rot1[64:96, :], rot2[64:96, :], add)
                    v.drain().then_inc(rotated, 1)
                for u in range(U):
                    if u % H == 0:
                        dve.wait_ge(root_done, n * 2 + u // H + 1)
                        v.reciprocal(rh[0:H, u // H, :], rh[0:H, u // H, :])
                        v.drain().then_inc(inv_done, 1)
                    h, r = u % H, pj[:, u % 2, :]
                    dve.wait_ge(spread_done, n * U + u + 1)
                    dve.wait_ge(up_copied, n * U + u + 1)
                    if u < H:
                        v.scalar_tensor_tensor(out=qT[0:DH, h, now], in0=qT[0:DH, h, now], scalar=C["wqk"][0:DH], in1=r[0:DH],
                                               op0=mul, op1=mul).then_inc(unit_out, 1)
                    else:
                        v.tensor_tensor(kT[0:DN, h, now], kT[0:DN, h, now], r[0:DN], mul)
                        v.tensor_tensor(kT[64:96, h, now], krT[64:96, now], r[64:96], mul)
                        v.drain().then_inc(unit_out, 1)


def pool_and_values(env):
    nc, I, O, ar, C = (env[k] for k in ("nc", "I", "O", "ar", "C"))
    cT, krT, uP = ar.at(CT, P, 2, TOK), ar.at(KRT, P, TOK), ar.at(UP, P, G, PAD + TOK)
    vv, zl = ar.at(VV, P, PT, 512), ar.at(ZL, P, G, TOK)
    w = ZL + G * TOK
    z = ar.at(w, P, G, TOK); w += G * TOK
    part = [ar.at(w + s * (PAD + SEQ), P, PAD + SEQ) for s in range(2)]; w += 2 * (PAD + SEQ)
    wuv = ar.at(w, P, 2, 512); w += 1024
    wlin = ar.at(w, P, G, P); w += G * P
    us = ar.at(w, P, G, DB * (STATE + DQ)); w += G * DB * (STATE + DQ)
    uspart = [ar.at(w + s * DB * 23, P, DB, STATE + DQ) for s in range(2)]; w += 2 * DB * 23
    rows = ar.at(w, P, KL + DR); w += KL + DR
    assert w <= UP
    us4 = [us[:, g, :].rearrange("p (b t) -> p b t", b=DB) for g in range(G)]
    NZ = 3
    with ExitStack() as ctx:
        sem = env["early_sem"]
        ps = ctx.enter_context(nc.psum_tensor("ps_b", [P, 8, 512], F32))
        loaded, stored, v_done, v_out = sem("b_loaded"), sem("b_stored"), sem("b_v_done"), sem("b_v_out")
        us_ready, window, z_done, lin_done, zl_done = (sem("b_" + n) for n in ("us", "window", "z", "lin", "zl"))
        rows_done, rows_out, z_started = sem("b_rows_done"), sem("b_rows_out"), sem("b_z_started")
        block = ctx.enter_context(nc.Block())

        @block.sync
        def _(sp):
            sp.dma_start(wuv, I["w_uv"]).then_inc(loaded, 16)
            sp.dma_start(wlin, I["pool_lin"]).then_inc(loaded, 16)
            for g in range(G):
                sp.dma_start(us4[g][:, :, 0:STATE], I["stateT"][:, g, :, :]).then_inc(loaded, 16)
            sp.dma_start(O["ckvT"], cT).then_inc(stored, 16)
            sp.dma_start(O["kropeT"], krT[64:96, :]).then_inc(stored, 16)
            sp.dma_start(O["poolT"], uP[:, :, PAD + SEQ - STATE:PAD + SEQ]).then_inc(stored, 16)
            sp.wait_ge(us_ready, 1)
            for g in range(G):
                sp.dma_start(O["poolsT"][:, g, :, :], us4[g][:, :, DQ:DQ + STATE]).then_inc(stored, 16)
            sp.wait_ge(rows_out, 2)
            sp.dma_start(env["new_rows"], rows).then_inc(stored, 16)
            sp.wait_ge(stored, 8 * 16)

        @block.tensor
        def _(pe):
            pe.wait_ge(loaded, 96)
            for t in range(PT):
                if t >= 2:
                    pe.wait_ge(v_out, t - 1)
                for k in range(2):
                    last = nc.tensor.matmul(ps[:, t % 2, :], cT[:, k, t * P:(t + 1) * P], wuv[:, k, :], start=k == 0, stop=k == 1)
                last.then_inc(v_done, 1)
            for k in range(2):
                nc.tensor.transpose(ps[:, 2, k * P:(k + 1) * P], cT[:, k, SEQ:TOK], C["ident"])
            nc.tensor.transpose(ps[:, 3, 0:DR], krT[64:96, SEQ:TOK], C["ident"][64:96, 64:96]).then_inc(rows_done, 1)
            for g in range(G):
                pe.wait_ge(z_done, g + 1)
                for n in range(NZ):
                    i = g * NZ + n
                    if i >= 4:
                        pe.wait_ge(zl_done, i - 3)
                    nc.tensor.matmul(ps[:, 4 + i % 4, 0:NW], wlin[:, g, :], z[:, g, n * NW:(n + 1) * NW],
                                     start=True, stop=True).then_inc(lin_done, 1)

        @block.scalar
        def _(act):
            for t in range(PT):
                act.wait_ge(v_done, t + 1)
                nc.scalar.activation(vv[:, t, :], ps[:, t % 2, :], ACT.Copy).then_inc(v_out, 1)
            act.wait_ge(rows_done, 1)
            nc.scalar.activation(rows[:, 0:KL], ps[:, 2, 0:KL], ACT.Copy).then_inc(rows_out, 1)
            nc.scalar.activation(rows[:, KL:KL + DR], ps[:, 3, 0:DR], ACT.Copy).then_inc(rows_out, 1)
            for g in range(G):
                for n in range(NZ):
                    i = g * NZ + n
                    act.wait_ge(lin_done, i + 1)
                    nc.scalar.activation(zl[:, g, n * NW:(n + 1) * NW], ps[:, 4 + i % 4, 0:NW], ACT.Copy,
                                         scale=C["pool_scale"][:, g:g + 1]).then_inc(zl_done, 1)

        @block.gpsimd
        def _(pool):
            pool.wait_ge(loaded, 96)
            for g in range(G):
                last = nc.gpsimd.tensor_copy(us4[g][:, :, STATE:], uP[:, g, PAD + SEQ:PAD + SEQ + NS].rearrange("p (b q) -> p b q", b=DB))
            last.then_inc(us_ready, 1)
            pool.wait_ge(us_ready, 1)
            step = 0
            for g in range(G):
                src, ssrc = uP[:, g, 0:PAD + SEQ], us4[g]
                for lv in range(g + 1):
                    lo, sh = (2 << lv) - 1, 1 << lv
                    dst, sdst = part[(step) % 2], uspart[(step) % 2]
                    if lv == 0 and g:
                        pool.wait_ge(z_started, g)
                    nc.gpsimd.tensor_tensor(dst[:, lo:], src[:, lo:], src[:, lo - sh:PAD + SEQ - sh], ALU.add)
                    nc.gpsimd.tensor_tensor(sdst[:, :, lo:], ssrc[:, :, lo:], ssrc[:, :, lo - sh:STATE + DQ - sh], ALU.add).then_inc(window, 1)
                    step += 1
                    pool.wait_ge(window, step)
                    src, ssrc = dst, sdst

        @block.vector
        def _(dve):
            step = 0
            for g in range(G):
                step += g + 1
                dve.wait_ge(window, step)
                s, t = part[(step - 1) % 2], uspart[(step - 1) % 2]
                width = 2 << g
                nc.vector.scalar_tensor_tensor(out=z[:, g, PAD:SEQ], in0=s[:, 2 * PAD:], scalar=1.0 / width,
                                               in1=uP[:, g, 2 * PAD:PAD + SEQ], op0=ALU.mult, op1=ALU.subtract)
                nc.vector.tensor_tensor(z[:, g, 0:PAD], s[:, PAD:2 * PAD], C["invcnt"][:, g * PAD:(g + 1) * PAD], ALU.mult)
                nc.vector.drain()
                nc.vector.tensor_tensor(z[:, g, 0:PAD], z[:, g, 0:PAD], uP[:, g, PAD:2 * PAD], ALU.subtract)
                zs = z[:, g, SEQ:SEQ + NS].rearrange("p (b q) -> p b q", b=DB)
                nc.vector.scalar_tensor_tensor(out=zs, in0=t[:, :, STATE:], scalar=1.0 / width, in1=us4[g][:, :, STATE:],
                                               op0=ALU.mult, op1=ALU.subtract).then_inc(z_started, 1)
                nc.vector.drain()
                nc.vector.tensor_copy(z[:, g, SEQ + NS:TOK], z[:, g, SEQ:SEQ + NS]).then_inc(z_done, 1)


def prompt_attention(env):
    nc, ar, C = env["nc"], env["ar"], env["C"]
    qT, kT, vv = ar.at(QT, P, H, TOK), ar.at(KT, P, H, TOK), ar.at(VV, P, PT, 512)
    w = ZL + G * TOK
    attn = ar.at(w, P, PT, 512); w += PT * 512
    qh = ar.at(w, P, SEQ); w += SEQ
    pr = ar.at(w, P, 2, SEQ); w += 2 * SEQ
    prT = ar.at(w, P, 2, SEQ); w += 2 * SEQ
    negm = ar.at(w, P, 2); w += 2
    l = ar.at(w, P, 4); w += 4
    rl = ar.at(w, P, 2); w += 2
    assert w <= AT
    attnT = ar.at(AT, P, 4, TOK)
    with ExitStack() as ctx:
        sem = env["early_sem"]
        S = ctx.enter_context(nc.psum_tensor("ps_s", [P, 2, SEQ], F32))
        PTp = ctx.enter_context(nc.psum_tensor("ps_pt", [P, SEQ], F32))
        Op = ctx.enter_context(nc.psum_tensor("ps_o", [P, 2, 512], F32))
        q_copied, s_done, max_done, exp_done, t_done, t_out, pv_done, o_out = (
            sem("c_" + n) for n in ("q_copied", "s", "max", "exp", "t", "t_out", "pv", "o_out"))
        at_done, at_out = sem("c_at_done"), sem("c_at_out")
        block = ctx.enter_context(nc.Block())

        @block.gpsimd
        def _(pool):
            with pool.Fori(0, H) as h:
                pool.wait_ge(s_done, h * PT)
                nc.gpsimd.tensor_copy(qh[0:DH, :], one(qT[0:DH, ds(h, 1), 0:SEQ])).then_inc(q_copied, 1)

        @block.tensor
        def _(pe):
            with pe.Fori(0, H) as h:
                def scores(i):
                    pe.wait_ge(q_copied, h + 1)
                    pe.wait_ge(exp_done, h * PT + max(i - 1, 0))
                    for c in range(0, (i + 1) * P, 512):
                        n = min(512, (i + 1) * P - c)
                        last = nc.tensor.matmul(S[:, i % 2, c:c + n], qh[0:DH, i * P:(i + 1) * P], one(kT[0:DH, ds(h, 1), c:c + n]),
                                                start=True, stop=True)
                    last.then_inc(s_done, 1)

                def transposed(i):
                    pe.wait_ge(exp_done, h * PT + i + 1)
                    pe.wait_ge(t_out, h * PT + i)
                    for j in range(i + 1):
                        last = nc.tensor.transpose(PTp[:, j * P:(j + 1) * P], pr[:, i % 2, j * P:(j + 1) * P], C["ident"])
                    last.then_inc(t_done, 1)

                def weighed(i):
                    pe.wait_ge(t_out, h * PT + i + 1)
                    pe.wait_ge(o_out, h * PT + max(i - 1, 0))
                    for j in range(i + 1):
                        last = nc.tensor.matmul(Op[:, i % 2, 0:DN], prT[:, i % 2, j * P:(j + 1) * P], vv[:, j, ds(h * DN, DN)],
                                                start=j == 0, stop=j == i)
                    last.then_inc(pv_done, 1)

                scores(0)
                scores(1)
                for i in range(PT):
                    transposed(i)
                    if i + 2 < PT:
                        scores(i + 2)
                    if i:
                        weighed(i - 1)
                weighed(PT - 1)
            for i in range(PT):
                if i >= 2:
                    pe.wait_ge(at_out, i - 1)
                else:
                    pe.wait_ge(o_out, H * PT)
                for k in range(4):
                    last = nc.tensor.transpose(S[:, i % 2, k * P:(k + 1) * P], attn[:, i, k * P:(k + 1) * P], C["ident"])
                last.then_inc(at_done, 1)

        @block.scalar
        def _(act):
            with act.Fori(0, H) as h:
                def exps(i):
                    act.wait_ge(max_done, h * PT + i + 1)
                    act.wait_ge(t_done, h * PT + max(i - 1, 0))
                    act.wait_ge(o_out, h * PT + max(i - 3, 0))
                    W = (i + 1) * P
                    nc.scalar.activation(pr[:, i % 2, 0:W], S[:, i % 2, 0:W], ACT.Exp, bias=negm[:, i % 2:i % 2 + 1],
                                         accum_out=l[:, i % 4:i % 4 + 1]).then_inc(exp_done, 1)

                exps(0)
                for i in range(PT):
                    if i + 1 < PT:
                        exps(i + 1)
                    act.wait_ge(t_done, h * PT + i + 1)
                    act.wait_ge(pv_done, h * PT + max(i - 1, 0))
                    nc.scalar.activation(prT[:, i % 2, 0:(i + 1) * P], PTp[:, 0:(i + 1) * P], ACT.Copy).then_inc(t_out, 1)
            for i in range(PT):
                act.wait_ge(at_done, i + 1)
                nc.scalar.activation(attnT[:, :, i * P:(i + 1) * P], S[:, i % 2, 0:512].rearrange("p (k t) -> p k t", k=4),
                                     ACT.Copy).then_inc(at_out, 1)

        @block.vector
        def _(dve):
            with dve.Fori(0, H) as h:
                def maxima(i):
                    dve.wait_ge(s_done, h * PT + i + 1)
                    W = (i + 1) * P
                    nc.vector.tensor_tensor(S[:, i % 2, W - P:W], S[:, i % 2, W - P:W], C["causal"], ALU.add)
                    nc.vector.drain()
                    nc.vector.tensor_reduce(out=negm[:, i % 2:i % 2 + 1], in_=S[:, i % 2, 0:W], axis=AX, op=ALU.max,
                                            negate=True).then_inc(max_done, 1)

                def finished(i):
                    dve.wait_ge(pv_done, h * PT + i + 1)
                    nc.vector.reciprocal(rl[:, i % 2:i % 2 + 1], l[:, i % 4:i % 4 + 1])
                    nc.vector.drain()
                    nc.vector.tensor_scalar(attn[:, i, ds(h * DN, DN)], Op[:, i % 2, 0:DN], rl[:, i % 2:i % 2 + 1], None, ALU.mult).then_inc(o_out, 1)

                maxima(0)
                for i in range(PT):
                    if i + 1 < PT:
                        maxima(i + 1)
                    if i:
                        finished(i - 1)
                finished(PT - 1)


def sample_queries(env, prompt):
    nc, I, ar, C = env["nc"], env["I"], env["ar"], env["C"]
    qT, zl = ar.at(QT, P, H, TOK), ar.at(ZL, P, G, TOK)
    wukT = ar.at(VV, P, H, KL)
    qlat0, qrope0 = ar.at(VV + H * KL, P, 2, H * NS), ar.at(VV + H * KL + 2 * H * NS, P, H * NS)
    assert VV + H * KL + 3 * H * NS <= ZL
    qlat, qrope, zls = ar.at(QLAT, P, 2 * H * NS), ar.at(QROPE, P, H * NS), ar.at(ZLS, P, G, P)

    def by_batch(ap, h):
        return ap.rearrange("p (b h q) -> p h b q", b=DB, h=H)[:, h, :, :]

    with ExitStack() as ctx:
        sem = lambda n: ctx.enter_context(nc.semaphore(n))
        ps = ctx.enter_context(nc.psum_tensor("ps_q", [P, 2, 512], F32))
        loaded, ql_done, ql_out, qr_done, shifted = (sem("q_" + n) for n in ("loaded", "ql", "ql_out", "qr", "shifted"))
        block = ctx.enter_context(nc.Block())

        @block.sync
        def _(sp):
            sp.dma_start(wukT[0:DN], I["w_ukT"]).then_inc(loaded, 16)
            prompt.load_merge(sp)
            sp.wait_ge(qr_done, 1)
            sp.wait_ge(ql_done, 1)
            sp.dma_start(qrope[0:DR, :], qrope0[64:96, :]).then_inc(shifted, 16)
            sp.wait_ge(shifted, 16)

        @block.tensor
        def _(pe):
            pe.wait_ge(loaded, 16)
            for h in range(H):
                for k in range(2):
                    last = nc.tensor.matmul(ps[:, k, h * NS:(h + 1) * NS], wukT[0:DN, h, k * P:(k + 1) * P], qT[0:DN, h, SEQ:SEQ + NS],
                                            start=True, stop=True)
            last.then_inc(ql_done, 1)

        @block.vector
        def _(dve):
            for h in range(H):
                last = nc.vector.tensor_copy(by_batch(qrope0, h)[64:96], qT[64:96, h, SEQ:SEQ + NS].rearrange("p (b q) -> p b q", b=DB))
            last.then_inc(qr_done, 1)

        @block.scalar
        def _(act):
            act.wait_ge(ql_done, 1)
            for k in range(2):
                for h in range(H):
                    last = nc.scalar.activation(by_batch(qlat0[:, k, :], h),
                                                ps[:, k, h * NS:(h + 1) * NS].rearrange("p (b q) -> p b q", b=DB), ACT.Copy)
            act.wait_ge(qr_done, 1)
            nc.scalar.drain()
            nc.scalar.activation(qlat, qlat0.rearrange("p a b -> p (a b)"), ACT.Copy)
            nc.scalar.activation(zls, zl[:, :, SEQ:TOK], ACT.Copy)


class Part:

    def __init__(self, env, tag, first, tiles, width, attnT, zl, x_free, sem):
        ar, self.env = env["ar"], env
        self.tag, self.first, self.tiles, self.width, self.x_free = tag, first, tiles, width, x_free
        self.cols = tiles * P
        self.steps = self.cols // width
        self.attnT, self.zl = attnT, zl
        self.mixed, self.xn2T = ar.at(MT, P, KD, self.cols), ar.at(XN2T, P, KD, self.cols)
        self.xnT, self.ring = ar.at(XNT, P, KD, self.cols), [ar.at(MERGE_RING + s * 24 * P, P, 24, P) for s in range(2)]
        self.xn_in, self.w_in, self.w_out_in = sem("e_xn_in" + tag), [sem(f"e_w_in{s}" + tag) for s in range(2)], sem("e_w_out_in" + tag)

    def load_merge(self, sp):
        cols = slice(self.first * P, self.first * P + self.cols)
        sp.dma_start(self.xnT, self.env["xn_dram"][:, :, cols]).then_inc(self.xn_in, 16)
        for s in range(2):
            sp.dma_start(self.ring[s], self.env["I"]["w_merge"][s]).then_inc(self.w_in[s], 16)


def merge(env, part):
    nc, I, ar = env["nc"], env["I"], env["ar"]
    zl, attnT, mixed = part.zl, part.attnT, part.mixed
    W, N = part.width, part.steps
    ring, xnT, w_in = part.ring, part.xnT, part.w_in
    w = MERGE_RING + 48 * P
    sig = ar.at(w, P, 4, W); w += 4 * W
    assert w <= AT
    prod = ar.at(MT - 4 * W, P, 4, W)
    assert MT - 4 * W >= AT + 4 * TOK
    with ExitStack() as ctx:
        sem = lambda n: ctx.enter_context(nc.semaphore("e_" + n + part.tag))
        ps = ctx.enter_context(nc.psum_tensor("ps_e" + part.tag, [P, 8, 512], F32))
        gate_done, branch_done, sig_done, mix_done = (sem(n) for n in ("gate", "branch", "sig", "mix"))
        block = ctx.enter_context(nc.Block())

        @block.sync
        def _(sp):
            sp.dma_start(ar.at(WOUT, P, WOUT_AHEAD, D), I["w_out"][:, 0:WOUT_AHEAD, :]).then_inc(part.w_out_in, 16)
            with sp.Fori(0, KD // 2 - 1) as dd:
                for s in range(2):
                    sp.wait_ge(branch_done, dd * 2 * N + N * (s + 1))
                    sp.dma_start(ring[s], I["w_merge"][ds(dd * 2 + 2 + s, 1)].rearrange("a p k c -> (a p) k c")).then_inc(w_in[s], 16)

        @block.tensor
        def _(pe):
            pe.wait_ge(part.xn_in, 16)
            with pe.Fori(0, KD // 2) as dd:
                for s in range(2):
                    pe.wait_ge(w_in[s], dd * 16 + 16)
                    for n in range(N):
                        i = s * N + n
                        c = slice(n * W, (n + 1) * W)
                        B = 4 * (i % 2)
                        pe.wait_ge(mix_done, dd * 2 * N + i + 1)
                        for a in range(2):
                            for k in range(KD):
                                last = nc.tensor.matmul(ps[:, B + a, 0:W], ring[s][:, a * KD + k, :], xnT[:, k, c], start=k == 0, stop=k == KD - 1)
                        last.then_inc(gate_done, 1)
                        for a, src in enumerate((attnT, zl)):
                            for k in range(4):
                                last = nc.tensor.matmul(ps[:, B + 2 + a, 0:W], ring[s][:, 16 + 4 * a + k, :], src[:, k, c], start=k == 0, stop=k == 3)
                        last.then_inc(branch_done, 1)

        @block.scalar
        def _(act):
            with act.Fori(0, KD // 2) as dd:
                for i in range(2 * N):
                    act.wait_ge(gate_done, dd * 2 * N + i + 1)
                    act.wait_ge(mix_done, dd * 2 * N + i + 1)
                    nc.scalar.activation(sig[:, 2 * (i % 2):2 * (i % 2) + 2, :], ps[:, 4 * (i % 2):4 * (i % 2) + 2, 0:W],
                                         ACT.Sigmoid).then_inc(sig_done, 1)

        @block.vector
        def _(dve):
            nc.vector.drain().then_inc(mix_done, 2)
            with dve.Fori(0, KD // 2) as dd:
                for i in range(2 * N):
                    s, n, h = i // N, i % N, 2 * (i % 2)
                    dve.wait_ge(sig_done, dd * 2 * N + i + 1)
                    dve.wait_ge(branch_done, dd * 2 * N + i + 1)
                    nc.vector.tensor_tensor(prod[:, h:h + 2, :], sig[:, h:h + 2, :], ps[:, 2 * h + 2:2 * h + 4, 0:W], ALU.mult)
                    nc.vector.drain()
                    nc.vector.tensor_tensor(one(mixed[:, ds(dd * 2 + s, 1), n * W:(n + 1) * W]), prod[:, h, :], prod[:, h + 1, :],
                                            ALU.add).then_inc(mix_done, 1)


def residual(env, part):
    nc, I, ar, C = env["nc"], env["I"], env["ar"], env["C"]
    mixed, xn2T = part.mixed, part.xn2T
    yall, xn2 = ar.at(YALL, P, NT, D), ar.at(XN2, P, NT, D)
    T, T0 = part.tiles, part.first
    w = XNT
    rest = ar.at(w, P, KD - WOUT_AHEAD, D); w += (KD - WOUT_AHEAD) * D
    wout = [ar.at(WOUT + k * D, P, D) for k in range(WOUT_AHEAD)] + [rest[:, k, :] for k in range(KD - WOUT_AHEAD)]
    mt = [ar.at(w + s * D, P, KD, P) for s in range(2)]; w += 2 * D
    xt = [ar.at(a, P, D) for a in part.x_free]
    w2 = ar.at(w, P, D); w += D
    xn = ar.at(w, P, D); w += D
    st = ar.at(w, P, 2); w += 2
    assert w <= WOUT
    with ExitStack() as ctx:
        sem = lambda n: ctx.enter_context(nc.semaphore("f_" + n + part.tag))
        ps = ctx.enter_context(nc.psum_tensor("ps_f" + part.tag, [P, 8, 512], F32))
        loaded, x_in = sem("loaded"), [sem(f"x_in{s}") for s in range(2)]
        m_copied, h_done, h_out, std_done, xn_done, t_done, t_out = (
            sem(n) for n in ("m_copied", "h", "h_out", "std", "xn", "t", "t_out"))
        block = ctx.enter_context(nc.Block())

        def ahead(eng, get):
            for s in range(min(2, T)):
                get(s, s, 0)
            if T > 2:
                with eng.Fori(0, T // 2 - 1) as tt:
                    for s in range(2):
                        get(tt * 2 + 2 + s, s, tt + 1)

        def each(eng, body):
            if T == 1:
                return body(0, 0, 0)
            with eng.Fori(0, T // 2) as tt:
                for s in range(2):
                    body(tt * 2 + s, s, tt)

        @block.sync
        def _(sp):
            sp.dma_start(rest, I["w_out"][:, WOUT_AHEAD:, :]).then_inc(loaded, 16)
            sp.dma_start(w2, I["norm2"]).then_inc(loaded, 16)

            def get(t, s, i):
                if not isinstance(t, int):
                    sp.wait_ge(h_out, t - 1)
                sp.dma_start(xt[s], I["x_tok"][ds(t + T0, 1)].rearrange("a p c -> (a p) c")).then_inc(x_in[s], 16)

            ahead(sp, get)
            if T0:
                sp.dma_start(env["O"]["y_prompt"].rearrange("(t p) d -> p t d", p=P), yall[:, 0:PT, :]).then_inc(env["y_stored"], 16)

        @block.gpsimd
        def _(pool):
            def get(t, s, i):
                if not isinstance(t, int):
                    pool.wait_ge(h_done, t - 1)
                nc.gpsimd.tensor_copy(mt[s], mixed[:, :, ds(t * P, P)]).then_inc(m_copied, 1)

            ahead(pool, get)

        @block.tensor
        def _(pe):
            def product(t, s):
                pe.wait_ge(m_copied, t + 1)
                if not isinstance(t, int) or t >= 2:
                    pe.wait_ge(h_out, t - 1)
                for c in range(2):
                    for k in range(KD):
                        if isinstance(t, int) and t == 0 and c == 0 and k == WOUT_AHEAD:
                            pe.wait_ge(loaded, 32)
                        last = nc.tensor.matmul(ps[:, 2 * s + c, :], mt[s][:, k, :], wout[k][:, c * 512:(c + 1) * 512], start=k == 0, stop=k == KD - 1)
                last.then_inc(h_done, 1)

            def transposed(t):
                pe.wait_ge(xn_done, t + 1)
                pe.wait_ge(t_out, t)
                for k in range(KD):
                    last = nc.tensor.transpose(ps[:, 4 + k // 4, (k % 4) * P:(k % 4 + 1) * P], xn[:, k * P:(k + 1) * P], C["ident"])
                last.then_inc(t_done, 1)

            pe.wait_ge(part.w_out_in, 16)
            product(0, 0)
            if T > 1:
                with pe.Fori(0, T // 2 - 1) as tt:
                    product(tt * 2 + 1, 1)
                    transposed(tt * 2)
                    product(tt * 2 + 2, 0)
                    transposed(tt * 2 + 1)
                product(T - 1, 1)
                transposed(T - 2)
            transposed(T - 1)

        @block.scalar
        def _(act):
            def body(t, s, i):
                act.wait_ge(h_out, t + 1)
                act.wait_ge(t_done, t)
                nc.scalar.activation(xn, one(yall[:, ds(t + T0, 1), :]), ACT.Square, accum_out=st[:, 0:1])
                nc.scalar.drain()
                nc.scalar.activation(st[:, 1:2], st[:, 0:1], ACT.Sqrt, bias=C["eps"], scale=1.0 / D).then_inc(std_done, 1)
                act.wait_ge(xn_done, t + 1)
                nc.scalar.activation(one(xn2[:, ds(t + T0, 1), :]), xn, ACT.Copy)
                act.wait_ge(t_done, t + 1)
                nc.scalar.activation(xn2T[:, :, ds(t * P, P)], ps[:, 4:6, :].rearrange("p a (b c) -> p (a b) c", b=4), ACT.Copy).then_inc(t_out, 1)
                nc.scalar.drain()

            each(act, body)

        @block.vector
        def _(dve):
            dve.wait_ge(loaded, 32)

            def body(t, s, i):
                y = one(yall[:, ds(t + T0, 1), :])
                dve.wait_ge(h_done, t + 1)
                dve.wait_ge(x_in[s], i * 16 + 16)
                nc.vector.tensor_tensor(y, ps[:, 2 * s:2 * s + 2, :].rearrange("p a b -> p (a b)"), xt[s], ALU.add).then_inc(h_out, 1)
                dve.wait_ge(std_done, t + 1)
                nc.vector.reciprocal(st[:, 1:2], st[:, 1:2])
                nc.vector.drain()
                nc.vector.scalar_tensor_tensor(out=xn, in0=y, scalar=st[:, 1:2], in1=w2, op0=ALU.mult, op1=ALU.mult).then_inc(xn_done, 1)

            each(dve, body)
            if T0:
                nc.vector.drain()
                nc.vector.memset(yall[NS:P, NT - 1, :], 0.0)


def peer_scores(env, part, rt):
    part.rt = rt
    r0 = part.first * H
    nc, I, ar = env["nc"], env["I"], env["ar"]
    xn2T = part.xn2T
    W, N, T = part.width, part.steps, part.tiles
    TW = W // P
    w = XN2T + KD * SEQ
    ring = [ar.at(w + s * 9 * P, P, 9, P) for s in range(2)]; w += 18 * P
    qb = [ar.at(w + s * part.cols, P, part.cols) for s in range(2)]; w += 2 * part.cols
    out = ar.at(w, P, T, 2, NK); w += T * 2 * NK
    assert w <= ROUTE_AT
    by_head = env["s_dram"][:, part.first * H:(part.first + T) * H, :].rearrange("p (t h) c -> p t h c", t=T)
    with ExitStack() as ctx:
        sem = lambda n: ctx.enter_context(nc.semaphore("g_" + n + part.tag))
        pq = ctx.enter_context(nc.psum_tensor("ps_g" + part.tag, [P, 4, 512], F32))
        pk = ctx.enter_context(nc.psum_tensor("ps_g2" + part.tag, [P, 4, 512], F32))
        w_in = [sem(f"w_in{s}") for s in range(2)]
        q_done, q_out, k_done, k_out, stored = (sem(n) for n in ("q", "q_out", "k", "k_out", "stored"))
        block = ctx.enter_context(nc.Block())

        @block.sync
        def _(sp):
            def store(h):
                sp.wait_ge(k_out, h * 2 * N + 2 * N)
                if T == 1:
                    dst, src = by_head[:, 0, ds(h, 1), :].rearrange("p a c -> p (a c)"), out.rearrange("p t s k -> p (t s k)")
                else:
                    dst, src = by_head[:, :, ds(h, 1), :].rearrange("p t a c -> p t (a c)"), out.rearrange("p t s k -> p t (s k)")
                sp.dma_start(dst, src).then_inc(stored, 16)

            for s in range(2):
                sp.dma_start(ring[s], I["w_peer"][s]).then_inc(w_in[s], 16)

            def head(h):
                for s in range(2):
                    sp.wait_ge(k_done, h * 2 * N + N * (s + 1))
                    sp.dma_start(ring[s], I["w_peer"][ds(h * 2 + 2 + s, 1)].rearrange("a p k c -> (a p) k c")).then_inc(w_in[s], 16)
                store(h)

            with sp.Fori(0, EARLY_AT) as h:
                head(h)
            for c in range(EARLY):
                head(EARLY_AT + c)
                if c < rt.early:
                    sp.wait_ge(stored, (EARLY_AT + c + 1) * 16)
                    rt.load(sp, c, r0 + c, env["s_dram"])
            store(H - 1)
            sp.wait_ge(stored, H * 16)

        @block.tensor
        def _(pe):
            with pe.Fori(0, H) as h:
                for s in range(2):
                    pe.wait_ge(w_in[s], h * 16 + 16)
                    for n in range(N):
                        for k in range(KD):
                            last = nc.tensor.matmul(pq[:, s * N + n, 0:W], ring[s][:, k, :], xn2T[:, k, n * W:(n + 1) * W], start=k == 0, stop=k == KD - 1)
                        last.then_inc(q_done, 1)
                    for n in range(N):
                        pe.wait_ge(q_out, h * 2 * N + s * N + n + 1)
                        pe.wait_ge(k_out, h * 2 * N)
                        for t in range(TW):
                            last = nc.tensor.matmul(pk[:, s * N + n, t * P:(t + 1) * P], qb[s][:, (TW * n + t) * P:(TW * n + t + 1) * P], ring[s][:, 8, :],
                                                    start=True, stop=True)
                        last.then_inc(k_done, 1)

        @block.scalar
        def _(act):
            def head(h, c=None):
                for i in range(2 * N):
                    act.wait_ge(q_done, h * 2 * N + i + 1)
                    act.wait_ge(k_done, h * 2 * N)
                    nc.scalar.activation(qb[i // N][:, (i % N) * W:(i % N + 1) * W], pq[:, i, 0:W], ACT.Copy).then_inc(q_out, 1)
                    if i == 2 * N - 1 and c is not None:
                        rt.softmax(act, c)

            with act.Fori(0, EARLY_AT + 1) as h:
                head(h)
            for c in range(EARLY):
                head(EARLY_AT + 1 + c, c if c < rt.early else None)

        @block.vector
        def _(dve):
            def head(h):
                for i in range(2 * N):
                    s, n = i // N, i % N
                    dve.wait_ge(k_done, h * 2 * N + i + 1)
                    dve.wait_ge(stored, h * 16)
                    nc.vector.tensor_copy(out[:, n * TW:(n + 1) * TW, s, :], pk[:, i, 0:W].rearrange("p (t k) -> p t k", t=TW)).then_inc(k_out, 1)

            with dve.Fori(0, EARLY_AT) as h:
                head(h)
            for c in range(EARLY):
                head(EARLY_AT + c)
                if c < rt.early:
                    rt.find(dve, c, r0 + c)
            head(H - 1)


def sample_output(env, sample):
    nc, I, ar = env["nc"], env["I"], env["ar"]
    latT, attnT = ar.at(LATT, P, 2, H * NS), ar.at(ATS, P, 4, P)
    wuv = ar.at(AT - 2 * 512, P, 2, 512)
    with ExitStack() as ctx:
        sem = lambda n: ctx.enter_context(nc.semaphore("o_" + n))
        ps = ctx.enter_context(nc.psum_tensor("ps_uv", [P, 4, 512], F32))
        loaded, done = sem("loaded"), sem("done")
        block = ctx.enter_context(nc.Block())

        @block.sync
        def _(sp):
            sp.dma_start(wuv, I["w_uv"]).then_inc(loaded, 16)
            sample.load_merge(sp)

        @block.tensor
        def _(pe):
            pe.wait_ge(loaded, 16)
            for h in range(H):
                o = (h % 2) * DN
                for k in range(2):
                    last = nc.tensor.matmul(ps[o:o + DN, h // 2, 0:NS], wuv[:, k, h * DN:(h + 1) * DN], latT[:, k, h * NS:(h + 1) * NS],
                                            start=k == 0, stop=k == 1)
            last.then_inc(done, 1)

        @block.scalar
        def _(act):
            act.wait_ge(done, 1)
            for r in range(2):
                nc.scalar.activation(attnT[:, :, r * NS:(r + 1) * NS], ps[:, :, 0:NS], ACT.Copy)


class Route:

    def __init__(self, env, sem, by_halves):
        w = ROUTE_AT
        self.by_halves, self.unit = by_halves, 32 if by_halves else 16
        self.early = 1 if by_halves else EARLY
        self.nc, self.C, self.ids, self.gates, ar = env["nc"], env["C"], env["ids"], env["gates"], env["ar"]

        def take(*dims):
            nonlocal w
            n = 1
            for d in dims:
                n *= d
            w += n
            return ar.at(w - n, P, *dims)

        self.s, self.s2 = take(2, NK), take(2, NK)
        self.top, self.topi, self.topf = take(2, TOPK), take(2, TOPK).bitcast(U32), take(2, TOPK)
        self.cand, self.best, self.pos = take(TOPK, TOPK), take(TOPK), take(TOPK).bitcast(U32)
        self.hilo, self.hilof, self.hit = take(2, TOPK).bitcast(U32), take(2, TOPK), take(2 * TOPK, TOPK)
        self.e2, self.ef, self.ex = take(2, TOPK), take(TOPK), take(TOPK)
        self.negb, self.sm = take(1), take(1)
        self.end = w
        self.s_in, self.s_used, self.b_done, self.e_done, self.done = (sem("h_" + n) for n in ("s_in", "s_used", "best", "exp", "done"))

    def load(self, sp, c, r, src):
        sp.wait_ge(self.s_used, c)
        if self.by_halves:
            for rows, head in ((slice(0, NS), r), (slice(NS, P), r + H // 2)):
                sp.dma_start(self.s[rows].rearrange("p a b -> p (a b)"), one(src[rows, ds(head, 1), :])).then_inc(self.s_in, 16)
        else:
            sp.dma_start(self.s.rearrange("p a b -> p (a b)"), one(src[:, ds(r, 1), :])).then_inc(self.s_in, 16)

    def softmax(self, act, c):
        act.wait_ge(self.b_done, c + 1)
        act.wait_ge(self.done, c)
        self.nc.scalar.activation(self.ex, self.best, ACT.Exp, bias=self.negb, accum_out=self.sm).then_inc(self.e_done, 1)

    def find(self, dve, c, r):
        self.top_eight(dve, c)
        self.top_sixteen()
        self.pairs()
        self.experts(dve, c, r)

    def top_eight(self, dve, c):
        v = self.nc.vector
        wait_apart(dve, self.s_in, c * self.unit + self.unit, (self.s_in, self.unit))
        for p in range(2):
            v.max(out=self.top[:, p, 0:8], in_=self.s[:, p, :])
        v.drain()
        for p in range(2):
            v.max_index(out=self.topi[:, p, 0:8], in_max=self.top[:, p, 0:8], in_values=self.s[:, p, :])
            v.match_replace(out=self.s2[:, p, :], in_to_replace=self.top[:, p, 0:8], in_values=self.s[:, p, :], imm_value=LOWEST)
        v.drain().then_inc(self.s_used, 1)

    def top_sixteen(self):
        v = self.nc.vector
        for p in range(2):
            v.max(out=self.top[:, p, 8:16], in_=self.s2[:, p, :])
        v.drain()
        for p in range(2):
            v.max_index(out=self.topi[:, p, 8:16], in_max=self.top[:, p, 8:16], in_values=self.s2[:, p, :])
        v.tensor_tensor(self.cand, self.top[:, 0, :].unsqueeze(2).to_broadcast([P, TOPK, TOPK]),
                        self.top[:, 1, :].unsqueeze(1).to_broadcast([P, TOPK, TOPK]), ALU.add)
        v.drain()

    def pairs(self):
        v = self.nc.vector
        candf, cand2 = self.cand.rearrange("p a b -> p (a b)"), self.s2.rearrange("p a b -> p (a b)")
        v.tensor_copy(self.topf, self.topi)
        v.max(out=self.best[:, 0:8], in_=candf)
        v.drain()
        v.tensor_scalar(self.topf[:, 0, :], self.topf[:, 0, :], float(NK), None, ALU.mult)
        v.max_index(out=self.pos[:, 0:8], in_max=self.best[:, 0:8], in_values=candf)
        v.match_replace(out=cand2, in_to_replace=self.best[:, 0:8], in_values=candf, imm_value=LOWEST)
        v.tensor_scalar(self.negb, self.best[:, 0:1], -1.0, None, ALU.mult)
        v.drain()
        v.max(out=self.best[:, 8:16], in_=cand2)
        v.drain().then_inc(self.b_done, 1)
        v.max_index(out=self.pos[:, 8:16], in_max=self.best[:, 8:16], in_values=cand2)
        v.drain()

    def experts(self, dve, c, r):
        v = self.nc.vector
        v.tensor_scalar(self.hilo[:, 0, :], self.pos, 4, None, ALU.logical_shift_right)
        v.tensor_scalar(self.hilo[:, 1, :], self.pos, TOPK - 1, None, ALU.bitwise_and)
        v.drain()
        v.tensor_copy(self.hilof, self.hilo)
        v.drain()
        v.tensor_tensor(self.hit, self.hilof.rearrange("p a b -> p (a b)").unsqueeze(2).to_broadcast([P, 2 * TOPK, TOPK]),
                        self.C["iota16"].unsqueeze(1).to_broadcast([P, 2 * TOPK, TOPK]), ALU.is_equal)
        v.drain()
        h4 = self.hit.rearrange("p (a b) c -> p a b c", a=2)
        v.tensor_tensor(h4, h4, self.topf.unsqueeze(2).to_broadcast([P, 2, TOPK, TOPK]), ALU.mult)
        v.drain()
        v.tensor_reduce(out=self.e2, in_=h4, axis=AX, op=ALU.add)
        v.drain()
        v.tensor_tensor(self.ef, self.e2[:, 0, :], self.e2[:, 1, :], ALU.add)
        v.drain()
        v.tensor_copy(self.ids[:, ds(r * TOPK, TOPK)], self.ef)
        dve.wait_ge(self.e_done, c + 1)
        v.reciprocal(self.sm, self.sm)
        v.drain()
        v.tensor_scalar(self.gates[:, ds(r * TOPK, TOPK)], self.ex, self.sm, None, ALU.mult)
        v.drain().then_inc(self.done, 1)


class Pages:

    PPB = NPAGES + 1

    def __init__(self, env, w, sem, ps):
        self.nc, self.I, self.C, self.env, ar = env["nc"], env["I"], env["C"], env, env["ar"]

        def take(parts, *dims):
            nonlocal w
            n = 1
            for d in dims:
                n *= d
            w += n
            return ar.at(w - n, parts, *dims)

        self.pages, self.new_page, self.wuk = [take(P, GP, PGW) for _ in range(2)], take(P, PGW), take(P, 2, 512)
        self.cTp, self.sqp = take(P, 2, KL + P), take(P, 2, 512)
        self.krsq, self.sskr, self.ssn, self.rk = take(P, GP + 1, DR), take(P, GP + 1), take(P, GP + 1, H), take(P, GP + 1, H)
        self.sc, self.pmax = take(P, GP + 1, NS), take(P, NS)
        self.prob = self.sc
        small = take(NS, 8)
        self.m, self.mnew, self.negm, self.corr, self.gmax, self.rl = (small[:, j:j + 1] for j in range(6))
        self.diag, self.acc, self.lat = take(NS, NS), take(NS, KL + 1), take(NS, KL)
        self.end = w
        self.qlat, self.qrope = ar.at(QLAT, P, 2, H * NS), ar.at(QROPE, P, H * NS)
        self.latT = ar.at(LATT, P, 2, H * NS)
        self.tp, self.key, self.small_ps, self.acc_ps = (ps[:, j, :] for j in range(4))
        s0 = (GP + 1) * NS
        self.maxT, self.spread = self.small_ps[0:NS, s0:s0 + P], self.small_ps[:, s0 + P:s0 + P + NS]
        assert s0 + P + NS <= 512
        self.loaded, self.new_in, self.zeroed = sem("d_loaded"), sem("d_new_in"), sem("d_zeroed")
        self.page_in = [sem(f"d_page_in{par}") for par in range(2)]
        (self.t_done, self.t_out, self.key_done, self.s_done, self.ksq_done, self.ks_done, self.kr_sq, self.norm_in, self.norm_root,
         self.scaled, self.pm_done, self.pmT_done, self.m_done, self.corr_done, self.mb_done, self.shift_done, self.exp_done,
         self.pv_done, self.acc_out, self.lat_done, self.latT_done, self.latT_out) = (sem("d_" + n) for n in (
             "t_done", "t_out", "key", "s", "ksq", "ks", "kr_sq", "norm_in", "norm_root", "scaled", "pm", "pmT", "m", "corr",
             "mb", "sub", "exp", "pv", "acc_out", "lat", "latT", "latT_out"))

    def load_first(self, sp):
        sp.dma_start(self.env["table"][:, :], self.I["page_table"]).then_inc(self.loaded, 16)
        sp.dma_start(self.wuk, self.I["w_uk"]).then_inc(self.loaded, 16)
        sp.wait_ge(self.loaded, 32)
        sp.wait_ge(self.zeroed, 1)

    def load_new(self, sp, b):
        sp.wait_ge(self.pv_done, b * GROUPS + 1)
        rows = self.env["new_rows"]
        sp.dma_start(self.new_page[0:DQ, 0:KL], rows[ds(b * DQ, DQ), 0:KL]).then_inc(self.new_in, 16)
        sp.dma_start(self.new_page[0:DQ, KL + 1:PGW], rows[ds(b * DQ, DQ), KL:KL + DR]).then_inc(self.new_in, 16)

    def load_group(self, sp, b, g, par):
        sp.wait_ge(self.pv_done, b * GROUPS + g)
        for j in range(GP):
            page = sp.value_load(self.env["table"][0:1, ds(b * NPAGES + g * GP + j, 1)], min_val=0, max_val=NPHYS - 1)
            for cols, src in ((slice(0, KL), "cache_ckv"), (slice(KL + 1, PGW), "cache_krope")):
                sp.dma_start(self.pages[par][:, j, cols], self.I[src][ds(page, 1)].rearrange("a p c -> (a p) c")).then_inc(self.page_in[par], 16)

    def clear(self):
        g = self.nc.gpsimd
        g.memset(self.new_page, 0.0)
        g.drain()
        g.memset(self.new_page[:, KL:KL + 1], 1.0)
        for par in range(2):
            for j in range(GP):
                g.memset(self.pages[par][:, j, KL:KL + 1], 1.0)
        g.drain().then_inc(self.zeroed, 1)

    def source(self, j, par):
        return self.pages[par][:, j, :] if j < GP else self.new_page

    def transposes(self, pe, j, at, par):
        t, src = self.nc.tensor, self.source(j, par)
        pe.wait_ge(self.t_out, at + j)
        for k in range(2):
            t.transpose(self.tp[:, k * P:(k + 1) * P], src[:, k * P:(k + 1) * P], self.C["ident"])
        t.transpose(self.tp[0:DR, KL:KL + P], src[:, KL + 1:PGW], self.C["ident"]).then_inc(self.t_done, 1)

    def keys(self, pe, j, at, gi, b):
        t = self.nc.tensor
        pe.wait_ge(self.t_out, at + j + 1)
        pe.wait_ge(self.ksq_done, at + j)
        for k in range(2):
            last = t.matmul(self.key, self.cTp[:, j % 2, k * P:(k + 1) * P], self.wuk[:, k, :], start=k == 0, stop=k == 1)
        last.then_inc(self.key_done, 1)
        if j == 0:
            pe.wait_ge(self.scaled, gi)
            pe.wait_ge(self.shift_done, gi)
        out = self.small_ps[:, j * NS:(j + 1) * NS]
        for k in range(2):
            t.matmul(out, self.cTp[:, j % 2, k * P:(k + 1) * P], self.qlat[:, k, ds(b * NS, NS)], start=k == 0, stop=False)
        t.matmul(out, self.cTp[0:DR, j % 2, KL:KL + P], self.qrope[0:DR, ds(b * NS, NS)], start=False, stop=True).then_inc(self.s_done, 1)

    def maxima(self, pe, gi):
        wait_apart(pe, self.pm_done, gi + 1, (self.loaded, 32))
        self.nc.tensor.transpose(self.maxT, self.pmax, self.C["ident"]).then_inc(self.pmT_done, 1)

    def spread_maxima(self, pe, gi):
        pe.wait_ge(self.m_done, gi + 1)
        self.nc.tensor.matmul(self.spread, self.C["ones"][0:NS, :], self.diag, start=True, stop=True).then_inc(self.mb_done, 1)

    def weigh(self, pe, n, gi, par):
        pe.wait_ge(self.exp_done, gi + 1)
        pe.wait_ge(self.acc_out, gi)
        for j in range(n):
            last = self.nc.tensor.matmul(self.acc_ps[0:NS, 0:KL + 1], self.prob[:, j, :], self.source(j, par)[:, 0:KL + 1], start=j == 0, stop=j == n - 1)
        last.then_inc(self.pv_done, 1)

    def group_arrived(self, pe, b, g, n, par):
        pe.wait_ge(self.page_in[par], ((b * GROUPS + g) // 2) * (32 * GP) + 32 * GP)
        if n > GP:
            pe.wait_ge(self.new_in, b * 32 + 32)

    def result(self, pe, b):
        wait_apart(pe, self.latT_out, b, (self.loaded, 32))
        wait_apart(pe, self.lat_done, b + 1, (self.loaded, 32))
        for k in range(2):
            last = self.nc.tensor.transpose(self.acc_ps[:, 320 + k * NS:320 + (k + 1) * NS], self.lat[:, k * P:(k + 1) * P], self.C["ident"][0:NS, 0:NS])
        last.then_inc(self.latT_done, 1)

    def copy_page(self, act, j, at):
        s = self.nc.scalar
        act.wait_ge(self.t_done, at + j + 1)
        act.wait_ge(self.s_done, at + max(j - 1, 0))
        s.activation(self.cTp[:, j % 2, 0:KL], self.tp[:, 0:KL], ACT.Copy)
        s.activation(self.cTp[0:DR, j % 2, KL:], self.tp[0:DR, KL:KL + P], ACT.Copy)
        s.drain().then_inc(self.t_out, 1)

    def square(self, act, j, at):
        act.wait_ge(self.key_done, at + j + 1)
        act.wait_ge(self.ks_done, at + max(j - 1, 0))
        self.nc.scalar.activation(self.sqp[:, j % 2, :], self.key, ACT.Square).then_inc(self.ksq_done, 1)

    def square_rope(self, act, n, gi, par):
        act.wait_ge(self.norm_in, gi)
        if n > GP:
            self.nc.scalar.activation(self.krsq[:, GP, :], self.new_page[:, KL + 1:PGW], ACT.Square)
        self.nc.scalar.activation(self.krsq[:, 0:GP, :], self.pages[par][:, :, KL + 1:PGW], ACT.Square)
        self.nc.scalar.drain().then_inc(self.kr_sq, 1)

    def root(self, act, n, gi):
        act.wait_ge(self.norm_in, gi + 1)
        self.nc.scalar.activation(self.rk[:, 0:n, :], self.rk[:, 0:n, :], ACT.Sqrt, bias=self.C["eps"], scale=1.0 / DH).then_inc(self.norm_root, 1)

    def correct(self, act, gi):
        act.wait_ge(self.m_done, gi + 1)
        self.nc.scalar.activation(self.corr, self.m, ACT.Exp, bias=self.negm).then_inc(self.corr_done, 1)

    def exponentials(self, act, n, gi):
        act.wait_ge(self.shift_done, gi + 1)
        self.nc.scalar.activation(self.prob[:, 0:n, :], self.sc[:, 0:n, :], ACT.Exp).then_inc(self.exp_done, 1)

    def copy_result(self, act, b):
        act.wait_ge(self.latT_done, b + 1)
        for k in range(2):
            dst = self.latT[:, k, :].rearrange("p (h t) -> p h t", h=H)[:, :, ds(b * DQ, DQ)]
            self.nc.scalar.activation(dst, self.acc_ps[:, 320 + k * NS:320 + (k + 1) * NS].rearrange("p (h q) -> p h q", h=H), ACT.Copy)
        self.nc.scalar.drain().then_inc(self.latT_out, 1)

    def start_batch(self):
        v = self.nc.vector
        v.memset(self.m, NEG)
        v.memset(self.acc, 0.0)
        v.drain()

    def key_norm(self, dve, j, at):
        dve.wait_ge(self.ksq_done, at + j + 1)
        self.nc.vector.tensor_reduce(out=self.ssn[:, j, :], in_=self.sqp[:, j % 2, :].rearrange("p (h d) -> p h d", h=H), axis=AX,
                                     op=ALU.add).then_inc(self.ks_done, 1)

    def norm_sum(self, dve, n, gi):
        v = self.nc.vector
        dve.wait_ge(self.kr_sq, gi + 1)
        v.tensor_reduce(out=self.sskr[:, 0:n], in_=self.krsq[:, 0:n, :], axis=AX, op=ALU.add)
        v.drain()
        v.tensor_tensor(self.rk[:, 0:n, :], self.ssn[:, 0:n, :], self.sskr[:, 0:n].unsqueeze(2).to_broadcast([P, n, H]),
                        ALU.add).then_inc(self.norm_in, 1)

    def scale(self, dve, n, at, gi):
        v = self.nc.vector
        dve.wait_ge(self.norm_root, gi + 1)
        v.reciprocal(self.rk[:, 0:n, :], self.rk[:, 0:n, :])
        v.drain()
        dve.wait_ge(self.s_done, at + n)
        rkb = self.rk[:, 0:n, :].rearrange("p a h -> p (a h)").unsqueeze(2).to_broadcast([P, n * H, DQ])
        v.tensor_tensor(self.sc[:, 0:n, :].rearrange("p a (h q) -> p (a h) q", h=H),
                        self.small_ps[:, 0:n * NS].rearrange("p (a q) -> p a q", q=DQ), rkb, ALU.mult).then_inc(self.scaled, 1)
        v.drain()
        if n > GP:
            v.tensor_tensor(self.sc[:, GP, :], self.sc[:, GP, :], self.C["page_mask"], ALU.add)
            v.drain()
        v.tensor_reduce(out=self.pmax, in_=self.sc[:, 0:n, :].rearrange("p a c -> p c a"), axis=AX, op=ALU.max).then_inc(self.pm_done, 1)

    def new_maximum(self, dve, gi):
        v = self.nc.vector
        dve.wait_ge(self.pmT_done, gi + 1)
        v.tensor_reduce(out=self.gmax, in_=self.maxT, axis=AX, op=ALU.max)
        v.drain()
        v.tensor_tensor(self.mnew, self.m, self.gmax, ALU.max)
        v.drain()
        v.tensor_scalar(self.diag, self.C["ident"][0:NS, 0:NS], self.mnew, None, ALU.mult)
        v.tensor_scalar(self.negm, self.mnew, -1.0, None, ALU.mult)
        v.drain().then_inc(self.m_done, 1)

    def subtract(self, dve, n, gi):
        dve.wait_ge(self.mb_done, gi + 1)
        self.nc.vector.tensor_tensor(self.sc[:, 0:n, :], self.sc[:, 0:n, :],
                                     self.spread.unsqueeze(1).to_broadcast([P, n, NS]), ALU.subtract).then_inc(self.shift_done, 1)

    def accumulate(self, dve, gi):
        v = self.nc.vector
        dve.wait_ge(self.corr_done, gi + 1)
        v.tensor_copy(self.m, self.mnew)
        dve.wait_ge(self.pv_done, gi + 2)
        v.scalar_tensor_tensor(out=self.acc, in0=self.acc, scalar=self.corr, in1=self.acc_ps[0:NS, 0:KL + 1], op0=ALU.mult,
                               op1=ALU.add).then_inc(self.acc_out, 1)
        v.drain()

    def divide(self, dve, b):
        v = self.nc.vector
        v.reciprocal(self.rl, self.acc[:, KL:KL + 1])
        v.drain()
        dve.wait_ge(self.latT_done, b)
        v.tensor_scalar(self.lat, self.acc[:, 0:KL], self.rl, None, ALU.mult).then_inc(self.lat_done, 1)
        v.drain()
        self.start_batch()


def peer(env, tag, r0, nr, rt):
    nc, I, O, ar, C = (env[k] for k in ("nc", "I", "O", "ar", "C"))
    with_pages = not rt.by_halves
    yall, xn2 = ar.at(YALL, P, NT, D), ar.at(XN2, P, NT, D)
    ids, gates, s_dram = env["ids"], env["gates"], env["s_dram"]
    w = XN2 + NT * D
    u_ring = ar.at(w, P, RING, D); w += RING * D
    v_ring = ar.at(w, P, RING, D); w += RING * D
    diag = ar.at(w, P, TOPK, P); w += TOPK * P
    xcur = ar.at(w, P, D); w += D
    uid = [ar.at(w + 8 * j, P, 8).bitcast(U32) for j in range(2)]; w += 16
    vid = [ar.at(w + 8 * j, P, 8).bitcast(U32) for j in range(2)]; w += 16
    a, a2, th, wt = (ar.at(w + 16 * j, P, TOPK) for j in range(4)); w += 64
    with ExitStack() as ctx:
        sem = lambda n: ctx.enter_context(nc.semaphore(tag + n))
        acc = ctx.enter_context(nc.psum_tensor("ps_acc" + tag, [P, 2, 2, 512], F32))
        ps = ctx.enter_context(nc.psum_tensor("ps_pages" + tag, [P, 4, 512], F32))
        assert w <= ROUTE_AT, w
        pg = Pages(env, rt.end, sem, ps) if with_pages else None
        assert (pg or rt).end <= LATE, ((pg or rt).end, LATE)
        PPB = Pages.PPB
        u_in, v_in = [sem(f"i_u_in{j}") for j in range(RING)], [sem(f"i_v_in{j}") for j in range(RING)]
        uid_set, vid_set, u_used, v_used = (sem("i_" + n) for n in ("uid", "vid", "u_used", "v_used"))
        x_set, act_in, tanh_done, w_done, diag_done, acc_out = (
            sem("i_" + n) for n in ("x_set", "act_in", "tanh", "w", "diag", "acc_out"))
        fold_done, fold_out, stored = sem("i_fold"), sem("i_fold_out"), sem("i_stored")
        block = ctx.enter_context(nc.Block())

        def steps(eng, step):
            if not with_pages:
                for c in range(nr):
                    step(c, 0, 0, c % 2, min(nr - 1 - c, 3))
                return
            with eng.Fori(0, DB - 1) as b:
                with eng.Fori(0, GROUPS // 2 - 1) as gg:
                    for par in range(2):
                        step(b * GROUPS + gg * 2 + par, b, gg * 2 + par, par, 3)
                for g in range(GROUPS - 2, GROUPS):
                    step(b * GROUPS + g, b, g, g % 2, 3)
            b = DB - 1
            with eng.Fori(0, GROUPS // 2 - 2) as gg:
                for par in range(2):
                    step(gg * 2 + b * GROUPS + par, b, gg * 2 + par, par, 3)
            for g in range(GROUPS - 4, GROUPS):
                step(b * GROUPS + g, b, g, g % 2, min(GROUPS - 1 - g, 3))

        def group_size(g):
            return GP + (isinstance(g, int) and g == GROUPS - 1)

        def gather(ring, j, idx, table, done):
            nc.gpsimd.indirect_dma_start(out=ring[:, j, :], out_offset=None, in_=I[table],
                                         in_offset=bass.IndirectOffsetOnAxis(ap=idx, axis=0)).then_inc(done[j], 16)

        @block.sync
        def _(sp):
            for c in range(rt.early, EARLY + 1):
                rt.load(sp, c, r0 + c, s_dram)
            if pg:
                pg.load_first(sp)
                pg.load_new(sp, 0)
                pg.load_group(sp, 0, 0, 0)
            if pg:
                def group_and_scores(b, g, par):
                    pg.load_group(sp, b, g, par)
                    rt.load(sp, b * GROUPS + g + 3, r0 + b * GROUPS + g + 3, s_dram)

                group_and_scores(0, 1, 1)
                with sp.Fori(1, GROUPS // 2) as gg:
                    for par in range(2):
                        group_and_scores(0, gg * 2 + par, par)
                with sp.Fori(1, DB - 1) as b:
                    for g in range(2):
                        group_and_scores(b, g, g)
                    pg.load_new(sp, b)
                    with sp.Fori(1, GROUPS // 2) as gg:
                        for par in range(2):
                            group_and_scores(b, gg * 2 + par, par)
                for g in range(2):
                    group_and_scores(DB - 1, g, g)
                pg.load_new(sp, DB - 1)
                for g in range(2, GROUPS - 3):
                    group_and_scores(DB - 1, g, g % 2)
                for g in range(GROUPS - 3, GROUPS):
                    pg.load_group(sp, DB - 1, g, g % 2)
            else:
                sp.wait_ge(fold_out, 1)
                sp.dma_start(O["y_sample"], xcur[0:NS, :]).then_inc(stored, 16)
                sp.wait_ge(env["y_stored"], 16)
                sp.wait_ge(stored, 16)

        @block.gpsimd
        def _(pool):
            if pg:
                pg.clear()
            pool.wait_ge(rt.done, 1)
            for half in range(2):
                nc.gpsimd.tensor_copy(uid[half], ids[:, r0 * TOPK + half * 8:r0 * TOPK + half * 8 + 8]).then_inc(uid_set, 1)
                pool.wait_ge(uid_set, half + 1)
                for j in range(RING):
                    if half:
                        pool.wait_ge(u_used, j + 1)
                    gather(u_ring, j, uid[half][:, j:j + 1], "peer_u", u_in)

            def step(c, more):
                for half in range(2):
                    if more:
                        pool.wait_ge(u_used, c * 16 + half * 8 + 8)
                        pool.wait_ge(rt.done, c + 2)
                        nc.gpsimd.tensor_copy(uid[half], ids[:, ds((c + r0 + 1) * TOPK + half * 8, 8)]).then_inc(uid_set, 1)
                        pool.wait_ge(uid_set, c * 2 + half + 3)
                    pool.wait_ge(v_used, c * 16 + half * 8 + 8)
                    nc.gpsimd.tensor_copy(vid[half], ids[:, ds((c + r0) * TOPK + half * 8, 8)]).then_inc(vid_set, 1)
                    pool.wait_ge(vid_set, c * 2 + half + 1)
                    for j in range(RING):
                        if more:
                            wait_apart(pool, u_used, c * 16 + half * 8 + 8 + j + 1, (uid_set, 1))
                            gather(u_ring, j, uid[half][:, j:j + 1], "peer_u", u_in)
                        wait_apart(pool, v_used, c * 16 + half * 8 + 8 + j + 1, (vid_set, 1))
                        gather(v_ring, j, vid[half][:, j:j + 1], "peer_v", v_in)

            with pool.Fori(0, nr - 1) as c:
                step(c, True)
            step(nr - 1, False)

        @block.scalar
        def _(act):
            def set_x(c):
                if not isinstance(c, int) or c:
                    act.wait_ge(u_used, c * 16)
                nc.scalar.activation(xcur, one(xn2[:, ds((c + r0) // H, 1), :]), ACT.Copy).then_inc(x_set, 1)

            def tanh(n):
                act.wait_ge(act_in, n)
                nc.scalar.activation(th, th, ACT.Tanh, scale=0.7978845608028654).then_inc(tanh_done, 1)

            def step(c, b, g, par, left):
                act.wait_ge(w_done, c + 1)
                for s in range(TOPK):
                    act.wait_ge(v_used, c * 16 + s + 1)
                    nc.scalar.activation(diag[:, s, :], C["ident"], ACT.Copy, scale=wt[:, s:s + 1]).then_inc(diag_done, 1)
                if pg:
                    at, gi, n = b * PPB + g * GP, b * GROUPS + g, group_size(g)
                    pg.copy_page(act, 0, at)
                    for j in range(1, n):
                        pg.copy_page(act, j, at)
                        pg.square(act, j - 1, at)
                    pg.square(act, n - 1, at)
                    pg.square_rope(act, n, gi, par)
                    pg.root(act, n, gi)
                    pg.correct(act, gi)
                    pg.exponentials(act, n, gi)
                if left >= 1:
                    tanh(c + 2)
                if left >= 2:
                    set_x(c + 2)
                if left >= 3:
                    rt.softmax(act, c + 3)
                if pg and n > GP:
                    pg.copy_result(act, b)

            set_x(0)
            for c in range(rt.early, EARLY):
                rt.softmax(act, c)
            tanh(1)
            set_x(1)
            steps(act, step)

        @block.tensor
        def _(pe):
            def add(c, s, par):
                pe.wait_ge(diag_done, c * 16 + s + 1)
                pe.wait_ge(v_in[s % RING], (c * 2 + s // RING) * 16 + 16)
                for n in range(2):
                    last = nc.tensor.matmul(acc[:, par, n, :], diag[:, s, :], v_ring[:, s % RING, n * 512:(n + 1) * 512],
                                            start=s == 0, stop=s == TOPK - 1)
                last.then_inc(v_used, 1)

            def step(c, b, g, par, left):
                pe.wait_ge(acc_out, c)
                if pg:
                    at, gi, n = b * PPB + g * GP, b * GROUPS + g, group_size(g)
                for s in range(TOPK):
                    add(c, s, par)
                    if not pg:
                        continue
                    if s == KEYS_AT[0] - 1:
                        pg.group_arrived(pe, b, g, n, par)
                        pg.transposes(pe, 0, at, par)
                    if s in KEYS_AT[:n]:
                        j = KEYS_AT.index(s)
                        if j + 1 < n:
                            pg.transposes(pe, j + 1, at, par)
                        pg.keys(pe, j, at, gi, b)
                    if s == SCORES_AT:
                        pg.maxima(pe, gi)
                    if s == SCORES_AT + 1:
                        pg.spread_maxima(pe, gi)
                    if s == SCORES_AT + 3:
                        pg.weigh(pe, n, gi, par)
                if pg and n > GP:
                    pg.result(pe, b)

            nc.tensor.drain().then_inc(v_used, 16)
            if pg:
                nc.tensor.drain().then_inc(pg.pv_done, 1)
                pe.wait_ge(pg.loaded, 32)
            steps(pe, step)
            if not with_pages:
                pe.wait_ge(acc_out, nr + 1)
                for n in range(2):
                    last = nc.tensor.matmul(ps[0:NS, n, :], C["fold"], yall[:, NT - 1, n * 512:(n + 1) * 512], start=True, stop=True)
                last.then_inc(fold_done, 1)

        @block.vector
        def _(dve):
            v, fence = nc.vector, nc.vector.drain

            def dot(c, s):
                if s == 0:
                    dve.wait_ge(x_set, c + 1)
                dve.wait_ge(u_in[s % RING], (c * 2 + s // RING) * 16 + 16)
                v.tensor_tensor_reduce(out=u_ring[:, s % RING, :], in0=u_ring[:, s % RING, :], in1=xcur, scale=1.0, scalar=0.0,
                                       op0=ALU.mult, op1=ALU.add, accum_out=a[:, s:s + 1]).then_inc(u_used, 1)

            def weights(c):
                fence()
                v.tensor_tensor(a2, a, a, ALU.mult)
                fence()
                v.tensor_scalar(a2, a2, 0.044715, 1.0, ALU.mult, ALU.add)
                fence()
                v.tensor_tensor(th, a2, a, ALU.mult)
                fence().then_inc(act_in, 1)
                v.scalar_tensor_tensor(out=a2, in0=a, scalar=0.5, in1=gates[:, ds((c + r0) * TOPK, TOPK)], op0=ALU.mult, op1=ALU.mult)
                fence()
                dve.wait_ge(tanh_done, c + 1)
                dve.wait_ge(diag_done, c * 16)
                v.scalar_tensor_tensor(out=wt, in0=th, scalar=1.0, in1=a2, op0=ALU.add, op1=ALU.mult).then_inc(w_done, 1)

            def collect(c, par):
                dve.wait_ge(v_used, c * 16 + 32)
                y = one(yall[:, ds((c + r0) // H, 1), :])
                v.tensor_tensor(y, y, acc[:, par, :, :].rearrange("p a b -> p (a b)"), ALU.add).then_inc(acc_out, 1)
                fence()

            def step(c, b, g, par, left):
                if pg:
                    at, gi, n = b * PPB + g * GP, b * GROUPS + g, group_size(g)
                for s in range(TOPK):
                    if s < TOPK - LEAD:
                        if left >= 1:
                            dot(c + 1, s + LEAD)
                    else:
                        if s == TOPK - LEAD and left >= 1:
                            weights(c + 1)
                        if left >= 2:
                            dot(c + 2, s - (TOPK - LEAD))
                    if left >= 3:
                        if s == 1:
                            rt.top_eight(dve, c + 3)
                        if s == 2:
                            rt.top_sixteen()
                        if s == 3:
                            rt.pairs()
                        if s == 15:
                            rt.experts(dve, c + 3, c + 3 + r0)
                    if pg:
                        if s - 1 in KEYS_AT[:n]:
                            pg.key_norm(dve, KEYS_AT.index(s - 1), at)
                        if s - 1 == KEYS_AT[n - 1]:
                            pg.norm_sum(dve, n, gi)
                        if s == SCORES_AT:
                            pg.scale(dve, n, at, gi)
                        if s == SCORES_AT + 1:
                            pg.new_maximum(dve, gi)
                        if s == SCORES_AT + 2:
                            pg.subtract(dve, n, gi)
                        if s == SCORES_AT + 4:
                            pg.accumulate(dve, gi)
                            if n > GP:
                                pg.divide(dve, b)
                collect(c, par)

            fence().then_inc(acc_out, 1)
            if pg:
                pg.start_batch()
            for s in range(TOPK):
                if s % RING == 0 and rt.early + s // RING < EARLY:
                    c = rt.early + s // RING
                    rt.find(dve, c, c + r0)
                dot(0, s)
            weights(0)
            for s in range(LEAD):
                dot(1, s)
            steps(dve, step)
            if not with_pages:
                dve.wait_ge(fold_done, 1)
                v.tensor_copy(xcur[0:NS, :], ps[0:NS, 0:2, :].rearrange("p a b -> p (a b)")).then_inc(fold_out, 1)


_OUTS = {"y_prompt": (SEQ, D), "y_sample": (NS, D), "ckvT": (P, 2, TOK), "kropeT": (DR, TOK),
         "poolT": (P, G, STATE), "poolsT": (P, G, DB, STATE)}


def constants():
    import numpy as np
    ident = np.eye(P, dtype=np.float32)
    k, q = np.arange(P), np.arange(P)
    causal = np.where(k[None, :] <= q[:, None], 0.0, NEG)
    hq = np.arange(NS) % DQ
    page_mask = np.where((k[:, None] < DQ) & (k[:, None] <= hq[None, :]), 0.0, NEG)
    inv = np.zeros((G, PAD))
    for g in range(G):
        inv[g] = 1.0 / np.minimum(np.arange(PAD) + 1, 2 << g)
    half = DR // 2
    pos = np.concatenate([np.arange(SEQ), 4096 + np.tile(np.arange(DQ), 2 * DB)]).astype(np.float32)
    freq = np.float32(10000.0) ** (-np.arange(half, dtype=np.float32) / np.float32(half))
    ang = (pos[None, :] * freq[:, None]).astype(np.float32)
    cos = np.concatenate([np.cos(ang)] * 2).astype(np.float32)
    sin = np.concatenate([-np.sin(ang), np.sin(ang)]).astype(np.float32)
    return dict(ident=ident, causal=causal, page_mask=page_mask, iota16=np.tile(np.arange(TOPK), (P, 1)),
                invcnt=np.tile(inv.reshape(1, -1), (P, 1)), fold=ident[:, 0:NS] + ident[:, NS:P],
                pick=np.tile(np.arange(2 * H - 1) == H - 1, (P, 1))), cos, sin


def kernel(**inp):
    import numpy as np
    import concourse.bacc as bacc
    from concourse.bass_utils import run_bass_kernel_spmd

    A = {k: np.asarray(v) for k, v in inp.items()}

    def chunked(w):
        return w.reshape(w.shape[0] // P, P, w.shape[1]).transpose(1, 0, 2)

    def cols(w):
        return w.reshape(-1, P).T

    xs = A["x_sample"].reshape(NS, D)
    x = np.concatenate([A["x_prompt"][0], xs, xs])
    win = A["w_in"][0]
    o_kr, o_pool, o_gate = QL + KL, QL + KL + DR, QL + KL + DR + G * P
    swap = np.r_[DR // 2:DR, 0:DR // 2]
    kr = win[:, o_kr:o_pool]
    front = np.concatenate([win[:, 0:o_kr], win[:, o_pool:o_gate], kr, kr[:, swap]], axis=1)
    wq = A["w_q_up"][0]
    tables, cos, sin = constants()
    norms = dict(ones=np.ones((P, P)), w1=cols(A["norm1_w"][0]), wq_lat=cols(A["q_lat_norm_w"][0]), wkv=cols(A["kv_lat_norm_w"][0]),
                 pool_scale=cols(A["pool_scale"][0]), eps=np.full((P, 1), EPS),
                 wqk=np.zeros((P, 1), np.float32))
    consts = np.concatenate([np.asarray({**tables, **norms}[n], np.float32) for n, _ in CONSTS], axis=1)
    merge_w = np.stack([np.concatenate([chunked(win[:, o_gate + a * D + d * P:o_gate + a * D + (d + 1) * P]) for a in range(2)]
                                       + [chunked(A[n][0][:, d * P:(d + 1) * P]) for n in ("w_attn_br", "w_pool_br")], axis=1)
                        for d in range(KD)])
    keys = A["peer_keys"][0].reshape(2 * H, NK, P).transpose(0, 2, 1)
    peer_w = np.stack([np.concatenate([chunked(A["peer_w_q"][0][:, j * P:(j + 1) * P]), keys[j][:, None, :]], axis=1) for j in range(2 * H)])
    arrays = {
        "consts": consts, "qk_norms": np.stack([A["q_norm_w"][0], A["k_norm_w"][0]], axis=1),
        "xT": chunked(x.T), "x_tok": x.reshape(NT, P, D), "cos": cos, "sin": sin,
        "spread": np.repeat(np.eye(H, dtype=np.float32)[:, :, None], DH, axis=2),
        "w_front": chunked(front), "w_q_up": chunked(wq.reshape(QL, H * DH)), "w_q_sw": chunked(wq[:, :, DN + swap].reshape(QL, H * DR)),
        "w_uk": chunked(A["w_uk"][0].reshape(KL, H * DN)), "w_ukT": A["w_uk"][0].transpose(2, 1, 0),
        "w_uv": chunked(A["w_uv"][0].reshape(KL, H * DN)), "pool_lin": A["pool_lin_w"][0].transpose(1, 0, 2),
        "stateT": A["state_pool"][0].reshape(DB, STATE, G, P).transpose(3, 2, 0, 1),
        "page_table": A["page_table"].reshape(1, DB * NPAGES), "cache_ckv": A["cache_ckv"][0], "cache_krope": A["cache_krope"][0],
        "w_merge": merge_w, "w_out": chunked(A["w_out"][0]), "norm2": np.tile(A["norm2_w"], (P, 1)), "w_peer": peer_w,
        "peer_u": A["peer_u"][0], "peer_v": A["peer_v"][0],
    }
    nc = bacc.Bacc("TRN2", target_bir_lowering=False, num_devices=1)
    ins, feed = {}, {}
    for name, a in arrays.items():
        a = np.ascontiguousarray(a)
        feed["in_" + name] = a
        ins[name] = nc.dram_tensor("in_" + name, a.shape, mybir.dt.from_np(a.dtype), kind="ExternalInput").ap()
    outs = {name: nc.dram_tensor("out_" + name, shape, F32, kind="ExternalOutput").ap() for name, shape in _OUTS.items()}
    build(nc, ins, outs)
    res = run_bass_kernel_spmd(nc, [feed], core_ids=[0]).results[0]
    got = {name: np.asarray(res["out_" + name]) for name in _OUTS}
    ckv = got["ckvT"].transpose(2, 1, 0).reshape(TOK, KL)
    kro = got["kropeT"].T
    return (got["y_prompt"].reshape(1, SEQ, D), got["y_sample"].reshape(DB, DQ, D),
            ckv[0:SEQ].reshape(1, 1, SEQ, KL), kro[0:SEQ].reshape(1, 1, SEQ, DR),
            got["poolT"].transpose(2, 1, 0).reshape(1, 1, STATE, G * P),
            ckv[SEQ:SEQ + NS].reshape(1, DB, DQ, KL), kro[SEQ:SEQ + NS].reshape(1, DB, DQ, DR),
            got["poolsT"].transpose(2, 3, 1, 0).reshape(1, DB, STATE, G * P))
```
